# Optimizing a Trainium2 kernel written in Bass

```python
import numpy as np
import jax
import jax.numpy as jnp
from jax import lax

D_MODEL = 1024
BATCH = 1
SEQ = 256
DEPTH = 2

HEAD_DIM = 64
N_HEADS = D_MODEL // HEAD_DIM
N_KV_HEADS = 4
GROUP = N_HEADS // N_KV_HEADS
ROPE_THETA = 10000.0
RMS_EPS = 1e-6
NEG_INF = -1e30
POS_INF = 1e30
IDX_HEADS = 8
IDX_DIM = HEAD_DIM
DSA_TOPK = 256
DSA_Q_BLOCK = 128
CMP_LEN = 32
CMP_STRIDE = 16
CMP_HIDDEN = 256
SLC_LEN = 64
SLC_TOPN = 16
WINDOW = 512
NSA_Q_BLOCK = 64
N_NSA_BRANCH = 3
D_FF = 256 * ((8 * D_MODEL // 3 + 255) // 256)
N_EXPERTS = 8
TOP_K_EXPERTS = 2
D_FF_EXPERT = 7 * D_MODEL // 2
N_A_LAYERS = max(1, DEPTH // 2)
N_B_LAYERS = DEPTH - N_A_LAYERS
N_DENSE_LAYERS = (DEPTH + 1) // 2
N_MOE_LAYERS = DEPTH // 2
A_WIDTHS = (N_HEADS * HEAD_DIM, N_KV_HEADS * HEAD_DIM, N_KV_HEADS * HEAD_DIM, IDX_HEADS * IDX_DIM, IDX_DIM, IDX_HEADS)
A_IN = sum(A_WIDTHS)
B_IN = N_HEADS * HEAD_DIM + N_NSA_BRANCH * N_HEADS
KV_WIDTH = 2 * N_NSA_BRANCH * N_KV_HEADS * HEAD_DIM


F32 = jnp.float32

def rmsnorm(x, g):
    xf = x.astype(F32)
    y = xf * lax.rsqrt(jnp.mean(xf * xf, axis=-1, keepdims=True) + RMS_EPS)
    return (y * g.astype(F32)).astype(x.dtype)

def modulate(u, shift, scale):
    return u * (1.0 + scale[:, None, :]) + shift[:, None, :]

def rope_tables(positions, dim):
    inv = 1.0 / (ROPE_THETA ** (jnp.arange(0, dim, 2, dtype=F32) / dim))
    ang = positions.astype(F32)[..., None] * inv
    return jnp.cos(ang), jnp.sin(ang)

def apply_rope(x, cos, sin):
    x1, x2 = jnp.split(x.astype(F32), 2, axis=-1)
    c = cos[:, :, None, :]
    s = sin[:, :, None, :]
    return jnp.concatenate([x1 * c - x2 * s, x2 * c + x1 * s], axis=-1).astype(x.dtype)

def masked_softmax(s, mask):
    p = jax.nn.softmax(jnp.where(mask, s, NEG_INF), axis=-1)
    return jnp.where(mask, p, 0.0)

def swiglu(u, wg, wu, wd):
    return (jax.nn.silu(u @ wg) * (u @ wu)) @ wd

def moe_swiglu(u, w_router, wg, wu, wd):
    bsz, seq, d = u.shape
    xf = u.reshape(bsz * seq, d)
    logits = (xf @ w_router).astype(F32)
    vals, idx = lax.top_k(logits, TOP_K_EXPERTS)
    w = jax.nn.softmax(vals, axis=-1)
    gate = jnp.sum(jax.nn.one_hot(idx, N_EXPERTS, dtype=F32) * w[..., None], axis=1)
    y = jnp.zeros_like(xf)
    for e in range(N_EXPERTS):
        y = y + gate[:, e:e + 1].astype(xf.dtype) * swiglu(xf, wg[e], wu[e], wd[e])
    return y.reshape(bsz, seq, d)

def dsa_mixer(u, cos, sin, w_in, w_out):
    bsz, seq, _ = u.shape
    splits = [int(i) for i in np.cumsum(A_WIDTHS[:-1])]
    q, k, v, iq, ik, iw = jnp.split(u @ w_in, splits, axis=-1)
    q = apply_rope(q.reshape(bsz, seq, N_HEADS, HEAD_DIM), cos, sin)
    k = apply_rope(k.reshape(bsz, seq, N_KV_HEADS, HEAD_DIM), cos, sin)
    v = v.reshape(bsz, seq, N_KV_HEADS, HEAD_DIM)
    iq = apply_rope(iq.reshape(bsz, seq, IDX_HEADS, IDX_DIM), cos, sin).astype(F32)
    ik = apply_rope(ik.reshape(bsz, seq, 1, IDX_DIM), cos, sin)[:, :, 0].astype(F32)
    iw = iw.astype(F32) * (IDX_HEADS ** -0.5 * IDX_DIM ** -0.5)
    n_keep = min(DSA_TOPK, seq // 4)
    key_pos = jnp.arange(seq)
    scale = HEAD_DIM ** -0.5

    def block(i):
        q0 = i * DSA_Q_BLOCK
        t = q0 + jnp.arange(DSA_Q_BLOCK)
        qb = lax.dynamic_slice_in_dim(q, q0, DSA_Q_BLOCK, axis=1)
        iqb = lax.dynamic_slice_in_dim(iq, q0, DSA_Q_BLOCK, axis=1)
        iwb = lax.dynamic_slice_in_dim(iw, q0, DSA_Q_BLOCK, axis=1)
        rel = jax.nn.relu(jnp.einsum('bqhd,bsd->bqhs', iqb, ik))
        score = jnp.einsum('bqh,bqhs->bqs', iwb, rel)
        score = jnp.where(key_pos[None, None, :] <= t[None, :, None], score, NEG_INF)
        _, idx = lax.top_k(score, n_keep)
        kg = jax.vmap(lambda kb, ib: kb[ib])(k, idx)
        vg = jax.vmap(lambda vb, ib: vb[ib])(v, idx)
        qg = qb.reshape(bsz, DSA_Q_BLOCK, N_KV_HEADS, GROUP, HEAD_DIM)
        s = jnp.einsum('bqgrd,bqkgd->bgrqk', qg, kg).astype(F32) * scale
        valid = (idx <= t[None, :, None])[:, None, None]
        p = masked_softmax(s, valid).astype(vg.dtype)
        o = jnp.einsum('bgrqk,bqkgd->bqgrd', p, vg)
        return o.reshape(bsz, DSA_Q_BLOCK, N_HEADS * HEAD_DIM)

    o = lax.map(block, jnp.arange(seq // DSA_Q_BLOCK))
    o = jnp.transpose(o, (1, 0, 2, 3)).reshape(bsz, seq, N_HEADS * HEAD_DIM)
    return o @ w_out

def compress_blocks(x, blk_idx, pe, w1, w2):
    bsz = x.shape[0]
    n_cmp = blk_idx.shape[0]
    xb = x[:, blk_idx] + pe[None, None, :, None, :]
    xb = jnp.transpose(xb, (0, 1, 3, 2, 4)).reshape(bsz, n_cmp, N_KV_HEADS, CMP_LEN * HEAD_DIM)
    return jax.nn.gelu(xb @ w1) @ w2

def nsa_shared_kv(h, c_act, kv_gain, w_kv_ada, b_kv_ada, w_kv, pe_k, w1_k, w2_k, pe_v, w1_v, w2_v, cos, sin):
    bsz, seq, _ = h.shape
    shift, scale = jnp.split(c_act @ w_kv_ada + b_kv_ada, 2, axis=-1)
    u = modulate(rmsnorm(h, kv_gain), shift, scale)
    kv = (u @ w_kv).reshape(bsz, seq, 2 * N_NSA_BRANCH, N_KV_HEADS, HEAD_DIM)
    k_cmp = apply_rope(kv[:, :, 0], cos, sin)
    v_cmp = kv[:, :, 1]
    k_slc = apply_rope(kv[:, :, 2], cos, sin)
    v_slc = kv[:, :, 3]
    k_win = apply_rope(kv[:, :, 4], cos, sin)
    v_win = kv[:, :, 5]
    n_cmp = (seq - CMP_LEN) // CMP_STRIDE + 1
    blk_idx = np.arange(n_cmp)[:, None] * CMP_STRIDE + np.arange(CMP_LEN)[None, :]
    kc = compress_blocks(k_cmp, blk_idx, pe_k, w1_k, w2_k)
    vc = compress_blocks(v_cmp, blk_idx, pe_v, w1_v, w2_v)
    return kc, vc, k_slc, v_slc, k_win, v_win

def nsa_mixer(u, cos, sin, kc, vc, k_slc, v_slc, k_win, v_win, w_q, w_out):
    bsz, seq, _ = u.shape
    proj = u @ w_q
    q = apply_rope(proj[..., :N_HEADS * HEAD_DIM].reshape(bsz, seq, N_HEADS, HEAD_DIM), cos, sin)
    gates = jax.nn.sigmoid(proj[..., N_HEADS * HEAD_DIM:].astype(F32)).reshape(bsz, seq, N_HEADS, N_NSA_BRANCH)
    n_cmp = kc.shape[1]
    n_slc = seq // SLC_LEN
    n_sel = min(SLC_TOPN, n_slc)
    cmp_start = np.arange(n_cmp) * CMP_STRIDE
    cmp_end = jnp.asarray(cmp_start + CMP_LEN - 1)
    slc_start = np.arange(n_slc) * SLC_LEN
    ov = np.minimum(cmp_start[:, None] + CMP_LEN, slc_start[None, :] + SLC_LEN) - np.maximum(cmp_start[:, None], slc_start[None, :])
    agg = jnp.asarray(np.clip(ov, 0, None) / CMP_LEN, dtype=F32)
    ks_blk = jnp.transpose(k_slc.reshape(bsz, n_slc, SLC_LEN, N_KV_HEADS, HEAD_DIM), (0, 3, 1, 2, 4))
    vs_blk = jnp.transpose(v_slc.reshape(bsz, n_slc, SLC_LEN, N_KV_HEADS, HEAD_DIM), (0, 3, 1, 2, 4))
    kw_pad = jnp.pad(k_win, ((0, 0), (WINDOW, 0), (0, 0), (0, 0)))
    vw_pad = jnp.pad(v_win, ((0, 0), (WINDOW, 0), (0, 0), (0, 0)))
    blk = jnp.arange(n_slc)
    in_blk = jnp.arange(SLC_LEN)
    scale = HEAD_DIM ** -0.5

    def block(i):
        q0 = i * NSA_Q_BLOCK
        t = q0 + jnp.arange(NSA_Q_BLOCK)
        qb = lax.dynamic_slice_in_dim(q, q0, NSA_Q_BLOCK, axis=1)
        qb = jnp.transpose(qb.reshape(bsz, NSA_Q_BLOCK, N_KV_HEADS, GROUP, HEAD_DIM), (0, 2, 3, 1, 4))
        gb = lax.dynamic_slice_in_dim(gates, q0, NSA_Q_BLOCK, axis=1)
        gb = jnp.transpose(gb.reshape(bsz, NSA_Q_BLOCK, N_KV_HEADS, GROUP, N_NSA_BRANCH), (0, 2, 3, 1, 4))
        sc = jnp.einsum('bgrqd,bngd->bgrqn', qb, kc).astype(F32) * scale
        pc = masked_softmax(sc, cmp_end[None, :] <= t[:, None])
        oc = jnp.einsum('bgrqn,bngd->bgrqd', pc.astype(vc.dtype), vc)
        imp = jnp.einsum('bgrqn,nj->bgqj', pc, agg)
        jt = t // SLC_LEN
        valid_b = blk[None, :] * SLC_LEN <= t[:, None]
        forced = (blk[None, :] == 0) | (blk[None, :] == jt[:, None]) | (blk[None, :] == jt[:, None] - 1)
        imp = jnp.where(valid_b, jnp.where(forced, POS_INF, imp), NEG_INF)
        _, sel = lax.top_k(imp, n_sel)
        kg = jax.vmap(jax.vmap(lambda kb, sb: kb[sb]))(ks_blk, sel)
        vg = jax.vmap(jax.vmap(lambda vb, sb: vb[sb]))(vs_blk, sel)
        tok = sel[..., None] * SLC_LEN + in_blk
        ss = jnp.einsum('bgrqd,bgqnld->bgrqnl', qb, kg).astype(F32) * scale
        ss = ss.reshape(bsz, N_KV_HEADS, GROUP, NSA_Q_BLOCK, n_sel * SLC_LEN)
        ms = (tok <= t[None, None, :, None, None]).reshape(bsz, N_KV_HEADS, 1, NSA_Q_BLOCK, n_sel * SLC_LEN)
        ps = masked_softmax(ss, ms)
        os_ = jnp.einsum('bgrqm,bgqmd->bgrqd', ps.astype(vg.dtype), vg.reshape(bsz, N_KV_HEADS, NSA_Q_BLOCK, n_sel * SLC_LEN, HEAD_DIM))
        kwb = lax.dynamic_slice_in_dim(kw_pad, q0, NSA_Q_BLOCK + WINDOW, axis=1)
        vwb = lax.dynamic_slice_in_dim(vw_pad, q0, NSA_Q_BLOCK + WINDOW, axis=1)
        s_pos = q0 - WINDOW + jnp.arange(NSA_Q_BLOCK + WINDOW)
        mw = (s_pos[None, :] >= 0) & (s_pos[None, :] <= t[:, None]) & (s_pos[None, :] > t[:, None] - WINDOW)
        sw = jnp.einsum('bgrqd,bkgd->bgrqk', qb, kwb).astype(F32) * scale
        pw = masked_softmax(sw, mw)
        ow = jnp.einsum('bgrqk,bkgd->bgrqd', pw.astype(vwb.dtype), vwb)
        o = gb[..., 0:1] * oc.astype(F32) + gb[..., 1:2] * os_.astype(F32) + gb[..., 2:3] * ow.astype(F32)
        return jnp.transpose(o, (0, 3, 1, 2, 4)).reshape(bsz, NSA_Q_BLOCK, N_HEADS * HEAD_DIM).astype(u.dtype)

    o = lax.map(block, jnp.arange(seq // NSA_Q_BLOCK))
    o = jnp.transpose(o, (1, 0, 2, 3)).reshape(bsz, seq, N_HEADS * HEAD_DIM)
    return o @ w_out

def first_inputs(seed: int = 0) -> dict:
    key = jax.random.key(seed)
    ks = jax.random.split(key, 32)
    d = D_MODEL

    def nrm(k, shape, scale):
        return jax.random.normal(k, shape, F32) * scale

    offset = jax.random.randint(ks[2], (BATCH, 1), 0, 1024, dtype=jnp.int32)
    positions = (offset + jnp.arange(SEQ, dtype=jnp.int32)[None, :]).astype(jnp.int32)
    return {
        'x': nrm(ks[0], (BATCH, SEQ, d), 1.0),
        'c': nrm(ks[1], (BATCH, d), 1.0),
        'positions': positions,
        'attn_gain': 1.0 + nrm(ks[3], (DEPTH, d), 0.05),
        'ffn_gain': 1.0 + nrm(ks[4], (DEPTH, d), 0.05),
        'w_ada': nrm(ks[5], (DEPTH, d, 6 * d), 0.5 * d ** -0.5),
        'b_ada': nrm(ks[6], (DEPTH, 6 * d), 0.01),
        'a_w_in': nrm(ks[7], (N_A_LAYERS, d, A_IN), d ** -0.5),
        'a_w_out': nrm(ks[8], (N_A_LAYERS, N_HEADS * HEAD_DIM, d), (N_HEADS * HEAD_DIM) ** -0.5),
        'b_w_q': nrm(ks[9], (N_B_LAYERS, d, B_IN), d ** -0.5),
        'b_w_out': nrm(ks[10], (N_B_LAYERS, N_HEADS * HEAD_DIM, d), (N_HEADS * HEAD_DIM) ** -0.5),
        'kv_gain': 1.0 + nrm(ks[11], (d,), 0.05),
        'w_kv_ada': nrm(ks[12], (d, 2 * d), 0.5 * d ** -0.5),
        'b_kv_ada': nrm(ks[13], (2 * d,), 0.01),
        'w_kv': nrm(ks[14], (d, KV_WIDTH), d ** -0.5),
        'cmp_pe_k': nrm(ks[15], (CMP_LEN, HEAD_DIM), 0.5),
        'cmp_w1_k': nrm(ks[16], (CMP_LEN * HEAD_DIM, CMP_HIDDEN), (CMP_LEN * HEAD_DIM) ** -0.5),
        'cmp_w2_k': nrm(ks[17], (CMP_HIDDEN, HEAD_DIM), CMP_HIDDEN ** -0.5),
        'cmp_pe_v': nrm(ks[18], (CMP_LEN, HEAD_DIM), 0.5),
        'cmp_w1_v': nrm(ks[19], (CMP_LEN * HEAD_DIM, CMP_HIDDEN), (CMP_LEN * HEAD_DIM) ** -0.5),
        'cmp_w2_v': nrm(ks[20], (CMP_HIDDEN, HEAD_DIM), CMP_HIDDEN ** -0.5),
        'ffn_w_gate': nrm(ks[21], (N_DENSE_LAYERS, d, D_FF), d ** -0.5),
        'ffn_w_up': nrm(ks[22], (N_DENSE_LAYERS, d, D_FF), d ** -0.5),
        'ffn_w_down': nrm(ks[23], (N_DENSE_LAYERS, D_FF, d), D_FF ** -0.5),
        'moe_w_router': nrm(ks[24], (N_MOE_LAYERS, d, N_EXPERTS), d ** -0.5),
        'moe_w_gate': nrm(ks[25], (N_MOE_LAYERS, N_EXPERTS, d, D_FF_EXPERT), d ** -0.5),
        'moe_w_up': nrm(ks[26], (N_MOE_LAYERS, N_EXPERTS, d, D_FF_EXPERT), d ** -0.5),
        'moe_w_down': nrm(ks[27], (N_MOE_LAYERS, N_EXPERTS, D_FF_EXPERT, d), D_FF_EXPERT ** -0.5),
        'final_gain': 1.0 + nrm(ks[28], (d,), 0.05),
    }

def first_block(x, c, positions, attn_gain, ffn_gain, w_ada, b_ada, a_w_in, a_w_out, b_w_q, b_w_out,
              kv_gain, w_kv_ada, b_kv_ada, w_kv, cmp_pe_k, cmp_w1_k, cmp_w2_k, cmp_pe_v, cmp_w1_v, cmp_w2_v,
              ffn_w_gate, ffn_w_up, ffn_w_down, moe_w_router, moe_w_gate, moe_w_up, moe_w_down, final_gain):
    cos, sin = rope_tables(positions, HEAD_DIM)
    c_act = jax.nn.silu(c)
    h = x
    kc = vc = k_slc = v_slc = k_win = v_win = None
    for layer in range(DEPTH):
        mod = c_act @ w_ada[layer] + b_ada[layer]
        a_shift, a_scale, a_gate, f_shift, f_scale, f_gate = jnp.split(mod, 6, axis=-1)
        if layer == N_A_LAYERS:
            kc, vc, k_slc, v_slc, k_win, v_win = nsa_shared_kv(
                h, c_act, kv_gain, w_kv_ada, b_kv_ada, w_kv,
                cmp_pe_k, cmp_w1_k, cmp_w2_k, cmp_pe_v, cmp_w1_v, cmp_w2_v, cos, sin)
        u = modulate(rmsnorm(h, attn_gain[layer]), a_shift, a_scale)
        if layer < N_A_LAYERS:
            mix = dsa_mixer(u, cos, sin, a_w_in[layer], a_w_out[layer])
        else:
            j = layer - N_A_LAYERS
            mix = nsa_mixer(u, cos, sin, kc, vc, k_slc, v_slc, k_win, v_win, b_w_q[j], b_w_out[j])
        h = h + a_gate[:, None, :] * mix
        u = modulate(rmsnorm(h, ffn_gain[layer]), f_shift, f_scale)
        if layer % 2 == 0:
            ff = swiglu(u, ffn_w_gate[layer // 2], ffn_w_up[layer // 2], ffn_w_down[layer // 2])
        else:
            m = layer // 2
            ff = moe_swiglu(u, moe_w_router[m], moe_w_gate[m], moe_w_up[m], moe_w_down[m])
        h = h + f_gate[:, None, :] * ff
    return rmsnorm(h, final_gain)


DEPTH_2 = 1

GRID_W = 64
CTX_LEN = 256
D_MIX = D_MODEL
D_MLSTM = D_MIX // 2
MLSTM_HEADS = 4
MLSTM_DH = D_MLSTM // MLSTM_HEADS
QKV_BLOCK = 4
N_QKV_BLOCKS = D_MLSTM // QKV_BLOCK
CONV_K = 3
CHUNK = 128
D_FOURIER = D_MIX - D_MLSTM
FOURIER_GROUPS = 4
FOURIER_CG = D_FOURIER // FOURIER_GROUPS
D_IN_PROJ = 2 * D_MLSTM + D_FOURIER
N_EXPERT_GROUPS = 4
EXPERTS_PER_GROUP = 4
N_EXPERTS_2 = N_EXPERT_GROUPS * EXPERTS_PER_GROUP
TOP_K = 2
D_EXPERT = D_MODEL // 2
N_MOD = 6
EPS = 1e-6
POS_BASE = 10000.0
F32_2 = jnp.float32


def rmsnorm_2(x, g):
    x32 = x.astype(F32_2)
    y = x32 * lax.rsqrt(jnp.mean(x32 * x32, axis=-1, keepdims=True) + EPS)
    return (y * g.astype(F32_2)).astype(x.dtype)

def modulate_2(h, shift, scale):
    return h * (1 + scale) + shift

def sincos_2d(rows, cols):
    quarter = D_MODEL // 4
    freq = 1.0 / (POS_BASE ** (jnp.arange(quarter, dtype=F32_2) / quarter))
    r = jnp.arange(rows, dtype=F32_2)[:, None] * freq
    cl = jnp.arange(cols, dtype=F32_2)[:, None] * freq
    er = jnp.concatenate([jnp.sin(r), jnp.cos(r)], axis=-1)
    ec = jnp.concatenate([jnp.sin(cl), jnp.cos(cl)], axis=-1)
    half = D_MODEL // 2
    emb = jnp.concatenate([jnp.broadcast_to(er[:, None, :], (rows, cols, half)),
                           jnp.broadcast_to(ec[None, :, :], (rows, cols, half))], axis=-1)
    return emb.reshape(rows * cols, D_MODEL)

def short_conv(x, w, b):
    y = lax.conv_general_dilated(x, w[:, None, :], window_strides=(1,), padding='SAME',
                                 dimension_numbers=('NWC', 'WIO', 'NWC'),
                                 feature_group_count=x.shape[-1])
    return y + b

def headwise(x, w):
    y = jnp.einsum('btni,nio->btno', x.reshape(x.shape[:-1] + (N_QKV_BLOCKS, QKV_BLOCK)), w)
    return y.reshape(x.shape)

def to_heads(t):
    B, T, _ = t.shape
    return t.astype(F32_2).reshape(B, T, MLSTM_HEADS, MLSTM_DH).transpose(0, 2, 1, 3)

def flip_seq(t):
    return jnp.flip(t, axis=2)

def mixer_features(h, lp):
    proj = h @ lp['w_in']
    x_m = proj[..., :D_MLSTM]
    z = proj[..., D_MLSTM:2 * D_MLSTM]
    u = proj[..., 2 * D_MLSTM:]
    act = jax.nn.silu(short_conv(x_m, lp['conv_w'], lp['conv_b']))
    q = headwise(act, lp['w_q'])
    k = headwise(act, lp['w_k'])
    v = headwise(x_m, lp['w_v'])
    qkv = jnp.concatenate([q, k, v], axis=-1)

    def gates(w, b):
        g = (qkv @ w + b).astype(F32_2).transpose(0, 2, 1)
        return g[:, :MLSTM_HEADS], jax.nn.log_sigmoid(g[:, MLSTM_HEADS:])

    heads = (to_heads(q) * (MLSTM_DH ** -0.5), to_heads(k), to_heads(v))
    return heads, gates(lp['w_if_fwd'], lp['b_if_fwd']), gates(lp['w_if_bwd'], lp['b_if_bwd']), act, z, u

def mlstm_scan(k, v, ig, lf, state):
    B, H, T, DH = k.shape
    nc = T // CHUNK
    kc = k.reshape(B, H, nc, CHUNK, DH)
    vc = v.reshape(B, H, nc, CHUNK, DH)
    b = jnp.cumsum(lf.reshape(B, H, nc, CHUNK), axis=-1)
    btot = b[..., -1]
    a = btot[..., None] - b + ig.reshape(B, H, nc, CHUNK)
    amax = jnp.max(a, axis=-1)

    def step(carry, xs):
        C, n, m = carry
        k_, v_, a_, amax_, bt_ = xs
        m_new = jnp.maximum(bt_ + m, amax_)
        decay = jnp.exp(bt_ + m - m_new)
        kw = k_ * jnp.exp(a_ - m_new[..., None])[..., None]
        C_new = decay[..., None, None] * C + jnp.einsum('bhlk,bhlv->bhkv', kw, v_)
        n_new = decay[..., None] * n + jnp.sum(kw, axis=2)
        return (C_new, n_new, m_new), (C, n, m)

    xs = tuple(jnp.moveaxis(t, 2, 0) for t in (kc, vc, a, amax, btot))
    final, starts = lax.scan(step, state, xs)
    starts = tuple(jnp.moveaxis(s, 0, 2) for s in starts)
    return starts, final

def mlstm_out(q, k, v, ig, lf, starts):
    C0, n0, m0 = starts
    B, H, T, DH = q.shape
    nc = T // CHUNK
    qc = q.reshape(B, H, nc, CHUNK, DH)
    kc = k.reshape(B, H, nc, CHUNK, DH)
    vc = v.reshape(B, H, nc, CHUNK, DH)
    igc = ig.reshape(B, H, nc, CHUNK)
    b = jnp.cumsum(lf.reshape(B, H, nc, CHUNK), axis=-1)
    tri = jnp.tril(jnp.ones((CHUNK, CHUNK), dtype=bool))
    logd = jnp.where(tri, b[..., :, None] - b[..., None, :] + igc[..., None, :], -jnp.inf)
    m_inter = b + m0[..., None]
    m_t = jnp.maximum(m_inter, jnp.max(logd, axis=-1))
    w_inter = jnp.exp(m_inter - m_t)
    s = jnp.einsum('bhctd,bhcsd->bhcts', qc, kc) * jnp.exp(logd - m_t[..., None])
    num = jnp.einsum('bhcts,bhcsd->bhctd', s, vc) + w_inter[..., None] * jnp.einsum('bhctk,bhckv->bhctv', qc, C0)
    nq = jnp.sum(s, axis=-1) + w_inter * jnp.einsum('bhctk,bhck->bhct', qc, n0)
    h = num / jnp.maximum(jnp.abs(nq), jnp.exp(-m_t))[..., None]
    return h.reshape(B, H, T, DH)

def mlstm_direction(ctx_in, lat_in, with_ctx):
    qc, kc, vc, igc, lfc = ctx_in
    ql, kl, vl, igl, lfl = lat_in
    B = kl.shape[0]
    zero = (jnp.zeros((B, MLSTM_HEADS, MLSTM_DH, MLSTM_DH), F32_2),
            jnp.zeros((B, MLSTM_HEADS, MLSTM_DH), F32_2),
            jnp.zeros((B, MLSTM_HEADS), F32_2))
    ctx_starts, ctx_final = mlstm_scan(kc, vc, igc, lfc, zero)
    lat_starts, _ = mlstm_scan(kl, vl, igl, lfl, ctx_final)
    h_lat = mlstm_out(ql, kl, vl, igl, lfl, lat_starts)
    h_ctx = mlstm_out(qc, kc, vc, igc, lfc, ctx_starts) if with_ctx else None
    return h_lat, h_ctx

def mlstm_readout(hf, hb, act, z, norm_w, skip):
    h = hf + hb
    mu = jnp.mean(h, axis=-1, keepdims=True)
    var = jnp.mean(jnp.square(h - mu), axis=-1, keepdims=True)
    hn = (h - mu) * lax.rsqrt(var + EPS)
    B, H, T, DH = hn.shape
    hn = hn.transpose(0, 2, 1, 3).reshape(B, T, D_MLSTM) * norm_w.astype(F32_2)
    out = (hn + skip.astype(F32_2) * act.astype(F32_2)) * jax.nn.silu(z.astype(F32_2))
    return out.astype(z.dtype)

def fourier_mix(u, w_fourier):
    B, T, _ = u.shape
    ug = u.astype(F32_2).reshape(B, T, FOURIER_GROUPS, FOURIER_CG)
    f = jnp.fft.fft2(ug, axes=(1, 3), norm='ortho').real
    y = jnp.einsum('btgc,gcd->btgd', f, w_fourier.astype(F32_2))
    return y.reshape(B, T, D_FOURIER).astype(u.dtype)

def token_mix(h, hc, lp, with_ctx):
    qkv_l, gf_l, gb_l, act_l, z_l, u_l = mixer_features(h, lp)
    qkv_c, gf_c, gb_c, act_c, z_c, u_c = mixer_features(hc, lp)
    hf_l, hf_c = mlstm_direction(qkv_c + gf_c, qkv_l + gf_l, with_ctx)
    hb_l, hb_c = mlstm_direction(tuple(flip_seq(t) for t in qkv_c + gb_c),
                                 tuple(flip_seq(t) for t in qkv_l + gb_l), with_ctx)

    def merge(hf, hb, act, z, u):
        m = mlstm_readout(hf, flip_seq(hb), act, z, lp['mlstm_norm_w'], lp['mlstm_skip'])
        f = fourier_mix(u, lp['w_fourier'])
        return jnp.concatenate([m, f], axis=-1) @ lp['w_out']

    y_l = merge(hf_l, hb_l, act_l, z_l, u_l)
    y_c = merge(hf_c, hb_c, act_c, z_c, u_c) if with_ctx else None
    return y_l, y_c

def hier_moe(h, lp):
    B, T, _ = h.shape
    g_logits = (h @ lp['w_router_group'] + lp['b_router_group']).astype(F32_2)
    p_group = jax.nn.softmax(g_logits, axis=-1)
    g_sel = jnp.argmax(g_logits, axis=-1)
    p_sel = jnp.take_along_axis(p_group, g_sel[..., None], axis=-1)
    e_logits = (h @ lp['w_router_expert'] + lp['b_router_expert']).astype(F32_2)
    e_logits = e_logits.reshape(B, T, N_EXPERT_GROUPS, EXPERTS_PER_GROUP)
    e_sel = jnp.take_along_axis(e_logits, g_sel[..., None, None], axis=2)[..., 0, :]
    top_v, top_i = lax.top_k(e_sel, TOP_K)
    w_top = jax.nn.softmax(top_v, axis=-1) * p_sel
    expert_id = g_sel[..., None] * EXPERTS_PER_GROUP + top_i
    combine = jnp.sum(jax.nn.one_hot(expert_id, N_EXPERTS_2, dtype=F32_2) * w_top[..., None], axis=-2)
    combine = combine.astype(h.dtype)
    y = jnp.zeros_like(h)
    for e in range(N_EXPERTS_2):
        a = jax.nn.silu(h @ lp['w_gate'][e]) * (h @ lp['w_up'][e])
        y = y + combine[..., e, None] * (a @ lp['w_down'][e])
    return y

def second_inputs(seed: int = 0) -> dict:
    key = jax.random.key(seed)
    ks = jax.random.split(key, 40)
    L = DEPTH_2
    H = MLSTM_HEADS

    def nrm(k, shape, s):
        return jax.random.normal(k, shape, F32_2) * s

    def b_if(k1, k2):
        return jnp.concatenate([nrm(k1, (L, H), 0.1),
                                jnp.linspace(3.0, 6.0, H, dtype=F32_2)[None, :] + nrm(k2, (L, H), 0.1)], axis=-1)

    return {
        'x': nrm(ks[0], (BATCH, SEQ, D_MODEL), 1.0),
        'c': nrm(ks[1], (BATCH, D_MODEL), 1.0),
        'ctx': nrm(ks[2], (BATCH, CTX_LEN, D_MODEL), 1.0),
        'c_ctx': nrm(ks[3], (D_MODEL,), 1.0),
        'w_ada': nrm(ks[4], (L, D_MODEL, N_MOD * D_MODEL), 0.5 * D_MODEL ** -0.5),
        'b_ada': nrm(ks[5], (L, N_MOD * D_MODEL), 0.01),
        'g_pre_mix': 1.0 + nrm(ks[6], (L, D_MODEL), 0.05),
        'g_post_mix': 1.0 + nrm(ks[7], (L, D_MODEL), 0.05),
        'g_pre_ffn': 1.0 + nrm(ks[8], (L, D_MODEL), 0.05),
        'g_post_ffn': 1.0 + nrm(ks[9], (L, D_MODEL), 0.05),
        'w_in': nrm(ks[10], (L, D_MODEL, D_IN_PROJ), D_MODEL ** -0.5),
        'conv_w': nrm(ks[11], (L, CONV_K, D_MLSTM), CONV_K ** -0.5),
        'conv_b': nrm(ks[12], (L, D_MLSTM), 0.01),
        'w_q': nrm(ks[13], (L, N_QKV_BLOCKS, QKV_BLOCK, QKV_BLOCK), QKV_BLOCK ** -0.5),
        'w_k': nrm(ks[14], (L, N_QKV_BLOCKS, QKV_BLOCK, QKV_BLOCK), QKV_BLOCK ** -0.5),
        'w_v': nrm(ks[15], (L, N_QKV_BLOCKS, QKV_BLOCK, QKV_BLOCK), QKV_BLOCK ** -0.5),
        'w_if_fwd': nrm(ks[16], (L, 3 * D_MLSTM, 2 * H), 0.02),
        'b_if_fwd': b_if(ks[17], ks[18]),
        'w_if_bwd': nrm(ks[19], (L, 3 * D_MLSTM, 2 * H), 0.02),
        'b_if_bwd': b_if(ks[20], ks[21]),
        'mlstm_norm_w': 1.0 + nrm(ks[22], (L, D_MLSTM), 0.05),
        'mlstm_skip': 1.0 + nrm(ks[23], (L, D_MLSTM), 0.05),
        'w_fourier': nrm(ks[24], (L, FOURIER_GROUPS, FOURIER_CG, FOURIER_CG), FOURIER_CG ** -0.5),
        'w_out': nrm(ks[25], (L, D_MIX, D_MODEL), D_MIX ** -0.5),
        'w_router_group': nrm(ks[26], (L, D_MODEL, N_EXPERT_GROUPS), D_MODEL ** -0.5),
        'b_router_group': nrm(ks[27], (L, N_EXPERT_GROUPS), 0.01),
        'w_router_expert': nrm(ks[28], (L, D_MODEL, N_EXPERTS_2), D_MODEL ** -0.5),
        'b_router_expert': nrm(ks[29], (L, N_EXPERTS_2), 0.01),
        'w_gate': nrm(ks[30], (L, N_EXPERTS_2, D_MODEL, D_EXPERT), D_MODEL ** -0.5),
        'w_up': nrm(ks[31], (L, N_EXPERTS_2, D_MODEL, D_EXPERT), D_MODEL ** -0.5),
        'w_down': nrm(ks[32], (L, N_EXPERTS_2, D_EXPERT, D_MODEL), D_EXPERT ** -0.5),
    }

def second_block(x, c, ctx, c_ctx, w_ada, b_ada, g_pre_mix, g_post_mix, g_pre_ffn, g_post_ffn,
              w_in, conv_w, conv_b, w_q, w_k, w_v, w_if_fwd, b_if_fwd, w_if_bwd, b_if_bwd,
              mlstm_norm_w, mlstm_skip, w_fourier, w_out, w_router_group, b_router_group,
              w_router_expert, b_router_expert, w_gate, w_up, w_down):
    T = x.shape[1]
    rows = T // GRID_W
    x = x + sincos_2d(rows, GRID_W).astype(x.dtype)[None]
    xc = ctx
    for l in range(DEPTH_2):
        with_ctx = l + 1 < DEPTH_2
        lp = {
            'w_in': w_in[l], 'conv_w': conv_w[l], 'conv_b': conv_b[l],
            'w_q': w_q[l], 'w_k': w_k[l], 'w_v': w_v[l],
            'w_if_fwd': w_if_fwd[l], 'b_if_fwd': b_if_fwd[l],
            'w_if_bwd': w_if_bwd[l], 'b_if_bwd': b_if_bwd[l],
            'mlstm_norm_w': mlstm_norm_w[l], 'mlstm_skip': mlstm_skip[l],
            'w_fourier': w_fourier[l], 'w_out': w_out[l],
            'w_router_group': w_router_group[l], 'b_router_group': b_router_group[l],
            'w_router_expert': w_router_expert[l], 'b_router_expert': b_router_expert[l],
            'w_gate': w_gate[l], 'w_up': w_up[l], 'w_down': w_down[l],
        }
        mod = [m[:, None, :] for m in jnp.split(jax.nn.silu(c) @ w_ada[l] + b_ada[l], N_MOD, axis=-1)]
        mod_c = [m[None, :] for m in jnp.split(jax.nn.silu(c_ctx) @ w_ada[l] + b_ada[l], N_MOD, axis=-1)]
        shift1, scale1, gate1, shift2, scale2, gate2 = mod
        h = modulate_2(rmsnorm_2(x, g_pre_mix[l]), shift1, scale1)
        hc = modulate_2(rmsnorm_2(xc, g_pre_mix[l]), mod_c[0], mod_c[1])
        y, yc = token_mix(h, hc, lp, with_ctx)
        x = x + gate1 * rmsnorm_2(y, g_post_mix[l])
        h2 = modulate_2(rmsnorm_2(x, g_pre_ffn[l]), shift2, scale2)
        x = x + gate2 * rmsnorm_2(hier_moe(h2, lp), g_post_ffn[l])
        if with_ctx:
            xc = xc + mod_c[2] * rmsnorm_2(yc, g_post_mix[l])
            hc2 = modulate_2(rmsnorm_2(xc, g_pre_ffn[l]), mod_c[3], mod_c[4])
            xc = xc + mod_c[5] * rmsnorm_2(hier_moe(hc2, lp), g_post_ffn[l])
    return x


def setup_inputs(seed=0):
    out = dict(first_inputs(seed))
    for name, value in second_inputs(seed + 1).items():
        if name != "x":
            out[name + "_2"] = value
    return out


def reference(
    x, c, positions, attn_gain, ffn_gain, w_ada, b_ada, a_w_in, a_w_out, b_w_q, b_w_out,
    kv_gain, w_kv_ada, b_kv_ada, w_kv, cmp_pe_k, cmp_w1_k, cmp_w2_k, cmp_pe_v, cmp_w1_v,
    cmp_w2_v, ffn_w_gate, ffn_w_up, ffn_w_down, moe_w_router, moe_w_gate, moe_w_up, moe_w_down,
    final_gain, c_2, ctx_2, c_ctx_2, w_ada_2, b_ada_2, g_pre_mix_2, g_post_mix_2, g_pre_ffn_2,
    g_post_ffn_2, w_in_2, conv_w_2, conv_b_2, w_q_2, w_k_2, w_v_2, w_if_fwd_2, b_if_fwd_2,
    w_if_bwd_2, b_if_bwd_2, mlstm_norm_w_2, mlstm_skip_2, w_fourier_2, w_out_2,
    w_router_group_2, b_router_group_2, w_router_expert_2, b_router_expert_2, w_gate_2, w_up_2,
    w_down_2,
):
    x = first_block(
        x, c, positions, attn_gain, ffn_gain, w_ada, b_ada, a_w_in, a_w_out, b_w_q, b_w_out,
        kv_gain, w_kv_ada, b_kv_ada, w_kv, cmp_pe_k, cmp_w1_k, cmp_w2_k, cmp_pe_v, cmp_w1_v,
        cmp_w2_v, ffn_w_gate, ffn_w_up, ffn_w_down, moe_w_router, moe_w_gate, moe_w_up,
        moe_w_down, final_gain,
    )
    return second_block(
        x, c_2, ctx_2, c_ctx_2, w_ada_2, b_ada_2, g_pre_mix_2, g_post_mix_2, g_pre_ffn_2,
        g_post_ffn_2, w_in_2, conv_w_2, conv_b_2, w_q_2, w_k_2, w_v_2, w_if_fwd_2, b_if_fwd_2,
        w_if_bwd_2, b_if_bwd_2, mlstm_norm_w_2, mlstm_skip_2, w_fourier_2, w_out_2,
        w_router_group_2, b_router_group_2, w_router_expert_2, b_router_expert_2, w_gate_2,
        w_up_2, w_down_2,
    )


_drawn_inputs = setup_inputs


def setup_inputs(seed=0):
    import zlib

    import numpy as np

    out = dict(_drawn_inputs(seed))
    spreads = {}
    factors = {'kv_gain': 3.488,
     'b_kv_ada': 8.0,
     'g_post_ffn_2': 4.748,
     'conv_b_2': 8.0,
     'mlstm_skip_2': 3.585,
     'b_router_group_2': 2.72,
     'b_router_expert_2': 8.0}
    for name, (base, spread) in spreads.items():
        noise = np.random.default_rng([zlib.crc32(name.encode()), seed]).standard_normal(out[name].shape)
        drawn = base * np.exp(spread * noise) if base else spread * noise
        out[name] = jnp.asarray(drawn.astype(out[name].dtype))
    for name, factor in factors.items():
        out[name] = (out[name] * factor).astype(out[name].dtype)
    return out
```

```python
import math
from contextlib import ExitStack

import numpy as np

import concourse.bass as bass
from concourse import mybir

F32 = mybir.dt.float32
I32 = mybir.dt.int32
ACT = mybir.ActivationFunctionType
ALU = mybir.AluOpType
AX = mybir.AxisListType.X

P = 128
D = 1024
KT = D // P
T = 256
NT = T // P
HD = 64
NH = 16
NKV = 4
IDX_H = 8
TOPK = 64
NCMP = 15
D_FF = 2816
E1 = 8
F1 = 3584
E2 = 16
F2 = 512
EG = 4
MH = 4
DH = 128
DM = 512
EPS = 1e-6
NEG = -1e30
TAKEN = -3e38
SCALE = HD ** -0.5
NSLOT = 6
SLOT = 4096
RR = (1, 2, 3, 4, 5)

PACK = [
    ("ident", 128), ("rot", 128), ("dup0", 128), ("dup1", 128), ("rotdup0", 128), ("rotdup1", 128),
    ("causal", NT * T), ("cmpneg", NT * NCMP), ("cmp01", NT * NCMP),
    ("inv", 1), ("rank", E2), ("bwd", 1),
    ("attn_gain", 2 * KT), ("ffn_gain", 2 * KT), ("kv_gain", KT), ("final_gain", KT),
    ("g_pre_mix", KT), ("g_post_mix", KT), ("g_pre_ffn", KT), ("g_post_ffn", KT),
    ("b_ada", 96), ("b_kv_ada", 16), ("b_ada_2", 48), ("c", KT), ("c2", KT * 2),
    ("router", KT * E1), ("router2", KT * 20), ("brouter2", 20), ("pe_k", 16), ("pe_v", 16),
    ("w2k", 2 * P), ("w2v", 2 * HD), ("conv_w", 12), ("conv_b", 4), ("norm_w", 4), ("skip", 4),
    ("wblk", 3 * 4 * 4), ("wif", 12 * 2 * 8), ("bif", 2),
]
PACK2 = [("anticausal", NT * T), ("blkmask", 32), ("dftc", 2 * P), ("dftt", NT * T), ("dfts", NT * T), ("wfour", 4 * P)]


def offsets(pack):
    off, n = {}, 0
    for name, w in pack:
        off[name] = (n, w)
        n += w
    return off, n


OFF, NPACK = offsets(PACK)
OFF2, NPACK2 = offsets(PACK2)


def program(nc, A, out):
    with ExitStack() as ctx:
        def sb(name, shape, dt=F32):
            return ctx.enter_context(nc.sbuf_tensor(name, shape, dt))

        def sem(name):
            return ctx.enter_context(nc.semaphore(name))

        def b3v(ap):
            return ap.rearrange("p (s n) -> p s n", s=2)

        ring = sb("ring", [P, NSLOT, SLOT])
        pack = sb("pack", [P, NPACK])
        posi = sb("posi", [P, T], I32)
        onesk = sb("onesk", [P, P])
        epsc = sb("epsc", [P, 1])
        zeros = sb("zeros", [P, P])
        hT = sb("hT", [P, KT, T])
        uT = sb("uT", [P, KT, T])
        sq = sb("sq", [P, KT, T])
        xn = sq
        root = sb("root", [P, T])
        rstd = sb("rstd", [P, T])
        trig = sb("trig", [P, 2, T])
        cact = sb("cact", [P, 3 * KT])
        mods = sb("mods", [P, 96 + 16 + 96])
        gsc = sb("gsc", [P, 10 * KT])
        arena = sb("arena", [P, 11296 + NPACK2])
        tmp = sb("tmp", [P, 2, 512])
        cols = sb("cols", [P, 96])
        small = sb("small", [P, 12, 48])
        psum = ctx.enter_context(nc.psum_tensor("psum", [P, 8, 512], F32))

        def pk(name, *dims):
            o, w = OFF[name]
            ap = pack[:, o:o + w]
            if dims:
                ap = ap.rearrange(f"p (a b) -> p a b", a=dims[0])
            return ap

        def ar(o, n):
            return arena[:, o:o + n]

        def pk2(name, a=None):
            o, w = OFF2[name]
            ap = arena[:, 11296 + o:11296 + o + w]
            return ap.rearrange("p (a b) -> p a b", a=a) if a else ap

        raw = ar(0, 1024).rearrange("p (i a n) -> p i a n", i=2, a=2)
        qT = ar(1024, 2048).rearrange("p (a n) -> p a n", a=8)
        iqT = ar(3072, 1024).rearrange("p (a n) -> p a n", a=4)
        kd = ar(4096, 3072).rearrange("p (b a n) -> p b a n", b=3, a=4)
        uk = qT
        uk_rows = ar(1024, 2048).rearrange("p (t n) -> p t n", t=NT)
        ang = ar(3072, 1024).rearrange("p (a n) -> p a n", a=4)
        selm = ar(5120, 512).rearrange("p (t n) -> p t n", t=2)
        ikd, acc8 = ar(5632, 256), ar(5888, 256)
        rel = ar(6144, 512).rearrange("p (i n) -> p i n", i=2)
        work = ar(6656, 256)
        vt = ar(7168, 1024).rearrange("p (b t n) -> p b t n", b=2, t=2)
        oT = ar(8192, 2048).rearrange("p (a n) -> p a n", a=8)
        xb = ar(3072, 960).rearrange("p (b g n) -> p b g n", b=16, g=4)
        hid60 = ar(10240, 240).rearrange("p (v c n) -> p v c n", v=2, c=2)
        kcT = ar(10480, 60).rearrange("p (g n) -> p g n", g=4)
        vc = ar(10540, 256).rearrange("p (g n) -> p g n", g=4)
        vcd = ar(8192, 1024)
        gb = ar(4096, E2 * T).rearrange("p (e n) -> p e n", e=E2)
        sg = ar(8192, 1024).rearrange("p (i a n) -> p i a n", i=2, a=2)
        hid = ar(9216, 1024).rearrange("p (i a n) -> p i a n", i=2, a=2)
        zs = ar(0, 1024).rearrange("p (a n) -> p a n", a=4)
        sincos = uk
        q2 = ar(1024, 2048).rearrange("p (a n) -> p a n", a=4)
        ab = ar(1024, 2048).rearrange("p (t g n) -> p t g n", t=2, g=4)
        yT = uk
        ktok = ar(3072, 1024).rearrange("p (t h n) -> p t h n", t=2, h=4)
        hsum = ktok
        ctxT = ar(4096, 2048).rearrange("p (a n) -> p a n", a=8)
        vtok = ar(4096, 4 * 4 * 129).rearrange("p (t h n) -> p t h n", t=4, h=4)
        ctx_rows = ar(6144, 2048).rearrange("p (t n) -> p t n", t=2)
        k2 = ar(6160, 2048).rearrange("p (a n) -> p a n", a=4)
        xm = ar(8208, 4 * 2 * 258).rearrange("p (a s n) -> p a s n", a=4, s=2)
        state0 = ar(8208, 8 * 129).rearrange("p (j n) -> p j n", j=8)
        kw = ar(9240, 512).rearrange("p (i t n) -> p i t n", i=2, t=2)
        qc = ar(9752, 258).rearrange("p (i n) -> p i n", i=2)
        uf = ar(10272, 1024).rearrange("p (a n) -> p a n", a=4)
        pack2 = ar(11296, NPACK2)
        act2 = uT.rearrange("p a n -> p (a n)").rearrange("p (a n) -> p a n", a=4)
        v2 = sq.rearrange("p a n -> p (a n)").rearrange("p (a n) -> p a n", a=4)
        score = sb("score", [P, 3, T])
        prob = sb("prob", [P, 3, T])
        probT = sb("probT", [P, 2, 2, P])
        nmx = sb("nmx", [P, 4])
        rsum = sb("rsum", [P, 4])
        rinv = sb("rinv", [P, 4])
        gates = sb("gates", [P, NT, 48])
        iw = sb("iw", [P, NT, 8])
        bdv = probT.rearrange("p i j n -> p (i j n)")
        bdq, bdk = tmp[:, 0], tmp[:, 1]
        igr, lfr = score[:, 0:2], prob[:, 0:2]
        t1r = bdv.rearrange("p (s n) -> p s n", s=2)
        prer, br_ = b3v(tmp[:, 0]), b3v(tmp[:, 1])
        top8 = sb("top8", [P, 8])

        s_pack = sem("pack_in"); s_pos = sem("pos_in"); s_x = sem("x_in"); s_ctx = sem("ctx_in")
        s_sc = sem("sincos_in"); s_out = sem("out_stored")
        land = [sem(f"landed{i}") for i in range(NSLOT)]
        used = sem("chunks_used")
        res = sem("results")
        act_took = sem("act_took"); dve_took = sem("dve_took")
        vec = sem("vector_steps")
        consts = sem("consts_ready")
        s_cact = sem("c_activated")
        s_hT = sem("h_ready")
        s_ang = sem("angles_ready"); s_trig = sem("trig_ready")
        s_sq = sem("squares_ready"); s_norm = sem("normed")
        s_rope = sem("roped")
        s_relused = sem("relu_used")
        s_scored = sem("scored"); s_exp = sem("exponentials"); s_prob = sem("probs_normed")
        s_pv = sem("pv_done"); s_otook = sem("heads_taken")
        s_mod = sem("mods_ready")
        s_g = sem("gate_done"); s_u = sem("up_done"); s_sg = sem("silu_done")
        s_hid = sem("hidden_ready"); s_dn = sem("down_done"); s_y = sem("y_taken")
        s_xb = sem("windows_ready")
        s_top = sem("top_found"); s_e = sem("top_exponential"); s_lg = sem("gates_by_token")
        s_prod = sem("products_ready")
        s_fin = sem("final_rows")
        s_ctxT = sem("context_ready"); s_pad = sem("pads_zero"); s_blk = sem("blocks_ready")
        s_conv = sem("convolved"); s_act2 = sem("conv_activated")
        s_soft = sem("log_sigmoid_in"); s_softd = sem("log_sigmoid_out"); s_rows = sem("gate_rows_in")
        s_decay = sem("context_decays"); s_lat = sem("latent_rows_ready"); s_kw = sem("keys_weighted")
        s_max = sem("row_maxima"); s_gcol = sem("gate_columns_in"); s_gcold = sem("gate_columns_out")
        s_pexp = sem("gate_exponentials"); s_sm = sem("gated_scores"); s_var = sem("variances")
        s_std = sem("deviations"); s_hn = sem("heads_normed"); s_m = sem("mlstm_ready"); s_p2 = sem("pack2_in")

        ones = onesk
        ident = pk("ident")
        stream, state = [], {"slot": 0}
        landed = [0] * NSLOT
        place, freed = {}, {}

        def add(name, src, a, b, rel=None, slot=None):
            if slot is None:
                slot = state["slot"]
                state["slot"] = (slot + 1) % NSLOT
            landed[slot] += 1
            place[name] = (slot, 16 * landed[slot], a, b)
            freed[name] = rel
            stream.append((name, src))

        def kcols(w, c0, c1):
            return w.rearrange("(k p) n -> p k n", p=P)[:, :, c0:c1]

        def add_cols(name, w, c0, c1, **kw):
            add(name, kcols(w, c0, c1), w.shape[0] // P, c1 - c0, **kw)

        for c in range(12):
            add_cols(f"ada0.{c}", A["w_ada"][0], 512 * c, 512 * c + 512)
        w_in = A["a_w_in"][0]
        for n, (c0, c1) in enumerate(((0, 512), (512, 1024), (1024, 1536), (1536, 2048), (2048, 2120))):
            add_cols(f"win.{n}", w_in, c0, c1)
        ada_rest = [("ada1", A["w_ada"][1], c) for c in range(12)] + \
                   [("kvada", A["w_kv_ada"], c) for c in range(4)] + \
                   [("ada2", A["w_ada_2"][0], c) for c in range(12)]
        for n, w, c in ada_rest:
            add_cols(f"{n}.{c}", w, 512 * c, 512 * c + 512)
        for n in range(2):
            add_cols(f"wout.{n}", A["a_w_out"][0], 512 * n, 512 * n + 512)

        def add_ffn(tag, wg, wu, wd, F, half, slots=None):
            for c in range(-(-F // 512)):
                f0, f1 = 512 * c, min(512 * c + 512, F)
                end = half + -(-f1 // 256)
                sl = slots[3 * c:3 * c + 3] if slots else [None] * 3
                add_cols(f"{tag}.g{c}", wg, f0, f1, rel=(s_g, end), slot=sl[0])
                add_cols(f"{tag}.u{c}", wu, f0, f1, rel=(s_u, end), slot=sl[1])
                add(f"{tag}.d{c}", wd[f0:f1, :].rearrange("(k p) n -> p k n", p=P), (f1 - f0) // P, D,
                    rel=(s_dn, end), slot=sl[2])

        add_ffn("ffn", A["ffn_w_gate"][0], A["ffn_w_up"][0], A["ffn_w_down"][0], D_FF, 0)
        HALVES0 = D_FF // 256
        HPE = F1 // 256
        for n in range(3):
            add_cols(f"wkv.{n}", A["w_kv"], 512 * n, 512 * n + 512)
        for n, w in (("w1k", "cmp_w1_k"), ("w1v", "cmp_w1_v")):
            add(n, A[w].rearrange("(k p) n -> p k n", p=P), 16, 256)
        for n, (c0, c1) in enumerate(((0, 512), (512, 1024), (1024, 1072))):
            add_cols(f"wq.{n}", A["b_w_q"][0], c0, c1)
        for n in range(2):
            add_cols(f"bout.{n}", A["b_w_out"][0], 512 * n, 512 * n + 512)
        BEFORE_MOE1 = len(stream)
        SLOT1 = state["slot"]
        for e in range(E1):
            add_ffn(f"x{e}", A["moe_w_gate"][0, e], A["moe_w_up"][0, e], A["moe_w_down"][0, e], F1,
                    HALVES0 + HPE * e)
        AFTER_MOE1 = len(stream)
        HALVES1 = HALVES0 + HPE * E1
        for n in range(3):
            add_cols(f"win2.{n}", A["w_in_2"][0], 512 * n, 512 * n + 512)
        for n in range(2):
            add_cols(f"out2.{n}", A["w_out_2"][0], 512 * n, 512 * n + 512)
        BEFORE_MOE2 = len(stream)
        S2 = [(state["slot"] + i) % NSLOT for i in range(6)]
        for e in range(E2):
            add_ffn(f"z{e}", A["w_gate_2"][0, e], A["w_up_2"][0, e], A["w_down_2"][0, e], F2,
                    HALVES1 + 2 * e, slots=S2[3 * (e % 2):3 * (e % 2) + 3])

        jobs = []
        taken = {"A": 0, "V": 0}
        took_sem = {"A": act_took, "V": dve_took}
        seen = {"A": 0, "V": 0}
        mark = {}

        def open_job(pe, label, who):
            n = len(jobs)
            if n >= len(RR):
                _, w, k = jobs[n - len(RR)]
                pe.wait_ge(took_sem[w], k)
            taken[who] += 1
            jobs.append((label, who, taken[who]))
            mark.setdefault(label, []).append((took_sem[who], taken[who]))
            return psum[:, RR[n % len(RR)], :], mark[label][-1]

        def next_job(eng, label, who):
            n = [i for i, j in enumerate(jobs) if j[1] == who][seen[who]]
            assert jobs[n][0] == label, (jobs[n], label)
            seen[who] += 1
            eng.wait_ge(res, n + 1)
            return psum[:, RR[n % len(RR)], :]

        def b3(ap, a):
            return ap.rearrange("p (a n) -> p a n", a=a)

        def bc(ap, a):
            return ap.rearrange("p (a n) -> p a n", a=1).to_broadcast([ap.shape[0], a, ap.shape[1]])

        ATT = {"dsa": 32, "nsa": 96}
        att_base = {"dsa": 0, "nsa": 32}

        def att_units(kind):
            if kind == "dsa":
                return [(h, t, 0, P * (t + 1)) for h in range(NH) for t in range(NT)]
            return [(h, t, b, NCMP if b == 0 else P * (t + 1)) for h in range(NH) for t in range(NT) for b in range(3)]

        cw = ar(3072, 1024).rearrange("p (i g n) -> p i g n", i=2, g=4)
        abv = ar(1024, 2048).rearrange("p (t c g n) -> p t c g n", t=2, c=2, g=4)
        M_SCALE = DH ** -0.5

        def srange(j, t):
            return (0, P * (t + 1)) if j < MH else (P * t, T)

        def mlstm_units():
            return [(j, t) for j in range(8) for t in range(NT)]

        block = ctx.enter_context(nc.Block())

        @block.tensor
        def _(pe):
            def chunk(name):
                slot, val, a, b = place[name]
                pe.wait_ge(land[slot], val)
                return ring[:, slot, 0:a * b].rearrange("p (a b) -> p a b", a=a)

            def ada(name, c, base, rhs, w):
                wt = chunk(f"{name}.{c}")
                for j in range(4):
                    o = base + (4 * c + j) * w
                    for k in range(KT):
                        mm = pe.matmul(psum[:, 0, o:o + w], wt[:, k, P * j:P * j + P], rhs[:, k, :],
                                       start=(k == 0), stop=(k == KT - 1))
                mm.then_inc(used, 1)
                ada.n += 1
                freed[f"{name}.{c}"] = (used, ada.n)
            ada.n = 0

            def norm():
                b, _ = open_job(pe, "ms", "A")
                norm.n += 1
                pe.wait_ge(s_sq, norm.n)
                for k in range(KT):
                    mm = pe.matmul(b[:, 0:T], ones[:], sq[:, k, :], start=(k == 0), stop=(k == KT - 1))
                mm.then_inc(res, 1)
            norm.n = 0

            def proj(label, who, wt, c0, nblk, X, rows=P, last=False, kt=KT):
                b, took = open_job(pe, label, who)
                for j in range(nblk):
                    for k in range(kt):
                        mm = pe.matmul(b[0:rows, T * j:T * j + T], wt[:, k, c0 + P * j:c0 + P * j + rows],
                                       X[:, k, :], start=(k == 0), stop=(k == kt - 1))
                mm.then_inc(res, 1)
                return took

            def tokproj(label, who, wt, c0, w, X):
                b, took = open_job(pe, label, who)
                for t in range(NT):
                    for k in range(KT):
                        mm = pe.matmul(b[:, w * t:w * t + w], X[:, k, P * t:P * t + P], wt[:, k, c0:c0 + w],
                                       start=(k == 0), stop=(k == KT - 1))
                mm.then_inc(res, 1)
                return took

            def frees(name):
                freed[name] = (res, len(jobs))

            def transposes_in(rows, signal, val):
                pe.wait_ge(signal, val)
                for t in range(NT):
                    for g in range(2):
                        b, _ = open_job(pe, "xT", "V")
                        for k in range(4):
                            mm = pe.transpose(b[:, P * k:P * k + P], rows[:, t, P * (4 * g + k):P * (4 * g + k) + P],
                                              ident)
                        mm.then_inc(res, 1)

            def rope_unit(kind, r):
                pe.wait_ge(*mark["raw"][r])
                src = raw[:, r % 2]
                if kind == "pair":
                    b, _ = open_job(pe, "rot", "V")
                    pe.matmul(b, pk("rot"), src, start=True, stop=True).then_inc(res, 1)
                elif kind in ("dup", "vdup"):
                    for j in range(2):
                        for m in (("dup", "rotdup") if kind == "dup" else ("dup",)):
                            b, _ = open_job(pe, m, "V")
                            for i in range(2):
                                mm = pe.matmul(b[:, T * i:T * i + T], pk(f"{m}{i}"), src[:, j, :], start=True, stop=True)
                            mm.then_inc(res, 1)
                else:
                    for m in ("dup0", "rotdup0"):
                        b, _ = open_job(pe, m, "V")
                        pe.matmul(b[:, 0:T], pk(m)[0:HD, :], src[0:HD, 0, :], start=True, stop=True).then_inc(res, 1)

            def attention(kind, ks, vs, extra=None):
                units = att_units(kind)
                base = att_base[kind]
                pt = {}
                for s in range(len(units) + 3):
                    if s < len(units):
                        h, t, br, L = units[s]
                        b, _ = open_job(pe, "S", "V")
                        r = (h % 2) * HD
                        pe.matmul(b[:, 0:L], qT[r:r + HD, h // 2, P * t:P * t + P], ks[br](r, h // 4, L),
                                  start=True, stop=True).then_inc(res, 1)
                    if extra and s in extra:
                        extra[s]()
                    if 2 <= s < len(units) + 2:
                        h, t, br, L = units[s - 2]
                        b, pt[s - 2] = open_job(pe, "T", "A")
                        pe.wait_ge(s_prob, base + s - 1)
                        for j in range(-(-L // P)):
                            w = min(P, L - P * j)
                            mm = pe.transpose(b[0:w, P * j:P * j + P], prob[:, (s - 2) % 3, P * j:P * j + w], ident)
                        mm.then_inc(res, 1)
                    if s >= 3:
                        u = s - 3
                        h, t, br, L = units[u]
                        pair = h // 2
                        first = (h % 2 == 0 and t == 0 and br == 0)
                        if first and pair >= 2:
                            pe.wait_ge(s_otook, base_pair(kind) + pair - 1)
                        pe.wait_ge(*pt.pop(u))
                        nbr = 1 if kind == "dsa" else 3
                        r = (h % 2) * HD
                        o = psum[r:r + HD, 6 + pair % 2, P * t:P * t + P]
                        nk = -(-L // P)
                        for j in range(nk):
                            w = min(P, L - P * j)
                            mm = pe.matmul(o, vs[br](w, j, h // 4), probT[0:w, u % 2, j, :],
                                           start=(br == 0 and j == 0), stop=(br == nbr - 1 and j == nk - 1))
                        mm.then_inc(s_pv, 1)

            def base_pair(kind):
                return 0 if kind == "dsa" else NH // 2

            def ffn(names, half, ntot, X, acc_first=True, acc_last=True):
                def down(h):
                    dchunk = names[h // 2][2]
                    pe.wait_ge(s_hid, half + h + 1)
                    if h % 2 == 0:
                        down.w = dchunk()
                    for f in range(2):
                        for j in range(KT):
                            st = acc_first and h == 0 and f == 0
                            mm = pe.matmul(psum[:, 4 + j // 2, T * (j % 2):T * (j % 2) + T],
                                           down.w[:, 2 * (h % 2) + f, P * j:P * j + P], hid[:, h % 2, f, :],
                                           start=(st and j % 2 == 0),
                                           stop=(acc_last and h == ntot - 1 and f == 1), skip_group_check=True)
                    mm.then_inc(s_dn, 1)

                for h in range(ntot):
                    if h % 2 == 0:
                        ffn.g = names[h // 2][0]()
                    if not (isinstance(half, int) and half + h < 2):
                        pe.wait_ge(s_sg, half + h - 1)
                    for f in range(2):
                        for k in range(KT):
                            mm = pe.matmul(psum[:, h % 2, T * f:T * f + T], ffn.g[:, k, 256 * (h % 2) + P * f:256 * (h % 2) + P * f + P],
                                           X[:, k, :], start=(k == 0), stop=(k == KT - 1), skip_group_check=True)
                    mm.then_inc(s_g, 1)
                    if h % 2 == 0:
                        ffn.u = names[h // 2][1]()
                    if not (isinstance(half, int) and half + h < 2):
                        pe.wait_ge(s_hid, half + h - 1)
                    for f in range(2):
                        for k in range(KT):
                            mm = pe.matmul(psum[:, 2 + h % 2, T * f:T * f + T], ffn.u[:, k, 256 * (h % 2) + P * f:256 * (h % 2) + P * f + P],
                                           X[:, k, :], start=(k == 0), stop=(k == KT - 1), skip_group_check=True)
                    mm.then_inc(s_u, 1)
                    if h >= 1:
                        down(h - 1)
                down(ntot - 1)

            def static_names(tag, n):
                return [[(lambda nm=f"{tag}.{x}{c}": chunk(nm)) for x in "gud"] for c in range(n)]

            def settle():
                pe.wait_ge(act_took, taken["A"])
                pe.wait_ge(dve_took, taken["V"])

            def zero_sums():
                for i in range(4):
                    pe.matmul(psum[:, 4 + i, :], zeros[:], pk("causal"), start=True, stop=False,
                              skip_group_check=True)

            def router(X, w, E):
                b, _ = open_job(pe, "router", "V")
                wr = pk(w, KT)
                for t in range(NT):
                    for k in range(KT):
                        mm = pe.matmul(b[:, E * t:E * t + E], X[:, k, P * t:P * t + P], wr[:, k, :],
                                       start=(k == 0), stop=(k == KT - 1))
                mm.then_inc(res, 1)

            def gate_rows(E, n):
                pe.wait_ge(s_lg, n)
                gt = small[:, 0:NT, 0:E]
                for e in range(0, E, 2):
                    b, _ = open_job(pe, "gb", "A")
                    for i in range(2):
                        for t in range(NT):
                            mm = pe.matmul(b[:, T * i + P * t:T * i + P * t + P],
                                           gt[:, t, e + i:e + i + 1].to_broadcast([P, P]), ident, start=True, stop=True)
                    mm.then_inc(res, 1)

            pe.wait_ge(s_pack, 16)
            pe.wait_ge(consts, 1)
            transposes_in(uk_rows, s_x, 16)
            pe.wait_ge(s_cact, 1)
            c1 = cact[:, 0:KT].rearrange("p (k a) -> p k a", a=1)
            c2 = cact[:, KT:3 * KT].rearrange("p (k a) -> p k a", a=2)
            for c in range(12):
                ada("ada0", c, 0, c1, 1)
            norm()
            pe.wait_ge(s_norm, 1)
            w = chunk("win.0")
            proj("raw", "A", w, 0, 2, uT)
            proj("raw", "A", w, 256, 2, uT)
            frees("win.0")
            rope_unit("pair", 0)
            w = chunk("win.1")
            proj("raw", "A", w, 0, 2, uT)
            rope_unit("pair", 1)
            proj("raw", "A", w, 256, 2, uT)
            frees("win.1")
            rope_unit("pair", 2)
            w = chunk("win.2")
            proj("raw", "A", w, 0, 2, uT)
            rope_unit("pair", 3)
            tokproj("v", "A", w, 256, 256, uT)
            frees("win.2")
            rope_unit("dup", 4)
            w = chunk("win.3")
            proj("raw", "A", w, 0, 2, uT)
            rope_unit("pair", 5)
            proj("raw", "A", w, 256, 2, uT)
            frees("win.3")
            rope_unit("pair", 6)
            w = chunk("win.4")
            proj("raw", "A", w, 0, 1, uT, rows=HD)
            tokproj("iw", "V", w, 64, 8, uT)
            frees("win.4")
            rope_unit("one", 7)
            pe.wait_ge(s_rope, 8)
            for t in range(NT):
                L = P * (t + 1)
                for h in range(IDX_H):
                    b, _ = open_job(pe, "I", "A")
                    r = (h % 2) * HD
                    pe.matmul(b[:, 0:L], iqT[r:r + HD, h // 2, P * t:P * t + P], ikd[r:r + HD, 0:L],
                              start=True, stop=True).then_inc(res, 1)
            pe.wait_ge(*mark["v"][0])
            bases = {"ada1": (48, c1, 1), "kvada": (96, c1, 1), "ada2": (112, c2, 2)}
            extra = {i: (lambda n=n, c=c: ada(n, c, *bases[n])) for i, (n, _, c) in enumerate(ada_rest)}
            attention("dsa", [lambda r, g, L: kd[r:r + HD, 0, g, 0:L]],
                      [lambda w, j, g: vt[0:w, 0, j, HD * g:HD * g + HD]], extra)
            pe.wait_ge(s_otook, 8)
            for n in range(2):
                w = chunk(f"wout.{n}")
                for i in range(2):
                    proj("mix", "V", w, 256 * i, 2, oT)
                frees(f"wout.{n}")
            norm()
            settle()
            pe.wait_ge(s_mod, 4)
            pe.wait_ge(s_norm, 2)
            ffn(static_names("ffn", 6), 0, HALVES0, uT)
            pe.wait_ge(s_y, 1)
            norm()
            pe.wait_ge(s_norm, 3)
            w = chunk("wkv.0")
            proj("raw", "A", w, 0, 2, uk)
            proj("raw", "A", w, 256, 2, uk)
            frees("wkv.0")
            rope_unit("dup", 8)
            w = chunk("wkv.1")
            proj("raw", "A", w, 0, 2, uk)
            rope_unit("vdup", 9)
            tokproj("v", "A", w, 256, 256, uk)
            frees("wkv.1")
            rope_unit("dup", 10)
            w = chunk("wkv.2")
            proj("raw", "A", w, 0, 2, uk)
            tokproj("v", "A", w, 256, 256, uk)
            frees("wkv.2")
            rope_unit("dup", 11)
            for n, nm in enumerate(("w1k", "w1v")):
                w = chunk(nm)
                b, _ = open_job(pe, "w1", "A")
                pe.wait_ge(s_xb, n + 1)
                for cb in range(2):
                    for j in range(16):
                        mm = pe.matmul(b[:, 60 * cb:60 * cb + 60], w[:, j, P * cb:P * cb + P], xb[:, j, :, :],
                                       start=(j == 0), stop=(j == 15))
                mm.then_inc(res, 1)
                frees(nm)
            w2k, w2v = pk("w2k", 2), pk("w2v", 2)
            pe.wait_ge(*mark["w1"][1])
            b, _ = open_job(pe, "kc", "V")
            for cb in range(2):
                mm = pe.matmul(b[:, 0:60], w2k[:, cb, :], hid60[:, 0, cb, :], start=(cb == 0), stop=(cb == 1))
            mm.then_inc(res, 1)
            b, _ = open_job(pe, "vc", "V")
            for g in range(NKV):
                for cb in range(2):
                    mm = pe.matmul(b[0:NCMP, HD * g:HD * g + HD], hid60[:, 1, cb, NCMP * g:NCMP * g + NCMP],
                                   w2v[:, cb, :], start=(cb == 0), stop=(cb == 1))
            mm.then_inc(res, 1)
            w = chunk("wq.0")
            proj("raw", "A", w, 0, 2, uT)
            proj("raw", "A", w, 256, 2, uT)
            frees("wq.0")
            rope_unit("pair", 12)
            w = chunk("wq.1")
            proj("raw", "A", w, 0, 2, uT)
            rope_unit("pair", 13)
            proj("raw", "A", w, 256, 2, uT)
            frees("wq.1")
            rope_unit("pair", 14)
            w = chunk("wq.2")
            tokproj("gates", "A", w, 0, 48, uT)
            frees("wq.2")
            rope_unit("pair", 15)
            pe.wait_ge(s_rope, 16)
            pe.wait_ge(*mark["vc"][0])
            pe.wait_ge(*mark["v"][2])
            attention("nsa",
                      [lambda r, g, L: kcT[r:r + HD, g, :], lambda r, g, L: kd[r:r + HD, 1, g, 0:L],
                       lambda r, g, L: kd[r:r + HD, 2, g, 0:L]],
                      [lambda w, j, g: vc[0:w, g, :], lambda w, j, g: vt[0:w, 0, j, HD * g:HD * g + HD],
                       lambda w, j, g: vt[0:w, 1, j, HD * g:HD * g + HD]])
            pe.wait_ge(s_otook, 16)
            for n in range(2):
                w = chunk(f"bout.{n}")
                for i in range(2):
                    proj("mix", "V", w, 256 * i, 2, oT)
                frees(f"bout.{n}")
            norm()
            pe.wait_ge(s_norm, 4)
            router(uT, "router", E1)
            gate_rows(E1, 1)
            settle()
            zero_sums()
            with pe.Fori(0, E1 // 2) as e:
                def loop_chunk(nm):
                    slot, val, a, b = place[nm]
                    pe.wait_ge(land[slot], 112 * e + val)
                    return ring[:, slot, 0:a * b].rearrange("p (a b) -> p a b", a=a)
                names = [[(lambda nm=f"x{i}.{x}{c}": loop_chunk(nm)) for x in "gud"] for i in range(2) for c in range(7)]
                ffn(names, 2 * HPE * e + HALVES0, 2 * HPE, uT, acc_first=False, acc_last=False)
            pe.wait_ge(s_y, 2)
            norm()
            pe.wait_ge(s_norm, 5)
            pe.wait_ge(s_ctx, 16)
            for t in range(NT):
                for g in range(2):
                    b, _ = open_job(pe, "xT", "V")
                    for k in range(4):
                        mm = pe.transpose(b[:, P * k:P * k + P], ctx_rows[:, t, P * (4 * g + k):P * (4 * g + k) + P], ident)
                    mm.then_inc(res, 1)
            norm()
            norm()
            pe.wait_ge(s_norm, 7)
            w = chunk("win2.0")
            for j in range(MH):
                b, _ = open_job(pe, "xm", "A")
                for sgm, X in enumerate((uT, ctxT)):
                    for k in range(KT):
                        mm = pe.matmul(b[:, T * sgm:T * sgm + T], w[:, k, P * j:P * j + P], X[:, k, :],
                                       start=(k == 0), stop=(k == KT - 1))
                mm.then_inc(res, 1)
            frees("win2.0")
            for n, label in ((1, "z"), (2, "uf")):
                w = chunk(f"win2.{n}")
                proj(label, "A", w, 0, 2, uT)
                proj(label, "A", w, 256, 2, uT)
                frees(f"win2.{n}")
            pe.wait_ge(s_p2, 16)
            wf, dc = pk("wfour", 4) if False else pk2("wfour", 4), pk2("dftc")
            for i in range(2):
                b, _ = open_job(pe, "cw", "A")
                mm = pe.matmul(b, dc[:, P * i:P * i + P], pk2("wfour"), start=True, stop=True)
                mm.then_inc(res, 1)
            pe.wait_ge(*mark["uf"][1])
            pe.wait_ge(*mark["cw"][1])
            for t in range(NT):
                for i in range(2):
                    b, _ = open_job(pe, "ab", "A")
                    for g in range(4):
                        mm = pe.matmul(b[:, P * g:P * g + P], uf[:, g, P * t:P * t + P],
                                       cw[:, i, g, :], start=True, stop=True)
                    mm.then_inc(res, 1)
            pe.wait_ge(*mark["ab"][3])
            dt_ = (pk2("dftt", 2), pk2("dfts", 2))
            for gp in range(2):
                b, _ = open_job(pe, "fT", "A")
                for i in range(2):
                    g = 2 * gp + i
                    for c in range(2):
                        for t in range(NT):
                            mm = pe.matmul(b[:, T * i:T * i + T], abv[:, t, c, g, :], dt_[c][:, t, :],
                                           start=(c == 0 and t == 0), stop=(c == 1 and t == 1))
                mm.then_inc(res, 1)
            pe.wait_ge(s_blk, 1)
            pe.wait_ge(*mark["xm"][3])
            for label, bd, dst in (("v2", bdv, v2),):
                for j in range(MH):
                    b, _ = open_job(pe, label, "A")
                    for sgm in range(2):
                        mm = pe.matmul(b[:, T * sgm:T * sgm + T], bd[:, P * j:P * j + P], xm[:, j, sgm, 1:1 + T],
                                       start=True, stop=True)
                    mm.then_inc(res, 1)
            for tt_ in range(4):
                b, _ = open_job(pe, "vtok", "A")
                for j in range(MH):
                    o = 1 + P * (tt_ % 2)
                    mm = pe.matmul(b[:, P * j:P * j + P], xm[:, j, tt_ // 2, o:o + P], bdv[:, P * j:P * j + P],
                                   start=True, stop=True)
                mm.then_inc(res, 1)
            pe.wait_ge(s_act2, 4)
            for label, bd in (("q2", bdq), ("k2", bdk)):
                for j in range(MH):
                    b, _ = open_job(pe, label, "A")
                    pe.matmul(b, bd[:, P * j:P * j + P], act2[:, j, :], start=True, stop=True).then_inc(res, 1)
            for tt_ in range(2):
                b, _ = open_job(pe, "ktok", "A")
                for j in range(MH):
                    mm = pe.matmul(b[:, P * j:P * j + P], act2[:, j, T + P * tt_:T + P * tt_ + P], bdk[:, P * j:P * j + P],
                                   start=True, stop=True)
                mm.then_inc(res, 1)
            pe.wait_ge(*mark["k2"][3])
            wif = pk("wif").rearrange("p (b i n) -> p b i n", b=12, i=2)
            for i in range(2):
                b, _ = open_job(pe, "gate8", "V")
                for n, X in enumerate((q2, k2, v2)):
                    for j in range(MH):
                        mm = pe.matmul(b[0:8, :], wif[:, 4 * n + j, i, :], X[:, j, :], start=(n == 0 and j == 0),
                                       stop=(n == 2 and j == 3))
                mm.then_inc(res, 1)
            pe.wait_ge(s_decay, 1)
            pe.wait_ge(s_lat, 1)
            b, _ = open_job(pe, "gcols", "V")
            for t in range(NT):
                pe.transpose(b[:, 8 * t:8 * t + 8], t1r[0:8, 1, P * t:P * t + P], ident[0:8, 0:8])
                pe.transpose(b[:, 16 + 8 * t:24 + 8 * t], br_[0:8, 0, P * t:P * t + P], ident[0:8, 0:8])
            pe.matmul(b[:, 32:40], cols[0:8, 60:61].to_broadcast([8, P]), ident[0:8, 0:8], start=True,
                      stop=True).then_inc(res, 1)

            def gate_scores(b, j, t):
                s0, s1 = srange(j, t)
                m = pk("causal", NT) if j < MH else pk2("anticausal", NT)
                pe.matmul(b[:, 0:s1 - s0], ident[0:8, j:j + 1].to_broadcast([8, P]), rstd[0:8, s0:s1], start=True, stop=False)
                return pe.matmul(b[:, 0:s1 - s0], ident, m[:, t, s0:s1], start=False, stop=True)

            for j in range(8):
                for t in range(NT):
                    b, _ = open_job(pe, "r1", "V")
                    gate_scores(b, j, t).then_inc(res, 1)
            for j in range(8):
                b, _ = open_job(pe, "c0", "A")
                pe.wait_ge(s_kw, j + 1)
                for t in range(NT):
                    mm = pe.matmul(b[:, 0:129], kw[:, j % 2, t, :], vtok[:, 2 + t, j % 4, :], start=(t == 0), stop=(t == 1))
                mm.then_inc(res, 1)
            pe.wait_ge(*mark["c0"][7])
            units = mlstm_units()
            for s in range(len(units) + 3):
                if s < len(units):
                    j, t = units[s]
                    s0, s1 = srange(j, t)
                    b, _ = open_job(pe, "r2", "A")
                    gate_scores(b, j, t).then_inc(res, 1)
                    b, _ = open_job(pe, "qk", "V")
                    pe.matmul(b[:, 0:s1 - s0], q2[:, j % 4, P * t:P * t + P], k2[:, j % 4, s0:s1], start=True,
                              stop=True).then_inc(res, 1)
                if 2 <= s < len(units) + 2:
                    u = s - 2
                    j, t = units[u]
                    s0, s1 = srange(j, t)
                    b, _ = open_job(pe, "sT", "A")
                    pe.wait_ge(s_sm, u + 1)
                    for i in range((s1 - s0) // P):
                        mm = pe.transpose(b[:, P * i:P * i + P], prob[:, u % 3, P * i:P * i + P], ident)
                    mm.then_inc(res, 1)
                if s >= 3:
                    u = s - 3
                    j, t = units[u]
                    s0, s1 = srange(j, t)
                    b, _ = open_job(pe, "num", "V")
                    pe.wait_ge(*mark["sT"][u])
                    n = (s1 - s0) // P
                    for i in range(n):
                        pe.matmul(b[:, 0:P], probT[:, u % 2, i, :], vtok[:, s0 // P + i, j % 4, 0:P], start=(i == 0),
                                  stop=(i == n - 1))
                    pe.matmul(b[:, 256:385], q2[:, j % 4, P * t:P * t + P], state0[:, j, :], start=True,
                              stop=True).then_inc(res, 1)
            pe.wait_ge(s_hn, 1)
            for hp in range(2):
                b, _ = open_job(pe, "hT", "V")
                for i in range(2):
                    for t in range(NT):
                        mm = pe.transpose(b[:, T * i + P * t:T * i + P * t + P], hsum[:, t, 2 * hp + i, :], ident)
                mm.then_inc(res, 1)
            pe.wait_ge(s_m, 1)
            pe.wait_ge(*mark["fT"][1])
            for n in range(2):
                w = chunk(f"out2.{n}")
                for i in range(2):
                    b, _ = open_job(pe, "y", "A")
                    for jj in range(2):
                        for k in range(KT):
                            X = sq[:, k, :] if k < 4 else uf[:, k - 4, :]
                            mm = pe.matmul(b[:, T * jj:T * jj + T], w[:, k, 256 * i + P * jj:256 * i + P * jj + P], X,
                                           start=(k == 0), stop=(k == KT - 1))
                    mm.then_inc(res, 1)
                frees(f"out2.{n}")
            norm()
            norm()
            pe.wait_ge(s_norm, 9)
            router(uT, "router2", 20)
            gate_rows(E2, 2)
            settle()
            zero_sums()
            with pe.Fori(0, E2 // 2) as e:
                def loop_chunk2(nm):
                    slot, val, a, b = place[nm]
                    pe.wait_ge(land[slot], 16 * e + val)
                    return ring[:, slot, 0:a * b].rearrange("p (a b) -> p a b", a=a)
                names = [[(lambda nm=f"z{i}.{x}0": loop_chunk2(nm)) for x in "gud"] for i in range(2)]
                ffn(names, 4 * e + HALVES1, 4, uT, acc_first=False, acc_last=False)
            pe.wait_ge(s_y, 3)
            norm()
            pe.wait_ge(s_hT, 8)
            for t in range(NT):
                for g in range(2):
                    b, _ = open_job(pe, "oT", "V")
                    for k in range(4):
                        mm = pe.transpose(b[:, P * k:P * k + P], hT[:, 4 * g + k, P * t:P * t + P], ident)
                    mm.then_inc(res, 1)

        @block.scalar
        def _(act):
            def copy_job(label, dst, view):
                b = next_job(act, label, "A")
                act.activation(dst, view(b), ACT.Copy).then_inc(act_took, 1)

            def norm(X, ready):
                act.wait_ge(*ready)
                if norm.n:
                    act.wait_ge(s_norm, norm.n)
                norm.n += 1
                act.activation(sq[:], X[:], ACT.Square).then_inc(s_sq, 1)
                b = next_job(act, "ms", "A")
                act.activation(root[:], b[:, 0:T], ACT.Sqrt, bias=epsc[:, 0:1]).then_inc(act_took, 1)

            norm.n = 0

            def raws(r, rows=P, n=2):
                if r >= 2:
                    act.wait_ge(s_rope, r - 1)
                copy_job("raw", raw[0:rows, r % 2, 0:n, :], lambda b: b3(b, 2)[0:rows, 0:n, :])

            def attention(kind):
                units, base = att_units(kind), att_base[kind]
                nbr = 1 if kind == "dsa" else 3
                for s in range(len(units) + 3):
                    if s < len(units):
                        h, t, br, L = units[s]
                        act.wait_ge(s_scored, base + s + 1)
                        act.activation(prob[:, s % 3, 0:L], score[:, s % 3, 0:L], ACT.Exp, bias=nmx[:, s % 4:s % 4 + 1],
                                       accum_out=rsum[:, s % 4:s % 4 + 1]).then_inc(s_exp, 1)
                    if 2 <= s < len(units) + 2:
                        u = s - 2
                        h, t, br, L = units[u]
                        b = next_job(act, "T", "A")
                        if base + u >= 2:
                            act.wait_ge(s_pv, base + u - 1)
                        w = min(P, L)
                        n = -(-L // P)
                        act.activation(probT[0:w, u % 2, 0:n, :], b3(b, 4)[0:w, 0:n, :], ACT.Copy).then_inc(act_took, 1)
                    if s >= 3 and (s - 3) % (4 * nbr) == 4 * nbr - 1:
                        pair = (s - 3) // (4 * nbr)
                        act.wait_ge(s_pv, base + s - 2)
                        act.activation(oT[:, pair, :], psum[:, 6 + pair % 2, 0:T], ACT.Copy).then_inc(s_otook, 1)

            def silu(half, n):
                for h in range(n):
                    act.wait_ge(s_g, half + h + 1)
                    if not (isinstance(half, int) and half + h < 2):
                        act.wait_ge(s_hid, half + h - 1)
                    act.activation(sg[:, h % 2], b3(psum[:, h % 2, :], 2), ACT.Silu).then_inc(s_sg, 1)

            def top(n):
                act.wait_ge(s_top, n)
                act.activation(small[:, 5:7, 0:1], small[:, 5:7, 0:1], ACT.Exp).then_inc(s_e, 1)

            act.dma_start(pack[:], A["pack"][:, :]).then_inc(s_pack, 16)
            act.dma_start(uk_rows, A["x"][0].rearrange("(t p) n -> p t n", p=P)).then_inc(s_x, 16)
            act.dma_start(posi[:], A["positions"][0:1, :].partition_broadcast(P) if False else A["positions"][0:1, :].to_broadcast([P, T])).then_inc(s_pos, 16)
            act.wait_ge(s_pack, 16)
            co = OFF["c"][0]
            act.activation(cact[:], pack[:, co:co + 3 * KT], ACT.Silu).then_inc(s_cact, 1)
            act.wait_ge(s_ang, 1)
            act.activation(trig[:], ang[:, 0:2, :], ACT.Sin).then_inc(s_trig, 1)
            norm(hT, (s_hT, 1))
            for r in range(5):
                raws(r)
            copy_job("v", vt[:, 0], lambda b: b3(b, 2))
            raws(5)
            raws(6)
            raws(7, rows=HD, n=1)
            for t in range(NT):
                L = P * (t + 1)
                for h in range(IDX_H):
                    b = next_job(act, "I", "A")
                    i = IDX_H * t + h
                    if i >= 2:
                        act.wait_ge(s_relused, i - 1)
                    act.activation(rel[:, i % 2, 0:L], b[:, 0:L], ACT.Relu).then_inc(act_took, 1)
            attention("dsa")
            norm(hT, (s_hT, 2))
            silu(0, HALVES0)
            norm(hT, (s_hT, 3))
            raws(8)
            raws(9)
            raws(10)
            copy_job("v", vt[:, 0], lambda b: b3(b, 2))
            raws(11)
            copy_job("v", vt[:, 1], lambda b: b3(b, 2))
            for n in range(2):
                copy = next_job(act, "w1", "A")
                act.activation(hid60[:, n], copy[:, 0:120].rearrange("p (c n) -> p c n", c=2),
                               ACT.Gelu_apprx_tanh).then_inc(act_took, 1)
            for r in range(12, 16):
                raws(r)
            b = next_job(act, "gates", "A")
            act.activation(gates[:], b[:, 0:96].rearrange("p (t n) -> p t n", t=2), ACT.Sigmoid).then_inc(act_took, 1)
            attention("nsa")
            norm(hT, (s_hT, 4))
            act.dma_start(sincos[:], A["sincos"][:, :, :]).then_inc(s_sc, 16)
            act.dma_start(pack2, A["pack2"][:, :]).then_inc(s_p2, 16)
            top(1)
            for e in range(0, E1, 2):
                copy_job("gb", gb[:, e:e + 2, :], lambda b: b3(b, 2))
            act.dma_start(ctx_rows, A["ctx_2"][0].rearrange("(t p) n -> p t n", p=P)).then_inc(s_ctx, 16)
            with act.Fori(0, E1 // 2) as e:
                silu(2 * HPE * e + HALVES0, 2 * HPE)
            norm(hT, (s_hT, 5))
            norm(hT, (s_hT, 6))
            norm(ctxT, (s_ctxT, 1))
            act.wait_ge(s_pad, 1)
            for j in range(MH):
                copy_job("xm", xm[:, j, :, 1:1 + T], lambda b: b3(b, 2))
            for i in range(2):
                b = next_job(act, "z", "A")
                act.activation(zs[:, 2 * i:2 * i + 2, :], b3(b, 2), ACT.Silu).then_inc(act_took, 1)
            for i in range(2):
                copy_job("uf", uf[:, 2 * i:2 * i + 2, :], lambda b: b3(b, 2))
            for i in range(2):
                copy_job("cw", cw[:, i], lambda b: b3(b, 4))
            for t in range(NT):
                for i in range(2):
                    copy_job("ab", abv[:, t, i], lambda b: b3(b, 4))
            for i in range(2):
                copy_job("fT", uf[:, 2 * i:2 * i + 2, :], lambda b: b3(b, 2))
            for j in range(MH):
                copy_job("v2", v2[:, j, :], lambda b: b)
            for i in range(4):
                copy_job("vtok", vtok[:, i, :, 0:P], lambda b: b3(b, 4))
            for j in range(MH):
                act.wait_ge(s_conv, j + 1)
                act.activation(act2[:, j, :], act2[:, j, :], ACT.Silu).then_inc(s_act2, 1)
            for dst, label in ((q2, "q2"), (k2, "k2")):
                for j in range(MH):
                    copy_job(label, dst[:, j, :], lambda b: b)
            for i in range(2):
                copy_job("ktok", ktok[:, i], lambda b: b3(b, 4))
            act.wait_ge(s_soft, 1)
            act.activation(t1r[0:8], t1r[0:8], ACT.Exp).then_inc(s_softd, 1)
            act.wait_ge(s_softd, 1)
            act.activation(t1r[0:8], t1r[0:8], ACT.Ln, bias=1.0).then_inc(s_softd, 1)
            act.wait_ge(s_rows, 1)
            act.activation(t1r[0:8, 1, :], t1r[0:8, 1, :], ACT.Exp, bias=cols[0:8, 61:62]).then_inc(s_decay, 1)
            for j in range(8):
                copy_job("c0", state0[:, j, :], lambda b: b[:, 0:129])
            act.wait_ge(s_gcol, 1)
            act.activation(small[:, 0:4, 16:32].rearrange("p a n -> p a n"), small[:, 0:4, 16:32], ACT.Exp).then_inc(s_gcold, 1)
            units = mlstm_units()
            for s in range(len(units) + 2):
                if s < len(units):
                    j, t = units[s]
                    s0, s1 = srange(j, t)
                    b = next_job(act, "r2", "A")
                    if s >= 3:
                        act.wait_ge(s_sm, s - 2)
                    act.activation(score[:, s % 3, 0:s1 - s0], b[:, 0:s1 - s0], ACT.Exp,
                                   bias=small[:, 4, 16 + 8 * t + j:17 + 8 * t + j]).then_inc(act_took, 1)
                if s >= 2:
                    u = s - 2
                    j, t = units[u]
                    s0, s1 = srange(j, t)
                    n = (s1 - s0) // P
                    if u >= 2:
                        act.wait_ge(*mark["num"][u - 2])
                    b = next_job(act, "sT", "A")
                    act.activation(probT[:, u % 2, 0:n, :], b3(b, 4)[:, 0:n, :], ACT.Copy).then_inc(act_took, 1)
            act.wait_ge(s_var, 1)
            act.activation(cols[:, 0:8], cols[:, 0:8], ACT.Sqrt, bias=epsc[:, 0:1]).then_inc(s_std, 1)
            for i in range(4):
                copy_job("y", yT[:, 2 * i:2 * i + 2, :], lambda b: b3(b, 2))
            norm(yT, mark["y"][3])
            norm(hT, (s_hT, 7))
            act.wait_ge(s_top, 2)
            act.activation(small[:, 5:7, 0:4], small[:, 5:7, 0:4], ACT.Exp).then_inc(s_e, 1)
            act.wait_ge(s_top, 3)
            act.activation(small[:, 5:7, 0:1], small[:, 5:7, 0:1], ACT.Exp).then_inc(s_e, 1)
            for e in range(0, E2, 2):
                copy_job("gb", gb[:, e:e + 2, :], lambda b: b3(b, 2))
            with act.Fori(0, E2 // 2) as e:
                silu(4 * e + HALVES1, 4)
            norm(yT, (s_y, 3))

        @block.vector
        def _(dve):
            count = {}

            def V(ins, s=None):
                s = s or vec
                count[s] = count.get(s, 0) + 1
                ins.then_inc(s, 1)
                dve.wait_ge(s, count[s])

            def N(ins, s):
                count[s] = count.get(s, 0) + 1
                ins.then_inc(s, 1)

            tt, ts, stt = dve.tensor_tensor, dve.tensor_scalar, dve.scalar_tensor_tensor

            def norm(n, X, outs):
                dve.wait_ge(*mark["ms"][n])
                V(dve.reciprocal(rstd[:], root[:]))
                V(tt(xn[:], X[:], bc(rstd[:], KT), ALU.mult))
                for i, (dst, g, s) in enumerate(outs):
                    for k in range(KT):
                        if s is None:
                            ins = ts(dst[:, k, :], xn[:, k, :], g[:, k:k + 1], None, ALU.mult)
                        else:
                            ins = ts(dst[:, k, :], xn[:, k, :], g[:, k:k + 1], s[:, k:k + 1], ALU.mult, ALU.add)
                N(ins, s_norm)

            def mods_from(n, chunks, src0, w, bias, rep):
                dve.wait_ge(used, chunks)
                o = psum[:, 0, src0:src0 + w].rearrange("p (a b) -> p a b", b=rep)
                m = mods[:, src0:src0 + w].rearrange("p (a b) -> p a b", b=rep)
                V(tt(m, o, bias.rearrange("p (a b) -> p a b", b=1).to_broadcast([P, w // rep, rep]), ALU.add), s_mod)

            def gain(dst, scale, g):
                V(stt(dst, scale, 1.0, g, ALU.add, ALU.mult))

            def G(i):
                return gsc[:, KT * i:KT * i + KT]

            def M(i):
                return mods[:, KT * i:KT * i + KT]

            def rope_pair(dst, src, src_ready, n=2):
                b = next_job(dve, "rot", "V")
                dve.wait_ge(*src_ready)
                V(tt(b3(tmp[:, 0], 2), b3(b, 2), bc(trig[:, 1, :], 2), ALU.mult), dve_took)
                V(tt(b3(tmp[:, 1], 2), src, bc(trig[:, 0, :], 2), ALU.mult))
                return tt(dst, b3(tmp[:, 0], 2), b3(tmp[:, 1], 2), ALU.add)

            def rope_dup(dst, names=("dup", "rotdup"), n=2):
                b = next_job(dve, names[0], "V")
                w = n * T
                V(tt(b3(tmp[:, 1, 0:w], n), b3(b[:, 0:w], n), bc(trig[:, 0, :], n), ALU.mult), dve_took)
                b = next_job(dve, names[1], "V")
                V(tt(b3(tmp[:, 0, 0:w], n), b3(b[:, 0:w], n), bc(trig[:, 1, :], n), ALU.mult), dve_took)
                return tt(dst, b3(tmp[:, 0, 0:w], n), b3(tmp[:, 1, 0:w], n), ALU.add)

            def residual(gate):
                for i in range(4):
                    b = next_job(dve, "mix", "V")
                    V(stt(hT[:, 2 * i, :], b[:, 0:T], gate[:, 2 * i:2 * i + 1], hT[:, 2 * i, :], ALU.mult, ALU.add))
                    V(stt(hT[:, 2 * i + 1, :], b[:, T:2 * T], gate[:, 2 * i + 1:2 * i + 2], hT[:, 2 * i + 1, :],
                          ALU.mult, ALU.add), dve_took)
                dve.sem_inc(s_hT, 1)

            def attention(kind, masks, gate=None):
                units, base = att_units(kind), att_base[kind]
                for s in range(len(units) + 1):
                    if s < len(units):
                        h, t, br, L = units[s]
                        b = next_job(dve, "S", "V")
                        V(stt(score[:, s % 3, 0:L], b[:, 0:L], SCALE, masks[br][:, t, 0:L], ALU.mult, ALU.add), dve_took)
                        V(dve.tensor_reduce(nmx[:, s % 4:s % 4 + 1], score[:, s % 3, 0:L], AX, ALU.max, negate=True), s_scored)
                    if s >= 1:
                        u = s - 1
                        h, t, br, L = units[u]
                        dve.wait_ge(s_exp, base + u + 1)
                        r = rinv[:, u % 4:u % 4 + 1]
                        V(dve.reciprocal(r, rsum[:, u % 4:u % 4 + 1]))
                        if gate is not None:
                            V(tt(r, r, gate[:, t, 3 * h + br:3 * h + br + 1], ALU.mult))
                        p = prob[:, u % 3, 0:L]
                        if kind == "nsa" and br == 0:
                            V(stt(p, p, r, pk("cmp01", NT)[:, t, :], ALU.mult, ALU.mult), s_prob)
                        else:
                            V(ts(p, p, r, None, ALU.mult), s_prob)

            def ffn_static(half, n):
                for h in range(n):
                    dve.wait_ge(s_sg, half + h + 1)
                    dve.wait_ge(s_u, half + h + 1)
                    if half + h >= 2:
                        dve.wait_ge(s_dn, half + h - 1)
                    N(tt(hid[:, h % 2], sg[:, h % 2], b3(psum[:, 2 + h % 2, :], 2), ALU.mult), s_hid)

            def ffn_gated(half, prod, n, row):
                for h in range(n):
                    dve.wait_ge(s_sg, half + h + 1)
                    dve.wait_ge(s_u, half + h + 1)
                    tt(b3(tmp[:, h % 2], 2), sg[:, h % 2], b3(psum[:, 2 + h % 2, :], 2), ALU.mult).then_inc(s_prod, 1)
                    dve.wait_ge(s_prod, prod + h + 1)
                    dve.wait_ge(s_dn, half + h - 1)
                    tt(hid[:, h % 2], b3(tmp[:, h % 2], 2), row.to_broadcast([P, 2, T]), ALU.mult).then_inc(s_hid, 1)

            def add_sums(total, gate):
                dve.wait_ge(s_dn, total)
                for j in range(KT):
                    ins = stt(hT[:, j, :], psum[:, 4 + j // 2, T * (j % 2):T * (j % 2) + T], gate[:, j:j + 1], hT[:, j, :],
                              ALU.mult, ALU.add)
                V(ins, s_y)
                dve.sem_inc(s_hT, 1)

            def first_max(oh, lg, shape, m, w):
                V(dve.tensor_reduce(m, lg, AX, ALU.max))
                V(tt(oh, lg, m.to_broadcast(shape), ALU.is_equal))
                V(tt(w, oh, pk("rank", 1)[:, :, 0:shape[-1]].to_broadcast(shape), ALU.mult))
                V(dve.tensor_reduce(cols3(40), w, AX, ALU.max))
                V(tt(oh, w, cols3(40).to_broadcast(shape), ALU.is_equal))

            def cols3(o):
                return cols[:, o:o + NT].rearrange("p (t a) -> p t a", a=1)

            def top2(lg, E, factor=None):
                shape = [P, NT, E]
                oh1, oh2, w, l2 = (small[:, a:a + 2, 0:E] for a in (1, 3, 7, 9))
                oh1 = small[:, 0:2, 16:16 + E]
                oh2 = small[:, 2:4, 16:16 + E]
                first_max(oh1, lg, shape, cols3(42), w)
                V(stt(l2, oh1, TAKEN, lg, ALU.mult, ALU.add))
                first_max(oh2, l2, shape, cols3(44), w)
                V(tt(small[:, 5:7, 0:1], cols3(44), cols3(42), ALU.subtract), s_top)
                dve.wait_ge(s_e, count[s_top])
                p1, p2 = cols3(46), cols3(48)
                V(ts(p1, small[:, 5:7, 0:1], 1.0, None, ALU.add))
                V(dve.reciprocal(p1, p1))
                if factor is not None:
                    V(tt(p1, p1, factor, ALU.mult))
                V(tt(p2, p1, small[:, 5:7, 0:1], ALU.mult))
                V(tt(oh1, oh1, p1.to_broadcast(shape), ALU.mult))
                V(tt(oh2, oh2, p2.to_broadcast(shape), ALU.mult))
                V(tt(small[:, 0:2, 0:E], oh1, oh2, ALU.add), s_lg)

            def windows(n, src, pe_cols):
                v = src.rearrange("p g (m r) -> p r g m", r=16)
                for half in range(2):
                    for hb in range(2):
                        p0 = HD * half
                        dst = xb[p0:p0 + HD, 8 * hb:8 * hb + 8, :, :]
                        ins = []
                        for j in range(8):
                            ins = ts(dst[:, j], v[p0:p0 + HD, 2 * j + half, :, hb:hb + NCMP],
                                     pe_cols[p0:p0 + HD, 8 * hb + j:8 * hb + j + 1], None, ALU.add)
                V(ins, s_xb)

            V(dve.memset(onesk[:], 1.0 / D))
            V(dve.memset(zeros[:], 0.0))
            V(dve.memset(epsc[:], EPS), consts)
            dve.wait_ge(s_pack, 16)
            dve.wait_ge(s_pos, 16)
            V(dve.tensor_copy(ang[:, 2, :], posi[:]))
            V(ts(ang[:, 2, :], ang[:, 2, :], pk("inv"), None, ALU.mult))
            two_pi = 2 * math.pi
            C1 = 6.28125
            C2 = float(np.float32(np.float32((two_pi - C1) * 2 ** 20).astype(np.int32).astype(np.float64) / 2 ** 20))
            C3 = two_pi - C1 - C2
            for i, (turn, lift) in enumerate(((0.25, math.pi / 2), (0.0, 0.0))):
                a, k = ang[:, i, :], ang[:, 3, :]
                V(ts(k, ang[:, 2, :], 1 / two_pi, turn, ALU.mult, ALU.add))
                V(ts(k, k, 12582912.0, 12582912.0, ALU.add, ALU.subtract))
                V(stt(a, k, -C1, ang[:, 2, :], ALU.mult, ALU.add))
                V(stt(a, k, -C2, a, ALU.mult, ALU.add))
                V(stt(a, k, -C3, a, ALU.mult, ALU.add))
                V(ts(a, a, lift, 3.1415925, ALU.add, ALU.min))
                V(ts(a, a, -3.1415925, None, ALU.max))
            dve.sem_inc(s_ang, 1)
            for t in range(NT):
                for g in range(2):
                    b = next_job(dve, "xT", "V")
                    V(dve.tensor_copy(hT[:, 4 * g:4 * g + 4, P * t:P * t + P], b3(b, 4)), dve_took)
            dve.sem_inc(s_hT, 1)
            mods_from(0, 12, 0, 48, pk("b_ada")[:, 0:48], 1)
            gain(G(0), M(1), pk("attn_gain")[:, 0:KT])
            gain(G(1), M(4), pk("ffn_gain")[:, 0:KT])
            norm(0, hT, [(uT, G(0), M(0))])
            dve.wait_ge(s_trig, 1)
            for i in range(4):
                V(rope_pair(qT[:, 2 * i:2 * i + 2, :], raw[:, i % 2], mark["raw"][i]), s_rope)
            V(rope_dup(kd[:, 0, 0:2, :]))
            V(rope_dup(kd[:, 0, 2:4, :]), s_rope)
            V(rope_pair(iqT[:, 0:2, :], raw[:, 1], mark["raw"][5]), s_rope)
            V(rope_pair(iqT[:, 2:4, :], raw[:, 0], mark["raw"][6]), s_rope)
            b = next_job(dve, "iw", "V")
            V(ts(iw[:], b[:, 0:16].rearrange("p (t n) -> p t n", t=2), IDX_H ** -0.5 * HD ** -0.5, None, ALU.mult), dve_took)
            V(rope_dup(b3(ikd, 1), ("dup0", "rotdup0"), 1), s_rope)
            causal = pk("causal", NT)
            for t in range(NT):
                L = P * (t + 1)
                for h in range(IDX_H):
                    i = IDX_H * t + h
                    dve.wait_ge(*mark["I"][i])
                    w = iw[:, t, h:h + 1]
                    if h == 0:
                        V(ts(acc8[:, 0:L], rel[:, i % 2, 0:L], w, None, ALU.mult), s_relused)
                    else:
                        V(stt(acc8[:, 0:L], rel[:, i % 2, 0:L], w, acc8[:, 0:L], ALU.mult, ALU.add), s_relused)
                V(tt(work[:, 0:L], acc8[:, 0:L], causal[:, t, 0:L], ALU.add))
                for _ in range(TOPK // 8):
                    V(dve.max(top8[:], work[:, 0:L]))
                    V(dve.match_replace(work[:, 0:L], top8[:], work[:, 0:L], TAKEN))
                V(ts(work[:, 0:L], work[:, 0:L], TAKEN, NEG, ALU.is_gt, ALU.mult))
                V(tt(selm[:, t, 0:L], work[:, 0:L], causal[:, t, 0:L], ALU.add))
            attention("dsa", [selm])
            residual(M(2))
            mods_from(1, 24, 48, 48, pk("b_ada")[:, 48:96], 1)
            mods_from(2, 28, 96, 16, pk("b_kv_ada"), 1)
            mods_from(3, 40, 112, 96, pk("b_ada_2"), 2)
            gain(G(2), M(13), pk("kv_gain"))
            gain(G(3), M(7), pk("attn_gain")[:, KT:2 * KT])
            gain(G(4), M(10), pk("ffn_gain")[:, KT:2 * KT])
            norm(1, hT, [(uT, G(1), M(3))])
            ffn_static(0, HALVES0)
            add_sums(HALVES0, M(5))
            norm(2, hT, [(uk, G(2), M(12)), (uT, G(3), M(6))])
            V(rope_dup(kd[:, 0, 0:2, :]))
            V(rope_dup(kd[:, 0, 2:4, :]), s_rope)
            for i in range(2):
                b = next_job(dve, "dup", "V")
                V(dve.tensor_copy(vcd[:, 512 * i:512 * i + 512], b), dve_took)
            dve.sem_inc(s_rope, 1)
            count[s_rope] += 1
            V(rope_dup(kd[:, 1, 0:2, :]))
            V(rope_dup(kd[:, 1, 2:4, :]), s_rope)
            V(rope_dup(kd[:, 2, 0:2, :]))
            V(rope_dup(kd[:, 2, 2:4, :]), s_rope)
            windows(0, kd[:, 0], pk("pe_k"))
            dve.wait_ge(*mark["w1"][0])
            windows(1, vcd.rearrange("p (g n) -> p g n", g=4), pk("pe_v"))
            b = next_job(dve, "kc", "V")
            V(dve.tensor_copy(kcT, b3(b[:, 0:60], 4)), dve_took)
            b = next_job(dve, "vc", "V")
            V(dve.tensor_copy(vc[0:NCMP], b3(b[0:NCMP, 0:256], 4)), dve_took)
            for i in range(4):
                V(rope_pair(qT[:, 2 * i:2 * i + 2, :], raw[:, i % 2], mark["raw"][12 + i]), s_rope)
            dve.wait_ge(*mark["gates"][0])
            attention("nsa", [pk("cmpneg", NT), causal, causal], gates)
            residual(M(8))
            norm(3, hT, [(uT, G(4), M(9))])
            b = next_job(dve, "router", "V")
            lg = small[:, 0:2, 32:32 + E1]
            V(dve.tensor_copy(lg, b[:, 0:2 * E1].rearrange("p (t n) -> p t n", t=2)), dve_took)
            top2(lg, E1)
            dve.wait_ge(*mark["gb"][E1 // 2 - 1])
            with dve.Fori(0, E1) as e:
                ffn_gated(HPE * e + HALVES0, HPE * e, HPE, gb[:, bass.ds(e, 1), :])
            add_sums(HALVES1, M(11))
            norm(4, hT, [(uT, pk("final_gain"), None)])
            def M2(i, which):
                return mods[:, 112:208].rearrange("p (a w) -> p a w", w=2)[:, KT * i:KT * i + KT, which]

            dve.wait_ge(s_norm, 5)
            dve.wait_ge(s_sc, 16)
            V(tt(hT[:], uT[:], sincos[:], ALU.add), s_hT)
            for t in range(NT):
                for g in range(2):
                    b = next_job(dve, "xT", "V")
                    V(dve.tensor_copy(ctxT[:, 4 * g:4 * g + 4, P * t:P * t + P], b3(b, 4)), dve_took)
            dve.sem_inc(s_ctxT, 1)
            gain(G(5), M2(1, 0), pk("g_pre_mix"))
            gain(G(6), M2(1, 1), pk("g_pre_mix"))
            V(tt(G(7), M2(2, 0), pk("g_post_mix"), ALU.mult))
            gain(G(8), M2(4, 0), pk("g_pre_ffn"))
            V(tt(G(9), M2(5, 0), pk("g_post_ffn"), ALU.mult))
            norm(5, hT, [(uT, G(5), M2(0, 0))])
            V(dve.memset(xm[:], 0.0), s_pad)
            norm(6, ctxT, [(ctxT, G(6), M2(0, 1))])
            wb = pk("wblk").rearrange("p (w j o) -> p w j o", w=3, j=4)
            dve.wait_ge(s_p2, 16)
            for i, bd in enumerate((bdq, bdk, bdv)):
                for j in range(MH):
                    ins = tt(bd[:, P * j:P * j + P].rearrange("p (m o) -> p m o", o=4),
                             pk2("blkmask").rearrange("p (m o) -> p m o", o=1).to_broadcast([P, 32, 4]),
                             wb[:, i, j:j + 1, :].to_broadcast([P, 32, 4]), ALU.mult)
            V(ins, s_blk)
            dve.wait_ge(*mark["uf"][1])
            cv = pk("conv_w", 3)
            for j in range(MH):
                o = act2[:, j, :].rearrange("p (s n) -> p s n", s=2)
                V(ts(o, xm[:, j, :, 1:1 + T], cv[:, 1, j:j + 1], pk("conv_b")[:, j:j + 1], ALU.mult, ALU.add))
                V(stt(o, xm[:, j, :, 0:T], cv[:, 0, j:j + 1], o, ALU.mult, ALU.add))
                V(stt(o, xm[:, j, :, 2:2 + T], cv[:, 2, j:j + 1], o, ALU.mult, ALU.add), s_conv)
            V(dve.memset(vtok[:, :, :, P:P + 1], 1.0))
            V(dve.memset(root[:], 1.0))
            R = slice(0, 8)
            b = next_job(dve, "gate8", "V")
            V(ts(igr[R], b3(b, 2)[R], pk("bif")[R, 0:1], None, ALU.add), dve_took)
            b = next_job(dve, "gate8", "V")
            V(ts(lfr[R], b3(b, 2)[R], pk("bif")[R, 1:2], None, ALU.add), dve_took)
            V(ts(t1r[R], lfr[R], -1.0, None, ALU.mult))
            V(tt(t1r[R], t1r[R], lfr[R], ALU.min), s_soft)
            dve.wait_ge(s_softd, 2)
            V(stt(lfr[R], lfr[R], 0.0, t1r[R], ALU.min, ALU.subtract))
            for s in range(2):
                V(dve.tensor_tensor_scan(prer[R, s, :], root[R, :], lfr[R, s, :], 0.0, ALU.mult, ALU.add))
            V(stt(t1r[R], prer[R], -2.0, lfr[R], ALU.mult, ALU.add))
            for s in range(2):
                V(ts(t1r[R, s, :], t1r[R, s, :], prer[R, s, T - 1:T], pk("bwd")[R], ALU.add, ALU.mult))
            V(tt(br_[R], t1r[R], prer[R], ALU.add))
            tot = prer[R, 1, T - 1:T]
            V(tt(t1r[R, 1, :], igr[R, 1, :], br_[R, 1, :], ALU.subtract))
            V(ts(t1r[R, 1, :], t1r[R, 1, :], tot, None, ALU.add))
            V(dve.tensor_reduce(cols[R, 60:61], t1r[R, 1, :], AX, ALU.max))
            V(tt(cols[R, 60:61], cols[R, 60:61], tot, ALU.max))
            V(ts(cols[R, 61:62], cols[R, 60:61], -1.0, None, ALU.mult), s_rows)
            V(tt(rstd[R, :], igr[R, 0, :], br_[R, 0, :], ALU.subtract), s_lat)
            b = next_job(dve, "gcols", "V")
            gc = small[:, 5:8, 16:32]
            V(dve.tensor_copy(gc[:, 0:2, :], b[:, 0:32].rearrange("p (a n) -> p a n", a=2)))
            V(dve.tensor_copy(gc[:, 2, 0:8], b[:, 32:40]), dve_took)
            wk, bcol, m0 = gc[:, 0, :], gc[:, 1, :].rearrange("p (t n) -> p t n", t=2), gc[:, 2, 0:8]
            for j in range(8):
                for t in range(NT):
                    b = next_job(dve, "r1", "V")
                    s0, s1 = srange(j, t)
                    ins = dve.tensor_reduce(cols[:, 64 + 8 * t + j:65 + 8 * t + j], b[:, 0:s1 - s0], AX, ALU.max)
                    N(ins, dve_took)
            for j in range(8):
                if j >= 2:
                    dve.wait_ge(*mark["c0"][j - 2])
                if j == 0:
                    dve.wait_ge(*mark["ktok"][1])
                for t in range(NT):
                    ins = ts(kw[:, j % 2, t, :], ktok[:, t, j % 4, :], wk[:, 8 * t + j:8 * t + j + 1], None, ALU.mult)
                N(ins, s_kw)
            dve.wait_ge(dve_took, count[dve_took])
            mx = cols[:, 64:80].rearrange("p (t n) -> p t n", t=2)
            ex = small[:, 0:4, 16:32].rearrange("p a (t n) -> p a t n", t=2)
            mt = small[:, 9, 16:32].rearrange("p (t n) -> p t n", t=2)
            mi = small[:, 8, 16:32].rearrange("p (t n) -> p t n", t=2)
            V(tt(mi, bcol, bc(m0, NT), ALU.add))
            V(tt(mt, bcol, mx, ALU.add))
            V(tt(mt, mt, mi, ALU.max))
            V(tt(small[:, 4, 16:32].rearrange("p (t n) -> p t n", t=2), bcol, mt, ALU.subtract))
            V(tt(ex[:, 0], mi, mt, ALU.subtract))
            V(ts(ex[:, 1], mt, -1.0, None, ALU.mult))
            V(dve.memset(small[:, 2:4, 16:32], 0.0), s_gcol)
            dve.wait_ge(s_gcold, 1)
            V(ts(ex[:, 0], ex[:, 0], M_SCALE, None, ALU.mult))
            units = mlstm_units()
            for s in range(len(units) + 3):
                if s < len(units):
                    j, t = units[s]
                    s0, s1 = srange(j, t)
                    b = next_job(dve, "qk", "V")
                    dve.wait_ge(*mark["r2"][s])
                    V(stt(prob[:, s % 3, 0:s1 - s0], b[:, 0:s1 - s0], M_SCALE, score[:, s % 3, 0:s1 - s0], ALU.mult, ALU.mult,
                          accum_out=cols[:, 80 + s % 4:81 + s % 4]), dve_took)
                    dve.sem_inc(s_sm, 1)
                if s >= 3:
                    u = s - 3
                    j, t = units[u]
                    b = next_job(dve, "num", "V")
                    c = 8 * t + j
                    V(ts(qc[:, u % 2, :], b[:, 256:385], small[:, 0, 16 + c:17 + c], None, ALU.mult))
                    nq, nn = cols[:, 84:85], cols[:, 85:86]
                    V(tt(nq, cols[:, 80 + u % 4:81 + u % 4], qc[:, u % 2, P:P + 1], ALU.add))
                    V(ts(nn, nq, -1.0, None, ALU.mult))
                    V(tt(nq, nq, nn, ALU.max))
                    V(tt(nq, nq, small[:, 1, 16 + c:17 + c], ALU.max))
                    V(dve.reciprocal(nq, nq))
                    V(tt(qc[:, u % 2, 0:P], b[:, 0:P], qc[:, u % 2, 0:P], ALU.add), dve_took)
                    o = hsum[:, t, j % 4, :]
                    if j < MH:
                        V(ts(o, qc[:, u % 2, 0:P], nq, None, ALU.mult))
                    else:
                        V(stt(o, qc[:, u % 2, 0:P], nq, o, ALU.mult, ALU.add))
            st = small[:, 10:12, :].rearrange("p a n -> p (a n)")
            mean = small[:, 4, 32:40]
            for i in range(8):
                t, h = i // 4, i % 4
                V(dve.bn_stats(st[:, 6 * i:6 * i + 6], hsum[:, t, h, :]))
                V(dve.bn_aggr(cols[:, 16 + 2 * i:18 + 2 * i], st[:, 6 * i:6 * i + 6]))
            mv = cols[:, 16:32].rearrange("p (i a) -> p i a", a=2)
            V(dve.tensor_copy(cols[:, 0:8], mv[:, :, 1]), s_var)
            dve.wait_ge(s_std, 1)
            V(dve.reciprocal(cols[:, 0:8], cols[:, 0:8]))
            for i in range(8):
                t, h = i // 4, i % 4
                ins = ts(hsum[:, t, h, :], hsum[:, t, h, :], mv[:, i, 0:1], cols[:, i:i + 1], ALU.subtract, ALU.mult)
            N(ins, s_hn)
            for hp in range(2):
                b = next_job(dve, "hT", "V")
                for i in range(2):
                    h = 2 * hp + i
                    V(ts(tmp[:, 0, 0:T], act2[:, h, 0:T], pk("skip")[:, h:h + 1], None, ALU.mult))
                    ins = stt(tmp[:, 1, 0:T], b[:, T * i:T * i + T], pk("norm_w")[:, h:h + 1], tmp[:, 0, 0:T], ALU.mult, ALU.add)
                    V(ins, dve_took if i else None)
                    V(tt(sq[:, h, :], tmp[:, 1, 0:T], zs[:, h, :], ALU.mult))
            dve.sem_inc(s_m, 1)

            def norm_residual(n, X, g):
                dve.wait_ge(*mark["ms"][n])
                V(dve.reciprocal(rstd[:], root[:]))
                V(tt(xn[:], X[:], bc(rstd[:], KT), ALU.mult))
                for k in range(KT):
                    ins = stt(hT[:, k, :], xn[:, k, :], g[:, k:k + 1], hT[:, k, :], ALU.mult, ALU.add)
                V(ins, s_norm)
                dve.sem_inc(s_hT, 1)
            norm_residual(7, yT, G(7))
            norm(8, hT, [(uT, G(8), M2(3, 0))])
            b = next_job(dve, "router", "V")
            lg20 = small[:, 11:12, 0:40].rearrange("p a (t n) -> p (a t) n", t=2)
            V(tt(lg20, b[:, 0:40].rearrange("p (t n) -> p t n", t=2), bc(pk("brouter2"), 2), ALU.add), dve_took)
            shape = [P, NT, EG]
            ohg = small[:, 9:11, 16:20]
            first_max(ohg, lg20[:, :, 0:4], shape, cols3(50), small[:, 7:9, 0:4])
            V(tt(small[:, 5:7, 0:4], lg20[:, :, 0:4], cols3(50).to_broadcast(shape), ALU.subtract), s_top)
            dve.wait_ge(s_e, 2)
            V(dve.tensor_reduce(cols3(52), small[:, 5:7, 0:4], AX, ALU.add))
            V(dve.reciprocal(cols3(52), cols3(52)))
            V(ts(ohg, ohg, -NEG, NEG, ALU.mult, ALU.add))
            lge = small[:, 0:2, 32:48]
            for t in range(NT):
                V(tt(lge[:, t].rearrange("p (g i) -> p g i", i=4), lg20[:, t, 4:20].rearrange("p (g i) -> p g i", i=4),
                     ohg[:, t].rearrange("p (g i) -> p g i", i=1).to_broadcast([P, 4, 4]), ALU.add))
            top2(lge, E2, cols3(52))
            dve.wait_ge(*mark["gb"][(E1 + E2) // 2 - 1])
            with dve.Fori(0, E2) as e:
                ffn_gated(2 * e + HALVES1, 2 * e + HPE * E1, 2, gb[:, bass.ds(e, 1), :])
            dve.wait_ge(s_dn, HALVES1 + 2 * E2)
            for i in range(4):
                ins = dve.tensor_copy(yT[:, 2 * i:2 * i + 2, :], b3(psum[:, 4 + i, :], 2))
            V(ins, s_y)
            norm_residual(9, yT, G(9))
            for t in range(NT):
                for g in range(2):
                    b = next_job(dve, "oT", "V")
                    V(dve.tensor_copy(uk_rows[:, t, 512 * g:512 * g + 512], b), dve_took)
            dve.sem_inc(s_fin, 1)

        @block.sync
        def _(sp):
            occupant = [None] * NSLOT

            def load(name, src=None, wait=True):
                slot, _, a, b = place[name]
                src = src if src is not None else SRC[name]
                if wait and occupant[slot] is not None:
                    sp.wait_ge(*freed[occupant[slot]])
                occupant[slot] = name
                sp.dma_start(ring[:, slot, 0:a * b].rearrange("p (a b) -> p a b", a=a), src).then_inc(land[slot], 16)

            SRC = dict(stream)
            names = [n for n, _ in stream]
            for n in names[:BEFORE_MOE1]:
                load(n)
            one = names[BEFORE_MOE1:BEFORE_MOE1 + 42]
            for n in one[:NSLOT]:
                load(n)

            def expert_src(n, e):
                kind, c = n.split(".")[1][0], int(n.split(".")[1][1:])
                if kind == "d":
                    w = A["moe_w_down"][0][bass.ds(e, 1), 512 * c:512 * c + 512, :]
                else:
                    w = A["moe_w_gate" if kind == "g" else "moe_w_up"][0][bass.ds(e, 1), :, 512 * c:512 * c + 512]
                return w.rearrange("e (k p) n -> p (e k) n", p=P)

            with sp.Fori(0, E1 // 2 - 1) as e:
                for i in range(42):
                    n = one[(i + NSLOT) % 42]
                    prev = one[i]
                    slot, _, a, b = place[n]
                    s, v = freed[prev]
                    sp.wait_ge(s, 2 * HPE * e + v)
                    src = expert_src(n, 2 * e + int(n[1]) + (0 if i + NSLOT < 42 else 2))
                    sp.dma_start(ring[:, slot, 0:a * b].rearrange("p (a b) -> p a b", a=a), src).then_inc(land[slot], 16)
            last = names[AFTER_MOE1 - 42:AFTER_MOE1]
            for n in last[:NSLOT]:
                occupant[place[n][0]] = n
            for n in last[NSLOT:] + names[AFTER_MOE1:BEFORE_MOE2]:
                load(n)
            pair = names[BEFORE_MOE2:BEFORE_MOE2 + 6]
            for n in pair:
                load(n)
            with sp.Fori(0, E2 // 2 - 1) as e:
                for n in pair:
                    slot, _, a, b = place[n]
                    s, v = freed[n]
                    sp.wait_ge(s, 4 * e + v)
                    w = A[{"g": "w_gate_2", "u": "w_up_2", "d": "w_down_2"}[n[3]]][0]
                    src = w[bass.ds(2 * e + 2 + int(n[1]), 1)].rearrange("e (k p) n -> p (e k) n", p=P)
                    sp.dma_start(ring[:, slot, 0:a * b].rearrange("p (a b) -> p a b", a=a), src).then_inc(land[slot], 16)
            sp.wait_ge(s_fin, 1)
            sp.dma_start(out[0].rearrange("(t p) n -> p t n", p=P), uk_rows).then_inc(s_out, 16)
            sp.wait_ge(s_out, 16)


def constants():
    C = {}
    C["ident"] = np.eye(P)
    rot = np.zeros((P, P))
    dup = np.zeros((2, P, P))
    rotdup = np.zeros((2, P, P))
    for m in range(P):
        i = m % HD
        src, sign = (i + 32, -1.0) if i < 32 else (i - 32, 1.0)
        rot[m - i + src, m] = sign
        for d in range(2):
            dup[d, HD * d + i, m] = 1.0
            rotdup[d, HD * d + src, m] = sign
    C["rot"], C["dup0"], C["dup1"], C["rotdup0"], C["rotdup1"] = rot, dup[0], dup[1], rotdup[0], rotdup[1]
    q = np.arange(T).reshape(NT, P).T[:, :, None]
    k = np.arange(T)[None, None, :]
    C["causal"] = np.where(k <= q, 0.0, NEG)
    C["anticausal"] = np.where(k >= q, 0.0, NEG)
    end = 16 * np.arange(NCMP)[None, None, :] + 31
    C["cmpneg"] = np.where(end <= q, 0.0, NEG)
    C["cmp01"] = np.where(end <= q, 1.0, 0.0)
    inv = (np.float32(1.0) / np.float32(10000.0) ** (np.arange(0, HD, 2, dtype=np.float32) / np.float32(HD)))
    C["inv"] = inv[np.arange(P) % 32][:, None]
    C["rank"] = np.tile(E2 - np.arange(E2), (P, 1))
    C["blkmask"] = np.arange(32)[None, :] == np.arange(P)[:, None] // 4
    C["bwd"] = (np.arange(P) >= MH).astype(np.float64)[:, None]
    a = 2 * np.pi * np.outer(np.arange(P), np.arange(P)) / P
    C["dftc"] = np.concatenate([np.cos(a), np.sin(a)], 1) / np.sqrt(P)
    b = 2 * np.pi * ((np.arange(T)[:, None] * np.arange(T)[None, :]) % T) / T
    C["dftt"] = (np.cos(b) / np.sqrt(T)).reshape(NT, P, T).transpose(1, 0, 2)
    C["dfts"] = (-np.sin(b) / np.sqrt(T)).reshape(NT, P, T).transpose(1, 0, 2)
    return C


def positions_2d():
    quarter = D // 4
    freq = (np.float32(1.0) / np.float32(10000.0) ** (np.arange(quarter, dtype=np.float32) / np.float32(quarter)))
    r = np.arange(T // 64, dtype=np.float32)[:, None] * freq
    cl = np.arange(64, dtype=np.float32)[:, None] * freq
    er = np.concatenate([np.sin(r), np.cos(r)], -1)
    ec = np.concatenate([np.sin(cl), np.cos(cl)], -1)
    emb = np.concatenate([np.repeat(er, 64, 0), np.tile(ec, (T // 64, 1))], -1)
    return emb.T.reshape(KT, P, T).transpose(1, 0, 2)


BIG = ["w_ada", "w_kv_ada", "w_ada_2", "a_w_in", "a_w_out", "ffn_w_gate", "ffn_w_up", "ffn_w_down", "w_kv",
       "cmp_w1_k", "cmp_w1_v", "b_w_q", "b_w_out", "moe_w_gate", "moe_w_up", "moe_w_down", "w_in_2", "w_out_2",
       "w_gate_2", "w_up_2", "w_down_2", "x", "positions", "ctx_2"]


def kernel(**inputs):
    import concourse.bacc as bacc
    from concourse.bass_utils import run_bass_kernel_spmd

    x = {k: np.asarray(v) for k, v in inputs.items()}

    def col(v):
        return v.reshape(-1, P).T

    def rows(w, k):
        return w.reshape(k, P, -1).transpose(1, 0, 2).reshape(P, -1)

    L = dict(constants())
    for n in ("attn_gain", "ffn_gain", "kv_gain", "final_gain", "b_ada", "b_kv_ada", "b_ada_2"):
        L[n] = col(x[n])
    for n in ("g_pre_mix", "g_post_mix", "g_pre_ffn", "g_post_ffn"):
        L[n] = col(x[n + "_2"])
    L["c"] = col(x["c"])
    L["c2"] = np.stack([col(x["c_2"]), col(x["c_ctx_2"])], -1)
    L["router"] = rows(x["moe_w_router"][0], KT)
    L["router2"] = rows(np.concatenate([x["w_router_group_2"][0], x["w_router_expert_2"][0]], 1), KT)
    L["brouter2"] = np.tile(np.concatenate([x["b_router_group_2"][0], x["b_router_expert_2"][0]]), (P, 1))
    L["pe_k"], L["pe_v"] = x["cmp_pe_k"].reshape(16, P).T, x["cmp_pe_v"].reshape(16, P).T
    L["w2k"] = rows(np.concatenate([x["cmp_w2_k"]] * 2, 1), 2)
    L["w2v"] = rows(x["cmp_w2_v"], 2)
    L["conv_w"] = x["conv_w_2"][0].reshape(3, MH, P).transpose(2, 0, 1)
    L["conv_b"], L["norm_w"], L["skip"] = col(x["conv_b_2"]), col(x["mlstm_norm_w_2"]), col(x["mlstm_skip_2"])
    L["wblk"] = np.stack([x[n][0].reshape(MH, 32, 4, 4).transpose(1, 2, 0, 3).reshape(P, 16)
                          for n in ("w_q_2", "w_k_2", "w_v_2")], 1)
    f, b = x["w_if_fwd_2"][0], x["w_if_bwd_2"][0]
    L["wif"] = np.stack([rows(np.concatenate([f[:, s], b[:, s]], 1), 12).reshape(P, 12, 8)
                         for s in (slice(0, 4), slice(4, 8))], 2)
    bf, bb = x["b_if_fwd_2"][0], x["b_if_bwd_2"][0]
    bif = np.zeros((P, 2), np.float32)
    for i, s in enumerate((slice(0, 4), slice(4, 8))):
        bif[0:8, i] = np.concatenate([bf[s], bb[s]])
    L["bif"] = bif
    L["wfour"] = x["w_fourier_2"][0].transpose(1, 0, 2)
    packed = np.concatenate([np.asarray(L[n], np.float32).reshape(P, w) for n, w in PACK], 1)

    nc = bacc.Bacc("TRN2", target_bir_lowering=False, num_devices=1)
    arrays = {n: np.ascontiguousarray(x[n]) for n in BIG}
    arrays["pack"] = np.ascontiguousarray(packed)
    arrays["pack2"] = np.ascontiguousarray(
        np.concatenate([np.asarray(L[n], np.float32).reshape(P, w) for n, w in PACK2], 1))
    arrays["sincos"] = np.ascontiguousarray(positions_2d().astype(np.float32))
    A = {n: nc.dram_tensor(f"in_{n}", a.shape, mybir.dt.from_np(a.dtype), kind="ExternalInput").ap()
         for n, a in arrays.items()}
    out = nc.dram_tensor("out", (1, T, D), F32, kind="ExternalOutput").ap()
    program(nc, A, out)
    r = run_bass_kernel_spmd(nc, [{f"in_{n}": a for n, a in arrays.items()}], core_ids=[0])
    return r.results[0]["out"]
```

```python
import math
from contextlib import ExitStack

import numpy as np

import concourse.bass as bass
from concourse import mybir

F32 = mybir.dt.float32
I32 = mybir.dt.int32
ACT = mybir.ActivationFunctionType
ALU = mybir.AluOpType
AX = mybir.AxisListType.X

P = 128
D = 1024
KT = D // P
T = 256
NT = T // P
HD = 64
NH = 16
NKV = 4
IDX_H = 8
TOPK = 64
NCMP = 15
D_FF = 2816
E1 = 8
F1 = 3584
E2 = 16
F2 = 512
EG = 4
MH = 4
DH = 128
DM = 512
EPS = 1e-6
NEG = -1e30
TAKEN = -3e38
SCALE = HD ** -0.5
NSLOT = 6
SLOT = 4096
RR = (1, 2, 3, 4, 5)
TABLE = 32
assert E2 + 2 * T // 96 < TABLE

PACK = [
    ("ident", 128), ("rot", 128), ("dup0", 128), ("dup1", 128), ("rotdup0", 128), ("rotdup1", 128),
    ("causal", NT * T), ("cmpneg", NT * NCMP), ("cmp01", NT * NCMP),
    ("inv", 1), ("rank", E2), ("bwd", 1),
    ("before", P), ("iota", 96), ("part", 1),
    ("attn_gain", 2 * KT), ("ffn_gain", 2 * KT), ("kv_gain", KT), ("final_gain", KT),
    ("g_pre_mix", KT), ("g_post_mix", KT), ("g_pre_ffn", KT), ("g_post_ffn", KT),
    ("b_ada", 96), ("b_kv_ada", 16), ("b_ada_2", 48), ("c", KT), ("c2", KT * 2),
    ("router", KT * E1), ("router2", KT * 20), ("brouter2", 20), ("pe_k", 16), ("pe_v", 16),
    ("w2k", 2 * P), ("w2v", 2 * HD), ("conv_w", 12), ("conv_b", 4), ("norm_w", 4), ("skip", 4),
    ("wblk", 3 * 4 * 4), ("wif", 12 * 2 * 8), ("bif", 2),
]
PACK2 = [("anticausal", NT * T), ("blkmask", 32), ("dftc", 2 * P), ("dftt", NT * T), ("dfts", NT * T), ("wfour", 4 * P)]


def offsets(pack):
    off, n = {}, 0
    for name, w in pack:
        off[name] = (n, w)
        n += w
    return off, n


OFF, NPACK = offsets(PACK)
OFF2, NPACK2 = offsets(PACK2)


def program(nc, A, out):
    with ExitStack() as ctx:
        def sb(name, shape, dt=F32):
            return ctx.enter_context(nc.sbuf_tensor(name, shape, dt))

        def sem(name):
            return ctx.enter_context(nc.semaphore(name))

        def b3v(ap):
            return ap.rearrange("p (s n) -> p s n", s=2)

        ring = sb("ring", [P, NSLOT, SLOT])
        pack = sb("pack", [P, NPACK])
        posi = sb("posi", [P, T], I32)
        onesk = sb("onesk", [P, P])
        epsc = sb("epsc", [P, 1])
        zeros = sb("zeros", [P, P])
        hT = sb("hT", [P, KT, T])
        uT = sb("uT", [P, KT, T])
        sq = sb("sq", [P, KT, T])
        xn = sq
        root = sb("root", [P, T])
        rstd = sb("rstd", [P, T])
        trig = sb("trig", [P, 2, T])
        cact = sb("cact", [P, 3 * KT])
        mods = sb("mods", [P, 96 + 16 + 96])
        gsc = sb("gsc", [P, 10 * KT])
        arena = sb("arena", [P, 11296 + NPACK2])
        tmp = sb("tmp", [P, 2, 512])
        cols = sb("cols", [P, 96])
        small = sb("small", [P, 12, 48])
        psum = ctx.enter_context(nc.psum_tensor("psum", [P, 8, 512], F32))

        def pk(name, *dims):
            o, w = OFF[name]
            ap = pack[:, o:o + w]
            if dims:
                ap = ap.rearrange(f"p (a b) -> p a b", a=dims[0])
            return ap

        def ar(o, n):
            return arena[:, o:o + n]

        def pk2(name, a=None):
            o, w = OFF2[name]
            ap = arena[:, 11296 + o:11296 + o + w]
            return ap.rearrange("p (a b) -> p a b", a=a) if a else ap

        raw = ar(0, 1024).rearrange("p (i a n) -> p i a n", i=2, a=2)
        qT = ar(1024, 2048).rearrange("p (a n) -> p a n", a=8)
        iqT = ar(3072, 1024).rearrange("p (a n) -> p a n", a=4)
        kd = ar(4096, 3072).rearrange("p (b a n) -> p b a n", b=3, a=4)
        uk = qT
        uk_rows = ar(1024, 2048).rearrange("p (t n) -> p t n", t=NT)
        ang = ar(3072, 1024).rearrange("p (a n) -> p a n", a=4)
        selm = ar(5120, 512).rearrange("p (t n) -> p t n", t=2)
        ikd, acc8 = ar(5632, 256), ar(5888, 256)
        rel = ar(6144, 512).rearrange("p (i n) -> p i n", i=2)
        work = ar(6656, 256)
        vt = ar(7168, 1024).rearrange("p (b t n) -> p b t n", b=2, t=2)
        oT = ar(8192, 2048).rearrange("p (a n) -> p a n", a=8)
        xb = ar(3072, 960).rearrange("p (b g n) -> p b g n", b=16, g=4)
        hid60 = ar(10240, 240).rearrange("p (v c n) -> p v c n", v=2, c=2)
        kcT = ar(10480, 60).rearrange("p (g n) -> p g n", g=4)
        vc = ar(10540, 256).rearrange("p (g n) -> p g n", g=4)
        vcd = ar(8192, 1024)
        slot7 = ar(3072, SLOT)
        grow, wrow = ar(7168, 512), ar(7680, 512)
        rows_by_slot = ar(9728, D)
        sg = ar(8192, 1024).rearrange("p (i a n) -> p i a n", i=2, a=2)
        hid = ar(9216, 1024).rearrange("p (i a n) -> p i a n", i=2, a=2)
        zs = ar(0, 1024).rearrange("p (a n) -> p a n", a=4)
        sincos = uk
        q2 = ar(1024, 2048).rearrange("p (a n) -> p a n", a=4)
        ab = ar(1024, 2048).rearrange("p (t g n) -> p t g n", t=2, g=4)
        yT = uk
        ktok = ar(3072, 1024).rearrange("p (t h n) -> p t h n", t=2, h=4)
        hsum = ktok
        ctxT = ar(4096, 2048).rearrange("p (a n) -> p a n", a=8)
        vtok = ar(4096, 4 * 4 * 129).rearrange("p (t h n) -> p t h n", t=4, h=4)
        k2 = ar(6160, 2048).rearrange("p (a n) -> p a n", a=4)
        xm = ar(8208, 4 * 2 * 258).rearrange("p (a s n) -> p a s n", a=4, s=2)
        state0 = ar(8208, 8 * 129).rearrange("p (j n) -> p j n", j=8)
        kw = ar(9240, 512).rearrange("p (i t n) -> p i t n", i=2, t=2)
        qc = ar(9752, 258).rearrange("p (i n) -> p i n", i=2)
        uf = ar(10272, 1024).rearrange("p (a n) -> p a n", a=4)
        pack2 = ar(11296, NPACK2)
        act2 = uT.rearrange("p a n -> p (a n)").rearrange("p (a n) -> p a n", a=4)
        v2 = sq.rearrange("p a n -> p (a n)").rearrange("p (a n) -> p a n", a=4)
        score = sb("score", [P, 3, T])
        prob = sb("prob", [P, 3, T])
        probT = sb("probT", [P, 2, 2, P])
        nmx = sb("nmx", [P, 4])
        rsum = sb("rsum", [P, 4])
        rinv = sb("rinv", [P, 4])
        gates = sb("gates", [P, NT, 48])
        iw = sb("iw", [P, NT, 8])
        bdv = probT.rearrange("p i j n -> p (i j n)")
        bdq, bdk = tmp[:, 0], tmp[:, 1]
        igr, lfr = score[:, 0:2], prob[:, 0:2]
        t1r = bdv.rearrange("p (s n) -> p s n", s=2)
        prer, br_ = b3v(tmp[:, 0]), b3v(tmp[:, 1])
        top8 = sb("top8", [P, 8])

        s_pack = sem("pack_in"); s_pos = sem("pos_in"); s_x = sem("x_in")
        s_sc = sem("sincos_in"); s_out = sem("out_stored")
        land = [sem(f"landed{i}") for i in range(NSLOT)]
        s_acc = sem("columns_weighted"); s_sums = sem("columns_summed")
        s_row = sem("modulation_row"); s_rowc = sem("modulation_row_taken")

        class Mix:

            def __init__(self, tag, E, F, N, U, nslot, tab):
                self.E, self.N, self.U, self.CH = E, N, U, F // 512
                self.tiles_max = -(-T // N)
                self.sel, self.gath = sem(f"{tag}_selection_ready"), sem(f"{tag}_gathered")
                self.xgA, self.xgV = sem(f"{tag}_inputs_low"), sem(f"{tag}_inputs_high")
                self.g, self.sg, self.u = sem(f"{tag}_gates_done"), sem(f"{tag}_silu_done"), sem(f"{tag}_ups_done")
                self.hid, self.dn = sem(f"{tag}_hidden_ready"), sem(f"{tag}_downs_done")
                self.s = sem(f"{tag}_scattered")
                self.yA, self.yV = sem(f"{tag}_rows_low"), sem(f"{tag}_rows_high")
                self.selg, self.v = sem(f"{tag}_scatter_ready"), sem(f"{tag}_vector_steps")
                self.slots = []
                self.land = [sem(f"{tag}_landed{i}") for i in range(nslot)]
                self.tab = tab
                flat = uT.rearrange("p a n -> p (a n)")
                self.xg = flat[:, 0:KT * N].rearrange("p (k n) -> p k n", k=KT)
                self.silu = ar(8192, 8 * N).rearrange("p (i n) -> p i n", i=2)
                self.hidden = ar(8960, 8 * N).rearrange("p (i n) -> p i n", i=2)
                self.pick = score[:, 0:NT, 0:N]
                self.selG = prob[:, 0, :]

            def buf(self, u, c):
                return (u + c) % 2

            def lag(self, c):
                return 2 if self.CH * self.U % 2 and c == 0 else 1

        mix = [Mix("m1", E1, F1, 96, 1, 7, posi[:, 0:64]), Mix("m2", E2, F2, 96, 1, 3, posi[:, 64:128])]
        by_token = sq.rearrange("p a n -> p (a n)").rearrange("p (t n) -> p t n", t=NT)
        res = sem("results")
        act_took = sem("act_took"); dve_took = sem("dve_took")
        vec = sem("vector_steps")
        consts = sem("consts_ready")
        s_cact = sem("c_activated")
        s_hT = sem("h_ready")
        s_ang = sem("angles_ready"); s_trig = sem("trig_ready")
        s_sq = sem("squares_ready"); s_norm = sem("normed"); s_part = sem("blocks_scaled")
        s_sqc = sem("context_squares"); s_normc = sem("context_normed")
        s_rope = sem("roped")
        s_relused = sem("relu_used")
        s_scored = sem("scored"); s_exp = sem("exponentials"); s_prob = sem("probs_normed")
        s_pv = sem("pv_done"); s_otook = sem("heads_taken")
        s_mod = sem("mods_ready")
        s_g = sem("gate_done"); s_u = sem("up_done"); s_sg = sem("silu_done")
        s_hid = sem("hidden_ready"); s_dn = sem("down_done"); s_y = sem("y_taken")
        s_xb = sem("windows_ready")
        s_top = sem("top_found"); s_e = sem("top_exponential"); s_lg = sem("gates_by_token")
        s_a = sem("choices_ready"); s_tab = sem("tables_ready")
        s_fin = sem("final_rows")
        s_ctxT = sem("context_ready"); s_pad = sem("pads_zero"); s_blk = sem("blocks_ready")
        s_conv = sem("convolved"); s_act2 = sem("conv_activated")
        s_soft = sem("log_sigmoid_in"); s_softd = sem("log_sigmoid_out"); s_rows = sem("gate_rows_in")
        s_decay = sem("context_decays"); s_lat = sem("latent_rows_ready"); s_kw = sem("keys_weighted")
        s_max = sem("row_maxima"); s_gcol = sem("gate_columns_in"); s_gcold = sem("gate_columns_out")
        s_pexp = sem("gate_exponentials"); s_sm = sem("gated_scores"); s_var = sem("variances")
        s_std = sem("deviations"); s_hn = sem("heads_normed"); s_m = sem("mlstm_ready"); s_p2 = sem("pack2_in")

        ones = onesk
        ident = pk("ident")
        stream, state = [], {"slot": 0}
        landed = [0] * NSLOT
        place, freed = {}, {}

        def add(name, src, a, b, rel=None, slot=None):
            if slot is None:
                slot = state["slot"]
                state["slot"] = (slot + 1) % NSLOT
            landed[slot] += 1
            place[name] = (slot, 16 * landed[slot], a, b)
            freed[name] = rel
            stream.append((name, src))

        def kcols(w, c0, c1):
            return w.rearrange("(k p) n -> p k n", p=P)[:, :, c0:c1]

        def add_cols(name, w, c0, c1, **kw):
            add(name, kcols(w, c0, c1), w.shape[0] // P, c1 - c0, **kw)

        for c in range(12):
            add_cols(f"ada0.{c}", A["w_ada"][0], 512 * c, 512 * c + 512)
        w_in = A["a_w_in"][0]
        for n, (c0, c1) in enumerate(((0, 512), (512, 1024), (1024, 1536), (1536, 2048), (2048, 2120))):
            add_cols(f"win.{n}", w_in, c0, c1)
        ada_rest = [("ada1", A["w_ada"][1], c) for c in range(12)] + [("kvada", A["w_kv_ada"], c) for c in range(4)]
        batches = [ada_rest[i:i + 3] for i in range(1, 16, 3)]
        add_cols("ada1.0", A["w_ada"][1], 0, 512)
        for n in range(2):
            add_cols(f"wout.{n}", A["a_w_out"][0], 512 * n, 512 * n + 512)

        def add_ffn(tag, wg, wu, wd, F, half, behind):
            for c in range(-(-F // 512)):
                f0, f1 = 512 * c, min(512 * c + 512, F)
                end = half + -(-f1 // 256)
                add_cols(f"{tag}.g{c}", wg, f0, f1, rel=(s_g, end))
                add_cols(f"{tag}.u{c}", wu, f0, f1, rel=(s_u, end))
                for n, w, k in (behind[c] if c < len(behind) else ()):
                    add_cols(f"{n}.{k}", w, 512 * k, 512 * k + 512)
                add(f"{tag}.d{c}", wd[f0:f1, :].rearrange("(k p) n -> p k n", p=P), (f1 - f0) // P, D,
                    rel=(s_dn, end))

        add_ffn("ffn", A["ffn_w_gate"][0], A["ffn_w_up"][0], A["ffn_w_down"][0], D_FF, 0, batches)
        HALVES0 = D_FF // 256
        for n in range(3):
            add_cols(f"wkv.{n}", A["w_kv"], 512 * n, 512 * n + 512)
        for n, w in (("w1k", "cmp_w1_k"), ("w1v", "cmp_w1_v")):
            add(n, A[w].rearrange("(k p) n -> p k n", p=P), 16, 256)
        for n, (c0, c1) in enumerate(((0, 512), (512, 1024), (1024, 1072))):
            add_cols(f"wq.{n}", A["b_w_q"][0], c0, c1)
        for c in range(12):
            add_cols(f"ada2.{c}", A["w_ada_2"][0], 512 * c, 512 * c + 512)
        for n in range(2):
            add_cols(f"bout.{n}", A["b_w_out"][0], 512 * n, 512 * n + 512)
        BEFORE_MOE1 = len(stream)
        SLOT1 = state["slot"]
        for j in range(7):
            mix[0].slots.append((SLOT1 + j) % NSLOT if j < 6 else NSLOT)
        AFTER_MOE1 = len(stream)
        add("ctx2", A["ctx_2"][0].rearrange("(t p) n -> p t n", p=P), NT, D)
        for n in range(3):
            add_cols(f"win2.{n}", A["w_in_2"][0], 512 * n, 512 * n + 512)
        for n in range(2):
            add_cols(f"out2.{n}", A["w_out_2"][0], 512 * n, 512 * n + 512)
        mix[1].slots = [(state["slot"] + i) % NSLOT for i in range(3)]

        def slot_view(slot, a, b):
            v = ring[:, slot, :] if slot < NSLOT else slot7
            return v[:, 0:a * b].rearrange("p (a b) -> p a b", a=a)

        def tile_chunk(m, u, c, r):
            M = mix[m]
            if m == 0:
                n = 3 * c + r
                return M.slots[n % 7], n % 7, 3, n // 7 + 1
            return M.slots[3 * u + r], 3 * u + r, 1, 1

        for n, nm in enumerate([f"ada0.{c}" for c in range(12)] + [f"{n}.{c}" for n, _, c in ada_rest]):
            freed[nm] = (s_acc, n + 1)

        jobs = []
        taken = {"A": 0, "V": 0}
        took_sem = {"A": act_took, "V": dve_took}
        seen = {"A": 0, "V": 0}
        mark = {}

        def open_job(pe, label, who):
            n = len(jobs)
            if n >= len(RR):
                _, w, k = jobs[n - len(RR)]
                pe.wait_ge(took_sem[w], k)
            taken[who] += 1
            jobs.append((label, who, taken[who]))
            mark.setdefault(label, []).append((took_sem[who], taken[who]))
            return psum[:, RR[n % len(RR)], :], mark[label][-1]

        def next_job(eng, label, who):
            n = [i for i, j in enumerate(jobs) if j[1] == who][seen[who]]
            assert jobs[n][0] == label, (jobs[n], label)
            seen[who] += 1
            eng.wait_ge(res, n + 1)
            return psum[:, RR[n % len(RR)], :]

        def b3(ap, a):
            return ap.rearrange("p (a n) -> p a n", a=a)

        def bc(ap, a):
            return ap.rearrange("p (a n) -> p a n", a=1).to_broadcast([ap.shape[0], a, ap.shape[1]])

        ATT = {"dsa": 32, "nsa": 96}
        att_base = {"dsa": 0, "nsa": 32}

        def att_units(kind):
            if kind == "dsa":
                return [(h, t, 0, P * (t + 1)) for h in range(NH) for t in range(NT)]
            return [(h, t, b, NCMP if b == 0 else P * (t + 1)) for h in range(NH) for t in range(NT) for b in range(3)]

        cw = ar(3072, 1024).rearrange("p (i g n) -> p i g n", i=2, g=4)
        abv = ar(1024, 2048).rearrange("p (t c g n) -> p t c g n", t=2, c=2, g=4)
        M_SCALE = DH ** -0.5

        def srange(j, t):
            return (0, P * (t + 1)) if j < MH else (P * t, T)

        def mlstm_units():
            return [(j, t) for j in range(8) for t in range(NT)]

        def M(i):
            return mods[:, KT * i:KT * i + KT]

        def M2(i, which):
            return mods[:, 112:208].rearrange("p (a w) -> p a w", w=2)[:, KT * i:KT * i + KT, which]

        ctx_sq = ar(6160, 2048).rearrange("p (k n) -> p k n", k=KT)
        root_c, rstd_c = trig[:, 0, :], trig[:, 1, :]

        def acc0(c):
            return ar(4096 + 512 * c, 512)

        def acc1(n):
            return ar(512 * n, 512)

        block = ctx.enter_context(nc.Block())

        @block.tensor
        def _(pe):
            def chunk(name):
                slot, val, a, b = place[name]
                pe.wait_ge(land[slot], val)
                return ring[:, slot, 0:a * b].rearrange("p (a b) -> p a b", a=a)

            def column_sums(n, acc, base):
                pe.wait_ge(s_acc, n)
                for j in range(4):
                    mm = pe.matmul(psum[:, 0, base + j:base + j + 1], acc[:, P * j:P * j + P], ones[:, 0:1],
                                   start=True, stop=True)
                mm.then_inc(s_sums, 1)

            def ada2_step(s):
                c, k = s // KT, s % KT
                if c < 12:
                    if k == 0:
                        ada2_step.w = chunk(f"ada2.{c}")
                        if c >= 2:
                            pe.wait_ge(s_rowc, c - 1)
                    r = HD * (c % 2)
                    mm = pe.matmul(psum[r:r + 2, 0, :], c2[:, k, :], ada2_step.w[:, k, :], start=(k == 0), stop=(k == KT - 1),
                                   skip_group_check=True)
                    if k == KT - 1:
                        mm.then_inc(s_row, 1)
                        freed[f"ada2.{c}"] = (s_row, c + 1)
                if s >= 10 and (s - 10) % KT == 0:
                    c = (s - 10) // KT
                    r = HD * (c % 2)
                    b, _ = open_job(pe, "acol", "V")
                    pe.wait_ge(s_rowc, c + 1)
                    for j in range(4):
                        mm = pe.transpose(b[:, 2 * j:2 * j + 2], tmp[r:r + 2, 0, P * j:P * j + P], ident[r:r + 2, r:r + 2])
                    mm.then_inc(res, 1)

            def norm():
                b, _ = open_job(pe, "ms", "A")
                norm.n += 1
                pe.wait_ge(s_sq, norm.n)
                for k in range(KT):
                    mm = pe.matmul(b[:, 0:T], ones[:], sq[:, k, :], start=(k == 0), stop=(k == KT - 1))
                mm.then_inc(res, 1)
            norm.n = 0

            def proj(label, who, wt, c0, nblk, X, rows=P, last=False, kt=KT):
                b, took = open_job(pe, label, who)
                for j in range(nblk):
                    for k in range(kt):
                        mm = pe.matmul(b[0:rows, T * j:T * j + T], wt[:, k, c0 + P * j:c0 + P * j + rows],
                                       X[:, k, :], start=(k == 0), stop=(k == kt - 1))
                mm.then_inc(res, 1)
                return took

            def tokproj(label, who, wt, c0, w, X):
                b, took = open_job(pe, label, who)
                for t in range(NT):
                    for k in range(KT):
                        mm = pe.matmul(b[:, w * t:w * t + w], X[:, k, P * t:P * t + P], wt[:, k, c0:c0 + w],
                                       start=(k == 0), stop=(k == KT - 1))
                mm.then_inc(res, 1)
                return took

            def frees(name):
                freed[name] = (res, len(jobs))

            def transposes_in(rows, signal, val):
                pe.wait_ge(signal, val)
                for t in range(NT):
                    for g in range(2):
                        b, _ = open_job(pe, "xT", "V")
                        for k in range(4):
                            mm = pe.transpose(b[:, P * k:P * k + P], rows[:, t, P * (4 * g + k):P * (4 * g + k) + P],
                                              ident)
                        mm.then_inc(res, 1)

            def rope_unit(kind, r):
                pe.wait_ge(*mark["raw"][r])
                src = raw[:, r % 2]
                if kind == "pair":
                    b, _ = open_job(pe, "rot", "V")
                    pe.matmul(b, pk("rot"), src, start=True, stop=True).then_inc(res, 1)
                elif kind in ("dup", "vdup"):
                    for j in range(2):
                        for m in (("dup", "rotdup") if kind == "dup" else ("dup",)):
                            b, _ = open_job(pe, m, "V")
                            for i in range(2):
                                mm = pe.matmul(b[:, T * i:T * i + T], pk(f"{m}{i}"), src[:, j, :], start=True, stop=True)
                            mm.then_inc(res, 1)
                else:
                    for m in ("dup0", "rotdup0"):
                        b, _ = open_job(pe, m, "V")
                        pe.matmul(b[:, 0:T], pk(m)[0:HD, :], src[0:HD, 0, :], start=True, stop=True).then_inc(res, 1)

            def attention(kind, ks, vs, extra=None):
                units = att_units(kind)
                base = att_base[kind]
                pt = {}
                for s in range(len(units) + 3):
                    if s < len(units):
                        h, t, br, L = units[s]
                        b, _ = open_job(pe, "S", "V")
                        r = (h % 2) * HD
                        pe.matmul(b[:, 0:L], qT[r:r + HD, h // 2, P * t:P * t + P], ks[br](r, h // 4, L),
                                  start=True, stop=True).then_inc(res, 1)
                    if extra:
                        extra(s)
                    if 2 <= s < len(units) + 2:
                        h, t, br, L = units[s - 2]
                        b, pt[s - 2] = open_job(pe, "T", "A")
                        pe.wait_ge(s_prob, base + s - 1)
                        for j in range(-(-L // P)):
                            w = min(P, L - P * j)
                            mm = pe.transpose(b[0:w, P * j:P * j + P], prob[:, (s - 2) % 3, P * j:P * j + w], ident)
                        mm.then_inc(res, 1)
                    if s >= 3:
                        u = s - 3
                        h, t, br, L = units[u]
                        pair = h // 2
                        first = (h % 2 == 0 and t == 0 and br == 0)
                        if first and pair >= 2:
                            pe.wait_ge(s_otook, base_pair(kind) + pair - 1)
                        pe.wait_ge(*pt.pop(u))
                        nbr = 1 if kind == "dsa" else 3
                        r = (h % 2) * HD
                        o = psum[r:r + HD, 6 + pair % 2, P * t:P * t + P]
                        nk = -(-L // P)
                        for j in range(nk):
                            w = min(P, L - P * j)
                            mm = pe.matmul(o, vs[br](w, j, h // 4), probT[0:w, u % 2, j, :],
                                           start=(br == 0 and j == 0), stop=(br == nbr - 1 and j == nk - 1))
                        mm.then_inc(s_pv, 1)

            def base_pair(kind):
                return 0 if kind == "dsa" else NH // 2

            def ffn(names, half, ntot, X):
                def down(h):
                    dchunk = names[h // 2][2]
                    pe.wait_ge(s_hid, half + h + 1)
                    if h % 2 == 0:
                        down.w = dchunk()
                    for f in range(2):
                        for j in range(KT):
                            st = h == 0 and f == 0
                            mm = pe.matmul(psum[:, 4 + j // 2, T * (j % 2):T * (j % 2) + T],
                                           down.w[:, 2 * (h % 2) + f, P * j:P * j + P], hid[:, h % 2, f, :],
                                           start=(st and j % 2 == 0),
                                           stop=(h == ntot - 1 and f == 1), skip_group_check=True)
                    mm.then_inc(s_dn, 1)

                for h in range(ntot):
                    if h % 2 == 0:
                        ffn.g = names[h // 2][0]()
                    if half + h >= 2:
                        pe.wait_ge(s_sg, half + h - 1)
                    for f in range(2):
                        for k in range(KT):
                            mm = pe.matmul(psum[:, h % 2, T * f:T * f + T], ffn.g[:, k, 256 * (h % 2) + P * f:256 * (h % 2) + P * f + P],
                                           X[:, k, :], start=(k == 0), stop=(k == KT - 1), skip_group_check=True)
                    mm.then_inc(s_g, 1)
                    if h % 2 == 0:
                        ffn.u = names[h // 2][1]()
                    if half + h >= 2:
                        pe.wait_ge(s_hid, half + h - 1)
                    for f in range(2):
                        for k in range(KT):
                            mm = pe.matmul(psum[:, 2 + h % 2, T * f:T * f + T], ffn.u[:, k, 256 * (h % 2) + P * f:256 * (h % 2) + P * f + P],
                                           X[:, k, :], start=(k == 0), stop=(k == KT - 1), skip_group_check=True)
                    mm.then_inc(s_u, 1)
                    if h >= 1:
                        down(h - 1)
                down(ntot - 1)

            def static_names(tag, n):
                return [[(lambda nm=f"{tag}.{x}{c}": chunk(nm)) for x in "gud"] for c in range(n)]

            def settle():
                pe.wait_ge(act_took, taken["A"])
                pe.wait_ge(dve_took, taken["V"])

            def zero_sums():
                for i in range(4):
                    pe.matmul(psum[:, 4 + i, :], zeros[:], pk("causal"), start=True, stop=False,
                              skip_group_check=True)

            def router(X, w, E):
                b, _ = open_job(pe, "router", "V")
                wr = pk(w, KT)
                for t in range(NT):
                    for k in range(KT):
                        mm = pe.matmul(b[:, E * t:E * t + E], X[:, k, P * t:P * t + P], wr[:, k, :],
                                       start=(k == 0), stop=(k == KT - 1))
                mm.then_inc(res, 1)

            def routing(m, X):
                M = mix[m]
                for t in range(NT):
                    for g in range(2):
                        b, _ = open_job(pe, "byt", "A")
                        for k in range(4):
                            mm = pe.transpose(b[:, P * k:P * k + P], X[:, 4 * g + k, P * t:P * t + P], ident)
                        mm.then_inc(res, 1)
                pe.wait_ge(s_a, m + 1)
                b, _ = open_job(pe, "rank", "V")
                a, E = small[:, 0:2, 0:M.E], M.E
                pe.matmul(b[:, 0:E], pk("before"), a[:, 0, :], start=True, stop=True)
                pe.matmul(b[:, E:2 * E], pk("before"), a[:, 1, :], start=True, stop=False)
                pe.matmul(b[:, E:2 * E], ones[:], a[:, 0, :], start=False, stop=True)
                pe.matmul(b[:, 2 * E:3 * E], ones[:], a[:, 0, :], start=True, stop=False)
                pe.matmul(b[:, 2 * E:3 * E], ones[:], a[:, 1, :], start=False, stop=True).then_inc(res, 1)
                pe.wait_ge(s_lg, m + 1)
                for o in (54, 46):
                    b, _ = open_job(pe, "gr", "A")
                    for q in range(4):
                        mm = pe.matmul(b[:, P * q:P * q + P], cols[:, o + q:o + q + 1].to_broadcast([P, P]), ident,
                                       start=True, stop=True)
                    mm.then_inc(res, 1)

            def mixture(m):
                M = mix[m]
                N, U, CH = M.N, M.U, M.CH

                def chunk_of(q, u, c, r):
                    slot, j, turns, k = tile_chunk(m, u, c, r)
                    pe.wait_ge(M.land[j], q * (16 * turns) + 16 * k)
                    return slot_view(slot, *((KT, 512) if r < 2 else (4, D)))

                def gather():
                    for k in range(KT):
                        for t in range(NT):
                            mm = pe.matmul(psum[:, k // 4, N * (k % 4):N * (k % 4) + N], by_token[:, t, P * k:P * k + P],
                                           M.pick[:, t, :], start=(t == 0), stop=(t == NT - 1), skip_group_check=True)
                    mm.then_inc(M.gath, 1)

                def scatter():
                    for k in range(KT):
                        mm = pe.matmul(psum[:, 4 + k // 2, T * (k % 2):T * (k % 2) + T], rows_by_slot[0:N, P * k:P * k + P],
                                       M.selG[0:N, :], start=False, stop=False, skip_group_check=True)
                    mm.then_inc(M.s, 1)

                def down(q, u, c):
                    w = chunk_of(q, u, c, 2)
                    pe.wait_ge(M.hid, q * (CH * U) + (CH * u + c + 3))
                    for f in range(4):
                        for half in range(2):
                            mm = pe.matmul(psum[0:N, 2 + half, :], M.hidden[:, M.buf(u, c), N * f:N * f + N],
                                           w[:, f, 512 * half:512 * half + 512], start=(c == 0 and f == 0),
                                           stop=(c == CH - 1 and f == 3), skip_group_check=True)
                    mm.then_inc(M.dn, 1)

                pe.sem_inc(M.dn, 2)
                pe.wait_ge(s_tab, m + 1)
                pe.wait_ge(M.sel, 1)
                pe.wait_ge(*mark["byt"][-1])
                gather()
                last = pe.value_load(M.tab[0:1, TABLE:TABLE + 1], min_val=0, max_val=TABLE - 2)
                with pe.Fori(0, last + 1) as q:
                    for u in range(U):
                        for c in range(CH):
                            n = CH * u + c
                            w = chunk_of(q, u, c, 0)
                            if c == 0:
                                pe.wait_ge(M.xgA, q * U + (u + 1))
                                pe.wait_ge(M.xgV, q * U + (u + 1))
                            else:
                                pe.wait_ge(M.sg, q * (CH * U) + n)
                            for f in range(4):
                                for k in range(KT):
                                    mm = pe.matmul(psum[:, 0, N * f:N * f + N], w[:, k, P * f:P * f + P], M.xg[:, k, :],
                                                   start=(k == 0), stop=(k == KT - 1), skip_group_check=True)
                            mm.then_inc(M.g, 1)
                            w = chunk_of(q, u, c, 1)
                            if c > 0:
                                pe.wait_ge(M.hid, q * (CH * U) + (n + 2))
                            for f in range(4):
                                for k in range(KT):
                                    mm = pe.matmul(psum[:, 1, N * f:N * f + N], w[:, k, P * f:P * f + P], M.xg[:, k, :],
                                                   start=(k == 0), stop=(k == KT - 1), skip_group_check=True)
                            mm.then_inc(M.u, 1)
                            if c == 0:
                                pe.wait_ge(M.yA, q * U + (u + 1))
                                pe.wait_ge(M.yV, q * U + (u + 1))
                                pe.wait_ge(M.selg, q * U + (u + 1))
                                scatter()
                            else:
                                down(q, u, c - 1)
                            if c == CH - 1:
                                pe.wait_ge(M.sel, q * U + (u + 2))
                                pe.wait_ge(M.hid, q * (CH * U) + (n + 3))
                                gather()
                                down(q, u, c)
                done = last * U + (U + 1)
                pe.wait_ge(M.yA, done)
                pe.wait_ge(M.yV, done)
                pe.wait_ge(M.selg, done)
                scatter()

            pe.wait_ge(s_pack, 16)
            pe.wait_ge(consts, 1)
            transposes_in(uk_rows, s_x, 16)
            pe.wait_ge(s_cact, 1)
            c2 = cact[:, KT:3 * KT].rearrange("p (k a) -> p k a", a=2)
            for c in range(12):
                column_sums(c + 1, acc0(c), 4 * c)
            norm()
            pe.wait_ge(s_norm, 1)
            w = chunk("win.0")
            proj("raw", "A", w, 0, 2, uT)
            proj("raw", "A", w, 256, 2, uT)
            frees("win.0")
            rope_unit("pair", 0)
            w = chunk("win.1")
            proj("raw", "A", w, 0, 2, uT)
            rope_unit("pair", 1)
            proj("raw", "A", w, 256, 2, uT)
            frees("win.1")
            rope_unit("pair", 2)
            w = chunk("win.2")
            proj("raw", "A", w, 0, 2, uT)
            rope_unit("pair", 3)
            tokproj("v", "A", w, 256, 256, uT)
            frees("win.2")
            rope_unit("dup", 4)
            w = chunk("win.3")
            proj("raw", "A", w, 0, 2, uT)
            rope_unit("pair", 5)
            proj("raw", "A", w, 256, 2, uT)
            frees("win.3")
            rope_unit("pair", 6)
            w = chunk("win.4")
            proj("raw", "A", w, 0, 1, uT, rows=HD)
            tokproj("iw", "V", w, 64, 8, uT)
            frees("win.4")
            rope_unit("one", 7)
            pe.wait_ge(s_rope, 8)
            for t in range(NT):
                L = P * (t + 1)
                for h in range(IDX_H):
                    b, _ = open_job(pe, "I", "A")
                    r = (h % 2) * HD
                    pe.matmul(b[:, 0:L], iqT[r:r + HD, h // 2, P * t:P * t + P], ikd[r:r + HD, 0:L],
                              start=True, stop=True).then_inc(res, 1)
            pe.wait_ge(*mark["v"][0])
            attention("dsa", [lambda r, g, L: kd[r:r + HD, 0, g, 0:L]],
                      [lambda w, j, g: vt[0:w, 0, j, HD * g:HD * g + HD]])
            pe.wait_ge(s_otook, 8)
            for n in range(2):
                w = chunk(f"wout.{n}")
                for i in range(2):
                    proj("mix", "V", w, 256 * i, 2, oT)
                frees(f"wout.{n}")
            norm()
            settle()
            pe.wait_ge(s_norm, 2)
            ffn(static_names("ffn", 6), 0, HALVES0, uT)
            pe.wait_ge(s_sg, HALVES0)
            for n in range(16):
                column_sums(13 + n, acc1(n), 48 + 4 * n)
            pe.wait_ge(s_y, 1)
            norm()
            pe.wait_ge(s_norm, 3)
            w = chunk("wkv.0")
            proj("raw", "A", w, 0, 2, uk)
            proj("raw", "A", w, 256, 2, uk)
            frees("wkv.0")
            rope_unit("dup", 8)
            w = chunk("wkv.1")
            proj("raw", "A", w, 0, 2, uk)
            rope_unit("vdup", 9)
            tokproj("v", "A", w, 256, 256, uk)
            frees("wkv.1")
            rope_unit("dup", 10)
            w = chunk("wkv.2")
            proj("raw", "A", w, 0, 2, uk)
            tokproj("v", "A", w, 256, 256, uk)
            frees("wkv.2")
            rope_unit("dup", 11)
            for n, nm in enumerate(("w1k", "w1v")):
                w = chunk(nm)
                b, _ = open_job(pe, "w1", "A")
                pe.wait_ge(s_xb, n + 1)
                for cb in range(2):
                    for j in range(16):
                        mm = pe.matmul(b[:, 60 * cb:60 * cb + 60], w[:, j, P * cb:P * cb + P], xb[:, j, :, :],
                                       start=(j == 0), stop=(j == 15))
                mm.then_inc(res, 1)
                frees(nm)
            w2k, w2v = pk("w2k", 2), pk("w2v", 2)
            pe.wait_ge(*mark["w1"][1])
            b, _ = open_job(pe, "kc", "V")
            for cb in range(2):
                mm = pe.matmul(b[:, 0:60], w2k[:, cb, :], hid60[:, 0, cb, :], start=(cb == 0), stop=(cb == 1))
            mm.then_inc(res, 1)
            b, _ = open_job(pe, "vc", "V")
            for g in range(NKV):
                for cb in range(2):
                    mm = pe.matmul(b[0:NCMP, HD * g:HD * g + HD], hid60[:, 1, cb, NCMP * g:NCMP * g + NCMP],
                                   w2v[:, cb, :], start=(cb == 0), stop=(cb == 1))
            mm.then_inc(res, 1)
            w = chunk("wq.0")
            proj("raw", "A", w, 0, 2, uT)
            proj("raw", "A", w, 256, 2, uT)
            frees("wq.0")
            rope_unit("pair", 12)
            w = chunk("wq.1")
            proj("raw", "A", w, 0, 2, uT)
            rope_unit("pair", 13)
            proj("raw", "A", w, 256, 2, uT)
            frees("wq.1")
            rope_unit("pair", 14)
            w = chunk("wq.2")
            tokproj("gates", "A", w, 0, 48, uT)
            frees("wq.2")
            rope_unit("pair", 15)
            pe.wait_ge(s_rope, 16)
            pe.wait_ge(*mark["vc"][0])
            pe.wait_ge(*mark["v"][2])
            attention("nsa",
                      [lambda r, g, L: kcT[r:r + HD, g, :], lambda r, g, L: kd[r:r + HD, 1, g, 0:L],
                       lambda r, g, L: kd[r:r + HD, 2, g, 0:L]],
                      [lambda w, j, g: vc[0:w, g, :], lambda w, j, g: vt[0:w, 0, j, HD * g:HD * g + HD],
                       lambda w, j, g: vt[0:w, 1, j, HD * g:HD * g + HD]], ada2_step)
            pe.wait_ge(s_otook, 16)
            for n in range(2):
                w = chunk(f"bout.{n}")
                for i in range(2):
                    proj("mix", "V", w, 256 * i, 2, oT)
                frees(f"bout.{n}")
            norm()
            pe.wait_ge(s_norm, 4)
            router(uT, "router", E1)
            routing(0, uT)
            settle()
            zero_sums()
            mixture(0)
            pe.wait_ge(s_y, 2)
            w = chunk("ctx2")
            for t in range(NT):
                for g in range(2):
                    b, _ = open_job(pe, "xT", "V")
                    for k in range(4):
                        mm = pe.transpose(b[:, P * k:P * k + P], w[:, t, P * (4 * g + k):P * (4 * g + k) + P], ident)
                    mm.then_inc(res, 1)
            frees("ctx2")
            norm()
            b, _ = open_job(pe, "msc", "A")
            pe.wait_ge(s_sqc, 1)
            for k in range(KT):
                mm = pe.matmul(b[:, 0:T], ones[:], ctx_sq[:, k, :], start=(k == 0), stop=(k == KT - 1))
            mm.then_inc(res, 1)
            norm()
            pe.wait_ge(s_normc, 1)
            pe.wait_ge(s_norm, 6)
            w = chunk("win2.0")
            for j in range(MH):
                b, _ = open_job(pe, "xm", "A")
                for sgm, X in enumerate((uT, ctxT)):
                    for k in range(KT):
                        mm = pe.matmul(b[:, T * sgm:T * sgm + T], w[:, k, P * j:P * j + P], X[:, k, :],
                                       start=(k == 0), stop=(k == KT - 1))
                mm.then_inc(res, 1)
            frees("win2.0")
            for n, label in ((1, "z"), (2, "uf")):
                w = chunk(f"win2.{n}")
                proj(label, "A", w, 0, 2, uT)
                proj(label, "A", w, 256, 2, uT)
                frees(f"win2.{n}")
            pe.wait_ge(s_p2, 16)
            dc = pk2("dftc")
            for i in range(2):
                b, _ = open_job(pe, "cw", "A")
                mm = pe.matmul(b, dc[:, P * i:P * i + P], pk2("wfour"), start=True, stop=True)
                mm.then_inc(res, 1)
            pe.wait_ge(*mark["uf"][1])
            pe.wait_ge(*mark["cw"][1])
            for t in range(NT):
                for i in range(2):
                    b, _ = open_job(pe, "ab", "A")
                    for g in range(4):
                        mm = pe.matmul(b[:, P * g:P * g + P], uf[:, g, P * t:P * t + P],
                                       cw[:, i, g, :], start=True, stop=True)
                    mm.then_inc(res, 1)
            pe.wait_ge(*mark["ab"][3])
            dt_ = (pk2("dftt", 2), pk2("dfts", 2))
            for gp in range(2):
                b, _ = open_job(pe, "fT", "A")
                for i in range(2):
                    g = 2 * gp + i
                    for c in range(2):
                        for t in range(NT):
                            mm = pe.matmul(b[:, T * i:T * i + T], abv[:, t, c, g, :], dt_[c][:, t, :],
                                           start=(c == 0 and t == 0), stop=(c == 1 and t == 1))
                mm.then_inc(res, 1)
            pe.wait_ge(s_blk, 1)
            pe.wait_ge(*mark["xm"][3])
            for label, bd, dst in (("v2", bdv, v2),):
                for j in range(MH):
                    b, _ = open_job(pe, label, "A")
                    for sgm in range(2):
                        mm = pe.matmul(b[:, T * sgm:T * sgm + T], bd[:, P * j:P * j + P], xm[:, j, sgm, 1:1 + T],
                                       start=True, stop=True)
                    mm.then_inc(res, 1)
            for tt_ in range(4):
                b, _ = open_job(pe, "vtok", "A")
                for j in range(MH):
                    o = 1 + P * (tt_ % 2)
                    mm = pe.matmul(b[:, P * j:P * j + P], xm[:, j, tt_ // 2, o:o + P], bdv[:, P * j:P * j + P],
                                   start=True, stop=True)
                mm.then_inc(res, 1)
            pe.wait_ge(s_act2, 4)
            for label, bd in (("q2", bdq), ("k2", bdk)):
                for j in range(MH):
                    b, _ = open_job(pe, label, "A")
                    pe.matmul(b, bd[:, P * j:P * j + P], act2[:, j, :], start=True, stop=True).then_inc(res, 1)
            for tt_ in range(2):
                b, _ = open_job(pe, "ktok", "A")
                for j in range(MH):
                    mm = pe.matmul(b[:, P * j:P * j + P], act2[:, j, T + P * tt_:T + P * tt_ + P], bdk[:, P * j:P * j + P],
                                   start=True, stop=True)
                mm.then_inc(res, 1)
            pe.wait_ge(*mark["k2"][3])
            wif = pk("wif").rearrange("p (b i n) -> p b i n", b=12, i=2)
            for i in range(2):
                b, _ = open_job(pe, "gate8", "V")
                for n, X in enumerate((q2, k2, v2)):
                    for j in range(MH):
                        mm = pe.matmul(b[0:8, :], wif[:, 4 * n + j, i, :], X[:, j, :], start=(n == 0 and j == 0),
                                       stop=(n == 2 and j == 3))
                mm.then_inc(res, 1)
            pe.wait_ge(s_decay, 1)
            pe.wait_ge(s_lat, 1)
            b, _ = open_job(pe, "gcols", "V")
            for t in range(NT):
                pe.transpose(b[:, 8 * t:8 * t + 8], t1r[0:8, 1, P * t:P * t + P], ident[0:8, 0:8])
                pe.transpose(b[:, 16 + 8 * t:24 + 8 * t], br_[0:8, 0, P * t:P * t + P], ident[0:8, 0:8])
            pe.matmul(b[:, 32:40], cols[0:8, 60:61].to_broadcast([8, P]), ident[0:8, 0:8], start=True,
                      stop=True).then_inc(res, 1)

            def gate_scores(b, j, t):
                s0, s1 = srange(j, t)
                m = pk("causal", NT) if j < MH else pk2("anticausal", NT)
                pe.matmul(b[:, 0:s1 - s0], ident[0:8, j:j + 1].to_broadcast([8, P]), rstd[0:8, s0:s1], start=True, stop=False)
                return pe.matmul(b[:, 0:s1 - s0], ident, m[:, t, s0:s1], start=False, stop=True)

            for j in range(8):
                for t in range(NT):
                    b, _ = open_job(pe, "r1", "V")
                    gate_scores(b, j, t).then_inc(res, 1)
            for j in range(8):
                b, _ = open_job(pe, "c0", "A")
                pe.wait_ge(s_kw, j + 1)
                for t in range(NT):
                    mm = pe.matmul(b[:, 0:129], kw[:, j % 2, t, :], vtok[:, 2 + t, j % 4, :], start=(t == 0), stop=(t == 1))
                mm.then_inc(res, 1)
            pe.wait_ge(*mark["c0"][7])
            units = mlstm_units()
            for s in range(len(units) + 3):
                if s < len(units):
                    j, t = units[s]
                    s0, s1 = srange(j, t)
                    b, _ = open_job(pe, "r2", "A")
                    gate_scores(b, j, t).then_inc(res, 1)
                    b, _ = open_job(pe, "qk", "V")
                    pe.matmul(b[:, 0:s1 - s0], q2[:, j % 4, P * t:P * t + P], k2[:, j % 4, s0:s1], start=True,
                              stop=True).then_inc(res, 1)
                if 2 <= s < len(units) + 2:
                    u = s - 2
                    j, t = units[u]
                    s0, s1 = srange(j, t)
                    b, _ = open_job(pe, "sT", "A")
                    pe.wait_ge(s_sm, u + 1)
                    for i in range((s1 - s0) // P):
                        mm = pe.transpose(b[:, P * i:P * i + P], prob[:, u % 3, P * i:P * i + P], ident)
                    mm.then_inc(res, 1)
                if s >= 3:
                    u = s - 3
                    j, t = units[u]
                    s0, s1 = srange(j, t)
                    b, _ = open_job(pe, "num", "V")
                    pe.wait_ge(*mark["sT"][u])
                    n = (s1 - s0) // P
                    for i in range(n):
                        pe.matmul(b[:, 0:P], probT[:, u % 2, i, :], vtok[:, s0 // P + i, j % 4, 0:P], start=(i == 0),
                                  stop=(i == n - 1))
                    pe.matmul(b[:, 256:385], q2[:, j % 4, P * t:P * t + P], state0[:, j, :], start=True,
                              stop=True).then_inc(res, 1)
            pe.wait_ge(s_hn, 1)
            for hp in range(2):
                b, _ = open_job(pe, "hT", "V")
                for i in range(2):
                    for t in range(NT):
                        mm = pe.transpose(b[:, T * i + P * t:T * i + P * t + P], hsum[:, t, 2 * hp + i, :], ident)
                mm.then_inc(res, 1)
            pe.wait_ge(s_m, 1)
            pe.wait_ge(*mark["fT"][1])
            for n in range(2):
                w = chunk(f"out2.{n}")
                for i in range(2):
                    b, _ = open_job(pe, "y", "A")
                    for jj in range(2):
                        for k in range(KT):
                            X = sq[:, k, :] if k < 4 else uf[:, k - 4, :]
                            mm = pe.matmul(b[:, T * jj:T * jj + T], w[:, k, 256 * i + P * jj:256 * i + P * jj + P], X,
                                           start=(k == 0), stop=(k == KT - 1))
                    mm.then_inc(res, 1)
                frees(f"out2.{n}")
            norm()
            norm()
            pe.wait_ge(s_norm, 8)
            router(uT, "router2", 20)
            routing(1, uT)
            settle()
            zero_sums()
            mixture(1)
            pe.wait_ge(s_y, 3)
            norm()
            pe.wait_ge(s_hT, 8)
            for t in range(NT):
                for g in range(2):
                    b, _ = open_job(pe, "oT", "V")
                    for k in range(4):
                        mm = pe.transpose(b[:, P * k:P * k + P], hT[:, 4 * g + k, P * t:P * t + P], ident)
                    mm.then_inc(res, 1)

        @block.scalar
        def _(act):
            def copy_job(label, dst, view):
                b = next_job(act, label, "A")
                act.activation(dst, view(b), ACT.Copy).then_inc(act_took, 1)

            def norm(X, ready):
                act.wait_ge(*ready)
                if norm.n:
                    act.wait_ge(s_norm, norm.n)
                norm.n += 1
                act.activation(sq[:], X[:], ACT.Square).then_inc(s_sq, 1)
                b = next_job(act, "ms", "A")
                act.activation(root[:], b[:, 0:T], ACT.Sqrt, bias=epsc[:, 0:1]).then_inc(act_took, 1)

            norm.n = 0

            def shift(dst, s, signal=None):
                for k in range(KT):
                    shift.n += 1
                    act.wait_ge(s_part, shift.n)
                    ins = act.activation(dst[:, k, :], dst[:, k, :], ACT.Identity, bias=s[:, k:k + 1])
                if signal is not None:
                    ins.then_inc(signal, 1)
            shift.n = 0

            def raws(r, rows=P, n=2):
                if r >= 2:
                    act.wait_ge(s_rope, r - 1)
                copy_job("raw", raw[0:rows, r % 2, 0:n, :], lambda b: b3(b, 2)[0:rows, 0:n, :])

            def attention(kind):
                units, base = att_units(kind), att_base[kind]
                nbr = 1 if kind == "dsa" else 3
                for s in range(len(units) + 3):
                    if s < len(units):
                        h, t, br, L = units[s]
                        act.wait_ge(s_scored, base + s + 1)
                        act.activation(prob[:, s % 3, 0:L], score[:, s % 3, 0:L], ACT.Exp, bias=nmx[:, s % 4:s % 4 + 1],
                                       accum_out=rsum[:, s % 4:s % 4 + 1]).then_inc(s_exp, 1)
                    if kind == "nsa" and s >= KT and s % KT == 0:
                        c = s // KT - 1
                        r = HD * (c % 2)
                        act.wait_ge(s_row, c + 1)
                        if c >= 2:
                            act.wait_ge(*mark["acol"][c - 2])
                        act.activation(tmp[r:r + 2, 0, :], psum[r:r + 2, 0, :], ACT.Copy).then_inc(s_rowc, 1)
                    if 2 <= s < len(units) + 2:
                        u = s - 2
                        h, t, br, L = units[u]
                        b = next_job(act, "T", "A")
                        if base + u >= 2:
                            act.wait_ge(s_pv, base + u - 1)
                        w = min(P, L)
                        n = -(-L // P)
                        act.activation(probT[0:w, u % 2, 0:n, :], b3(b, 4)[0:w, 0:n, :], ACT.Copy).then_inc(act_took, 1)
                    if s >= 3 and (s - 3) % (4 * nbr) == 4 * nbr - 1:
                        pair = (s - 3) // (4 * nbr)
                        act.wait_ge(s_pv, base + s - 2)
                        act.activation(oT[:, pair, :], psum[:, 6 + pair % 2, 0:T], ACT.Copy).then_inc(s_otook, 1)

            def silu(half, n):
                for h in range(n):
                    act.wait_ge(s_g, half + h + 1)
                    if half + h >= 2:
                        act.wait_ge(s_hid, half + h - 1)
                    act.activation(sg[:, h % 2], b3(psum[:, h % 2, :], 2), ACT.Silu).then_inc(s_sg, 1)

            def top(n):
                act.wait_ge(s_top, n)
                act.activation(small[:, 5:7, 0:1], small[:, 5:7, 0:1], ACT.Exp).then_inc(s_e, 1)

            def routing():
                for t in range(NT):
                    for g in range(2):
                        copy_job("byt", by_token[:, t, 512 * g:512 * g + 512], lambda b: b)
                for dst in (grow, wrow):
                    copy_job("gr", dst, lambda b: b)

            def mixture(m):
                M = mix[m]
                N, U, CH = M.N, M.U, M.CH

                def inputs():
                    act.activation(M.xg[:, 0:4, :], psum[:, 0, 0:4 * N].rearrange("p (k n) -> p k n", k=4),
                                   ACT.Copy).then_inc(M.xgA, 1)

                def by_slot():
                    act.activation(rows_by_slot[0:N, 0:512], psum[0:N, 2, :], ACT.Copy).then_inc(M.yA, 1)

                act.sem_inc(M.yA, 1)
                last = act.value_load(M.tab[0:1, TABLE:TABLE + 1], min_val=0, max_val=TABLE - 2)
                act.wait_ge(M.gath, 1)
                inputs()
                with act.Fori(0, last + 1) as q:
                    for u in range(U):
                        for c in range(CH):
                            n = CH * u + c
                            act.wait_ge(M.g, q * (CH * U) + (n + 1))
                            act.wait_ge(M.hid, q * (CH * U) + (n + M.lag(c)))
                            act.activation(M.silu[:, M.buf(u, c), :], psum[:, 0, 0:4 * N], ACT.Silu).then_inc(M.sg, 1)
                        act.wait_ge(M.gath, q * U + (u + 2))
                        inputs()
                        act.wait_ge(M.dn, q * (CH * U) + (CH * u + CH + 2))
                        by_slot()

            act.dma_start(pack[:], A["pack"][:, :]).then_inc(s_pack, 16)
            act.dma_start(uk_rows, A["x"][0].rearrange("(t p) n -> p t n", p=P)).then_inc(s_x, 16)
            act.dma_start(posi[:], A["positions"][0:1, :].to_broadcast([P, T])).then_inc(s_pos, 16)
            act.wait_ge(s_pack, 16)
            co = OFF["c"][0]
            act.activation(cact[:], pack[:, co:co + 3 * KT], ACT.Silu).then_inc(s_cact, 1)
            norm(hT, (s_hT, 1))
            shift(uT, M(0), s_norm)
            act.wait_ge(s_ang, 1)
            act.activation(trig[:], ang[:, 0:2, :], ACT.Sin).then_inc(s_trig, 1)
            for r in range(5):
                raws(r)
            copy_job("v", vt[:, 0], lambda b: b3(b, 2))
            raws(5)
            raws(6)
            raws(7, rows=HD, n=1)
            for t in range(NT):
                L = P * (t + 1)
                for h in range(IDX_H):
                    b = next_job(act, "I", "A")
                    i = IDX_H * t + h
                    if i >= 2:
                        act.wait_ge(s_relused, i - 1)
                    act.activation(rel[:, i % 2, 0:L], b[:, 0:L], ACT.Relu).then_inc(act_took, 1)
            attention("dsa")
            norm(hT, (s_hT, 2))
            shift(uT, M(3), s_norm)
            silu(0, HALVES0)
            norm(hT, (s_hT, 3))
            shift(uk, M(12))
            shift(uT, M(6), s_norm)
            raws(8)
            raws(9)
            raws(10)
            copy_job("v", vt[:, 0], lambda b: b3(b, 2))
            raws(11)
            copy_job("v", vt[:, 1], lambda b: b3(b, 2))
            for n in range(2):
                copy = next_job(act, "w1", "A")
                act.activation(hid60[:, n], copy[:, 0:120].rearrange("p (c n) -> p c n", c=2),
                               ACT.Gelu_apprx_tanh).then_inc(act_took, 1)
            for r in range(12, 16):
                raws(r)
            b = next_job(act, "gates", "A")
            act.activation(gates[:], b[:, 0:96].rearrange("p (t n) -> p t n", t=2), ACT.Sigmoid).then_inc(act_took, 1)
            attention("nsa")
            norm(hT, (s_hT, 4))
            shift(uT, M(9), s_norm)
            act.dma_start(sincos[:], A["sincos"][:, :, :]).then_inc(s_sc, 16)
            act.dma_start(pack2, A["pack2"][:, :]).then_inc(s_p2, 16)
            top(1)
            routing()
            act.wait_ge(s_tab, 1)
            mixture(0)
            norm(hT, (s_hT, 5))
            act.wait_ge(s_ctxT, 1)
            act.activation(ctx_sq, ctxT, ACT.Square).then_inc(s_sqc, 1)
            b = next_job(act, "msc", "A")
            act.activation(root_c, b[:, 0:T], ACT.Sqrt, bias=epsc[:, 0:1]).then_inc(act_took, 1)
            norm(hT, (s_hT, 6))
            shift(ctxT, M2(0, 1), s_normc)
            shift(uT, M2(0, 0), s_norm)
            act.wait_ge(s_pad, 1)
            for j in range(MH):
                copy_job("xm", xm[:, j, :, 1:1 + T], lambda b: b3(b, 2))
            for i in range(2):
                b = next_job(act, "z", "A")
                act.activation(zs[:, 2 * i:2 * i + 2, :], b3(b, 2), ACT.Silu).then_inc(act_took, 1)
            for i in range(2):
                copy_job("uf", uf[:, 2 * i:2 * i + 2, :], lambda b: b3(b, 2))
            for i in range(2):
                copy_job("cw", cw[:, i], lambda b: b3(b, 4))
            for t in range(NT):
                for i in range(2):
                    copy_job("ab", abv[:, t, i], lambda b: b3(b, 4))
            for i in range(2):
                copy_job("fT", uf[:, 2 * i:2 * i + 2, :], lambda b: b3(b, 2))
            for j in range(MH):
                copy_job("v2", v2[:, j, :], lambda b: b)
            for i in range(4):
                copy_job("vtok", vtok[:, i, :, 0:P], lambda b: b3(b, 4))
            for j in range(MH):
                act.wait_ge(s_conv, j + 1)
                act.activation(act2[:, j, :], act2[:, j, :], ACT.Silu).then_inc(s_act2, 1)
            for dst, label in ((q2, "q2"), (k2, "k2")):
                for j in range(MH):
                    copy_job(label, dst[:, j, :], lambda b: b)
            for i in range(2):
                copy_job("ktok", ktok[:, i], lambda b: b3(b, 4))
            act.wait_ge(s_soft, 1)
            act.activation(t1r[0:8], t1r[0:8], ACT.Exp).then_inc(s_softd, 1)
            act.wait_ge(s_softd, 1)
            act.activation(t1r[0:8], t1r[0:8], ACT.Ln, bias=1.0).then_inc(s_softd, 1)
            act.wait_ge(s_rows, 1)
            act.activation(t1r[0:8, 1, :], t1r[0:8, 1, :], ACT.Exp, bias=cols[0:8, 61:62]).then_inc(s_decay, 1)
            for j in range(8):
                copy_job("c0", state0[:, j, :], lambda b: b[:, 0:129])
            act.wait_ge(s_gcol, 1)
            act.activation(small[:, 0:4, 16:32].rearrange("p a n -> p a n"), small[:, 0:4, 16:32], ACT.Exp).then_inc(s_gcold, 1)
            units = mlstm_units()
            for s in range(len(units) + 2):
                if s < len(units):
                    j, t = units[s]
                    s0, s1 = srange(j, t)
                    b = next_job(act, "r2", "A")
                    if s >= 3:
                        act.wait_ge(s_sm, s - 2)
                    act.activation(score[:, s % 3, 0:s1 - s0], b[:, 0:s1 - s0], ACT.Exp,
                                   bias=small[:, 4, 16 + 8 * t + j:17 + 8 * t + j]).then_inc(act_took, 1)
                if s >= 2:
                    u = s - 2
                    j, t = units[u]
                    s0, s1 = srange(j, t)
                    n = (s1 - s0) // P
                    if u >= 2:
                        act.wait_ge(*mark["num"][u - 2])
                    b = next_job(act, "sT", "A")
                    act.activation(probT[:, u % 2, 0:n, :], b3(b, 4)[:, 0:n, :], ACT.Copy).then_inc(act_took, 1)
            act.wait_ge(s_var, 1)
            act.activation(cols[:, 0:8], cols[:, 0:8], ACT.Sqrt, bias=epsc[:, 0:1]).then_inc(s_std, 1)
            for i in range(4):
                copy_job("y", yT[:, 2 * i:2 * i + 2, :], lambda b: b3(b, 2))
            norm(yT, mark["y"][3])
            norm(hT, (s_hT, 7))
            shift(uT, M2(3, 0), s_norm)
            act.wait_ge(s_top, 2)
            act.activation(small[:, 5:7, 0:4], small[:, 5:7, 0:4], ACT.Exp).then_inc(s_e, 1)
            act.wait_ge(s_top, 3)
            act.activation(small[:, 5:7, 0:1], small[:, 5:7, 0:1], ACT.Exp).then_inc(s_e, 1)
            routing()
            act.wait_ge(s_tab, 2)
            mixture(1)
            norm(yT, (s_y, 3))

        @block.vector
        def _(dve):
            count = {}

            def V(ins, s=None):
                s = s or vec
                count[s] = count.get(s, 0) + 1
                ins.then_inc(s, 1)
                dve.wait_ge(s, count[s])

            def N(ins, s):
                count[s] = count.get(s, 0) + 1
                ins.then_inc(s, 1)

            tt, ts, stt = dve.tensor_tensor, dve.tensor_scalar, dve.scalar_tensor_tensor

            def scaled(dst, X, g, r):
                for k in range(KT):
                    stt(dst[:, k, :], X[:, k, :], g[:, k:k + 1], r, ALU.mult, ALU.mult).then_inc(s_part, 1)

            def norm(n, X, outs):
                dve.wait_ge(*mark["ms"][n])
                V(dve.reciprocal(rstd[:], root[:]))
                for dst, g in outs:
                    scaled(dst, X, g, rstd[:])
                count[s_norm] = count.get(s_norm, 0) + 1

            def mods_from(n, chunks, src0, w, bias, rep):
                dve.wait_ge(s_sums, chunks)
                o = psum[:, 0, src0:src0 + w].rearrange("p (a b) -> p a b", b=rep)
                m = mods[:, src0:src0 + w].rearrange("p (a b) -> p a b", b=rep)
                V(stt(m, o, float(D), bias.rearrange("p (a b) -> p a b", b=1).to_broadcast([P, w // rep, rep]), ALU.mult, ALU.add), s_mod)

            def weigh(name, acc):
                slot, val, a, b = place[name]
                dve.wait_ge(land[slot], val)
                w = slot_view(slot, a, b)
                V(ts(acc, w[:, 0, :], cact[:, 0:1], None, ALU.mult))
                for k in range(1, KT):
                    V(stt(acc, w[:, k, :], cact[:, k:k + 1], acc, ALU.mult, ALU.add), s_acc if k == KT - 1 else None)

            def gain(dst, scale, g):
                V(stt(dst, scale, 1.0, g, ALU.add, ALU.mult))

            def G(i):
                return gsc[:, KT * i:KT * i + KT]

            def rope_pair(dst, src, src_ready, n=2):
                b = next_job(dve, "rot", "V")
                dve.wait_ge(*src_ready)
                V(tt(b3(tmp[:, 0], 2), b3(b, 2), bc(trig[:, 1, :], 2), ALU.mult), dve_took)
                V(tt(b3(tmp[:, 1], 2), src, bc(trig[:, 0, :], 2), ALU.mult))
                return tt(dst, b3(tmp[:, 0], 2), b3(tmp[:, 1], 2), ALU.add)

            def rope_dup(dst, names=("dup", "rotdup"), n=2):
                b = next_job(dve, names[0], "V")
                w = n * T
                V(tt(b3(tmp[:, 1, 0:w], n), b3(b[:, 0:w], n), bc(trig[:, 0, :], n), ALU.mult), dve_took)
                b = next_job(dve, names[1], "V")
                V(tt(b3(tmp[:, 0, 0:w], n), b3(b[:, 0:w], n), bc(trig[:, 1, :], n), ALU.mult), dve_took)
                return tt(dst, b3(tmp[:, 0, 0:w], n), b3(tmp[:, 1, 0:w], n), ALU.add)

            def residual(gate):
                for i in range(4):
                    b = next_job(dve, "mix", "V")
                    V(stt(hT[:, 2 * i, :], b[:, 0:T], gate[:, 2 * i:2 * i + 1], hT[:, 2 * i, :], ALU.mult, ALU.add))
                    V(stt(hT[:, 2 * i + 1, :], b[:, T:2 * T], gate[:, 2 * i + 1:2 * i + 2], hT[:, 2 * i + 1, :],
                          ALU.mult, ALU.add), dve_took)
                dve.sem_inc(s_hT, 1)

            def ada2_columns(c):
                b = next_job(dve, "acol", "V")
                m = mods[:, 112 + 8 * c:120 + 8 * c].rearrange("p (a b) -> p a b", b=2)
                bias = pk("b_ada_2")[:, 4 * c:4 * c + 4].rearrange("p (a b) -> p a b", b=1).to_broadcast([P, 4, 2])
                V(tt(m, b[:, 0:8].rearrange("p (a b) -> p a b", b=2), bias, ALU.add), dve_took)

            def attention(kind, masks, gate=None):
                units, base = att_units(kind), att_base[kind]
                for s in range(len(units) + 1):
                    if s < len(units):
                        h, t, br, L = units[s]
                        b = next_job(dve, "S", "V")
                        V(stt(score[:, s % 3, 0:L], b[:, 0:L], SCALE, masks[br][:, t, 0:L], ALU.mult, ALU.add), dve_took)
                        V(dve.tensor_reduce(nmx[:, s % 4:s % 4 + 1], score[:, s % 3, 0:L], AX, ALU.max, negate=True), s_scored)
                    if kind == "nsa" and s >= 10 and (s - 10) % KT == 0:
                        ada2_columns((s - 10) // KT)
                    if s >= 1:
                        u = s - 1
                        h, t, br, L = units[u]
                        dve.wait_ge(s_exp, base + u + 1)
                        r = rinv[:, u % 4:u % 4 + 1]
                        V(dve.reciprocal(r, rsum[:, u % 4:u % 4 + 1]))
                        if gate is not None:
                            V(tt(r, r, gate[:, t, 3 * h + br:3 * h + br + 1], ALU.mult))
                        p = prob[:, u % 3, 0:L]
                        if kind == "nsa" and br == 0:
                            V(stt(p, p, r, pk("cmp01", NT)[:, t, :], ALU.mult, ALU.mult), s_prob)
                        else:
                            V(ts(p, p, r, None, ALU.mult), s_prob)

            def ffn_static(half, n):
                for h in range(n):
                    dve.wait_ge(s_sg, half + h + 1)
                    dve.wait_ge(s_u, half + h + 1)
                    if half + h >= 2:
                        dve.wait_ge(s_dn, half + h - 1)
                    N(tt(hid[:, h % 2], sg[:, h % 2], b3(psum[:, 2 + h % 2, :], 2), ALU.mult), s_hid)
                    if h % 2 == 0 and h // 2 < len(batches):
                        for name, _, c in batches[h // 2]:
                            weigh(f"{name}.{c}", acc1(ffn_static.n))
                            ffn_static.n += 1

            ffn_static.n = 1

            def mixture(m):
                M = mix[m]
                N, U, CH = M.N, M.U, M.CH
                iota = pk("iota")[:, 0:N]
                g1, g2 = 54, 56
                slot_no = cols[:, 58:59]
                STEPS = 4

                def selection(step):
                    for t in range(NT):
                        ins = ts(M.pick[:, t, :], iota, cols[:, g1 + t:g1 + t + 1], None, ALU.is_equal)
                    step(ins)
                    for t in range(NT):
                        ins = stt(M.pick[:, t, :], iota, cols[:, g2 + t:g2 + t + 1], M.pick[:, t, :], ALU.is_equal, ALU.add)
                    ins.then_inc(M.sel, 1)

                def inputs():
                    dve.tensor_copy(M.xg[:, 4:8, :], psum[:, 1, 0:4 * N].rearrange("p (k n) -> p k n", k=4)).then_inc(M.xgV, 1)

                def by_slot():
                    dve.tensor_copy(rows_by_slot[0:N, 512:1024], psum[0:N, 3, :]).then_inc(M.yV, 1)

                V(dve.tensor_copy(slot_no, pk("part")))
                selection(V)
                V(dve.memset(M.selG[0:N, :], 0.0))
                V(dve.memset(rows_by_slot[0:N, :], 0.0))
                dve.sem_inc(M.selg, 1)
                dve.sem_inc(M.yV, 1)
                dve.sem_inc(M.hid, 2)
                last = dve.value_load(M.tab[0:1, TABLE:TABLE + 1], min_val=0, max_val=TABLE - 2)
                dve.wait_ge(M.gath, 1)
                inputs()
                with dve.Fori(0, last + 1) as q:
                    for u in range(U):
                        k = [0]

                        def step(ins):
                            k[0] += 1
                            ins.then_inc(M.v, 1)
                            dve.wait_ge(M.v, q * (STEPS * U) + (STEPS * u + k[0]))
                        dve.wait_ge(M.sel, q * U + (u + 1))
                        dve.wait_ge(M.gath, q * U + (u + 1))
                        step(ts(cols[:, g1:g1 + 4], cols[:, g1:g1 + 4], -float(N), None, ALU.add))
                        selection(step)
                        for c in range(CH):
                            n = CH * u + c
                            dve.wait_ge(M.sg, q * (CH * U) + (n + 1))
                            dve.wait_ge(M.u, q * (CH * U) + (n + 1))
                            dve.wait_ge(M.dn, q * (CH * U) + (n + M.lag(c)))
                            tt(M.hidden[:, M.buf(u, c), :], M.silu[:, M.buf(u, c), :], psum[:, 1, 0:4 * N],
                               ALU.mult).then_inc(M.hid, 1)
                            if c == 0:
                                dve.wait_ge(M.s, q * U + (u + 1))
                                step(stt(tmp[0:N, 0, :], grow[0:N], slot_no[0:N], wrow[0:N], ALU.is_equal, ALU.mult))
                                tt(M.selG[0:N, :], tmp[0:N, 0, 0:T], tmp[0:N, 0, T:2 * T], ALU.add).then_inc(M.selg, 1)
                                step(ts(slot_no, slot_no, float(N), None, ALU.add))
                        assert k[0] == STEPS
                        dve.wait_ge(M.gath, q * U + (u + 2))
                        inputs()
                        dve.wait_ge(M.dn, q * (CH * U) + (CH * u + CH + 2))
                        by_slot()
                dve.wait_ge(M.s, last * U + (U + 1))

            def add_sums(gate):
                for j in range(KT):
                    ins = stt(hT[:, j, :], psum[:, 4 + j // 2, T * (j % 2):T * (j % 2) + T], gate[:, j:j + 1], hT[:, j, :],
                              ALU.mult, ALU.add)
                V(ins, s_y)
                dve.sem_inc(s_hT, 1)

            def first_max(oh, lg, shape, m, w):
                V(dve.tensor_reduce(m, lg, AX, ALU.max))
                V(tt(oh, lg, m.to_broadcast(shape), ALU.is_equal))
                V(tt(w, oh, pk("rank", 1)[:, :, 0:shape[-1]].to_broadcast(shape), ALU.mult))
                V(dve.tensor_reduce(cols3(40), w, AX, ALU.max))
                V(tt(oh, w, cols3(40).to_broadcast(shape), ALU.is_equal))

            def cols3(o):
                return cols[:, o:o + NT].rearrange("p (t a) -> p t a", a=1)

            def top2(m, lg, factor=None):
                M = mix[m]
                E, N = M.E, M.N
                shape = [P, NT, E]
                a, w, l2 = (small[:, o:o + 2, 0:E] for o in (0, 7, 9))
                oh1 = small[:, 0:2, 16:16 + E]
                oh2 = small[:, 2:4, 16:16 + E]
                first_max(oh1, lg, shape, cols3(42), w)
                V(stt(l2, oh1, TAKEN, lg, ALU.mult, ALU.add))
                first_max(oh2, l2, shape, cols3(44), w)
                V(tt(small[:, 5:7, 0:1], cols3(44), cols3(42), ALU.subtract), s_top)
                V(tt(a, oh1, oh2, ALU.add), s_a)
                dve.wait_ge(s_e, count[s_top])
                p1, p2 = cols3(46), cols3(48)
                V(ts(p1, small[:, 5:7, 0:1], 1.0, None, ALU.add))
                V(dve.reciprocal(p1, p1))
                if factor is not None:
                    V(tt(p1, p1, factor, ALU.mult))
                V(tt(p2, p1, small[:, 5:7, 0:1], ALU.mult))
                b = next_job(dve, "rank", "V")
                rkc = small[:, 7:10, 16:16 + E]
                V(ts(rkc, b[:, 0:3 * E].rearrange("p (a n) -> p a n", a=3), float(D), None, ALU.mult), dve_took)
                cnt, tiles, incl, base = rkc[:, 2, :], small[:, 4, 0:E], small[:, 4, 16:16 + E], small[:, 4, 32:32 + E]
                one = small[:, 6, 0:E]
                V(ts(tiles, cnt, float(N), 1.0, ALU.is_gt, ALU.add))
                for j in range(2, M.tiles_max):
                    V(stt(tiles, cnt, float(N * j), tiles, ALU.is_gt, ALU.add))
                V(dve.memset(one, 1.0))
                V(dve.tensor_tensor_scan(incl, one, tiles, 0.0, ALU.mult, ALU.add))
                V(tt(base, incl, tiles, ALU.subtract))
                V(ts(base, base, float(N), None, ALU.mult))
                V(tt(rkc[:, 0:2, :], rkc[:, 0:2, :], bc(base, NT), ALU.add))
                for i, oh in enumerate((oh1, oh2)):
                    V(tt(w, rkc[:, 0:2, :], oh, ALU.mult))
                    V(dve.tensor_reduce(cols3(54 + 2 * i), w, AX, ALU.add), s_lg if i else None)
                table, less, iota = small[:, 5, 16:48], small[:, 6, 16:48], pk("iota")[:, 0:TABLE]
                V(ts(table, iota, incl[:, 0:1], None, ALU.is_ge))
                for e in range(1, E):
                    V(stt(table, iota, incl[:, e:e + 1], table, ALU.is_ge, ALU.add))
                V(ts(table, table, float(E - 1), None, ALU.min))
                V(ts(less, iota, float(M.U), incl[:, E - 1:E], ALU.mult, ALU.is_lt))
                V(dve.tensor_reduce(cols[:, 59:60], less, AX, ALU.add))
                V(ts(cols[:, 59:60], cols[:, 59:60], -1.0, None, ALU.add))
                V(dve.tensor_copy(M.tab[:, 0:TABLE], table))
                V(dve.tensor_copy(M.tab[:, TABLE:TABLE + 1], cols[:, 59:60]), s_tab)

            def windows(n, src, pe_cols):
                v = src.rearrange("p g (m r) -> p r g m", r=16)
                for half in range(2):
                    for hb in range(2):
                        p0 = HD * half
                        dst = xb[p0:p0 + HD, 8 * hb:8 * hb + 8, :, :]
                        ins = []
                        for j in range(8):
                            ins = ts(dst[:, j], v[p0:p0 + HD, 2 * j + half, :, hb:hb + NCMP],
                                     pe_cols[p0:p0 + HD, 8 * hb + j:8 * hb + j + 1], None, ALU.add)
                V(ins, s_xb)

            V(dve.memset(onesk[:], 1.0 / D))
            V(dve.memset(zeros[:], 0.0))
            V(dve.memset(epsc[:], EPS), consts)
            dve.wait_ge(s_pack, 16)
            for t in range(NT):
                for g in range(2):
                    b = next_job(dve, "xT", "V")
                    V(dve.tensor_copy(hT[:, 4 * g:4 * g + 4, P * t:P * t + P], b3(b, 4)), dve_took)
            dve.sem_inc(s_hT, 1)
            dve.wait_ge(s_cact, 1)
            for c in range(12):
                weigh(f"ada0.{c}", acc0(c))
            mods_from(0, 12, 0, 48, pk("b_ada")[:, 0:48], 1)
            gain(G(0), M(1), pk("attn_gain")[:, 0:KT])
            gain(G(1), M(4), pk("ffn_gain")[:, 0:KT])
            norm(0, hT, [(uT, G(0))])
            dve.wait_ge(s_pos, 16)
            V(dve.tensor_copy(ang[:, 2, :], posi[:]))
            V(ts(ang[:, 2, :], ang[:, 2, :], pk("inv"), None, ALU.mult))
            two_pi = 2 * math.pi
            C1 = 6.28125
            C2 = float(np.float32(np.float32((two_pi - C1) * 2 ** 20).astype(np.int32).astype(np.float64) / 2 ** 20))
            C3 = two_pi - C1 - C2
            for i, (turn, lift) in enumerate(((0.25, math.pi / 2), (0.0, 0.0))):
                a, k = ang[:, i, :], ang[:, 3, :]
                V(ts(k, ang[:, 2, :], 1 / two_pi, turn, ALU.mult, ALU.add))
                V(ts(k, k, 12582912.0, 12582912.0, ALU.add, ALU.subtract))
                V(stt(a, k, -C1, ang[:, 2, :], ALU.mult, ALU.add))
                V(stt(a, k, -C2, a, ALU.mult, ALU.add))
                V(stt(a, k, -C3, a, ALU.mult, ALU.add))
                V(ts(a, a, lift, 3.1415925, ALU.add, ALU.min))
                V(ts(a, a, -3.1415925, None, ALU.max))
            dve.sem_inc(s_ang, 1)
            dve.wait_ge(s_trig, 1)
            for i in range(4):
                V(rope_pair(qT[:, 2 * i:2 * i + 2, :], raw[:, i % 2], mark["raw"][i]), s_rope)
            V(rope_dup(kd[:, 0, 0:2, :]))
            V(rope_dup(kd[:, 0, 2:4, :]), s_rope)
            V(rope_pair(iqT[:, 0:2, :], raw[:, 1], mark["raw"][5]), s_rope)
            V(rope_pair(iqT[:, 2:4, :], raw[:, 0], mark["raw"][6]), s_rope)
            b = next_job(dve, "iw", "V")
            V(ts(iw[:], b[:, 0:16].rearrange("p (t n) -> p t n", t=2), IDX_H ** -0.5 * HD ** -0.5, None, ALU.mult), dve_took)
            V(rope_dup(b3(ikd, 1), ("dup0", "rotdup0"), 1), s_rope)
            causal = pk("causal", NT)
            for t in range(NT):
                L = P * (t + 1)
                for h in range(IDX_H):
                    i = IDX_H * t + h
                    dve.wait_ge(*mark["I"][i])
                    w = iw[:, t, h:h + 1]
                    if h == 0:
                        V(ts(acc8[:, 0:L], rel[:, i % 2, 0:L], w, None, ALU.mult), s_relused)
                    else:
                        V(stt(acc8[:, 0:L], rel[:, i % 2, 0:L], w, acc8[:, 0:L], ALU.mult, ALU.add), s_relused)
                V(tt(work[:, 0:L], acc8[:, 0:L], causal[:, t, 0:L], ALU.add))
                for _ in range(TOPK // 8):
                    V(dve.max(top8[:], work[:, 0:L]))
                    V(dve.match_replace(work[:, 0:L], top8[:], work[:, 0:L], TAKEN))
                V(ts(work[:, 0:L], work[:, 0:L], TAKEN, NEG, ALU.is_gt, ALU.mult))
                V(tt(selm[:, t, 0:L], work[:, 0:L], causal[:, t, 0:L], ALU.add))
            attention("dsa", [selm])
            weigh("ada1.0", acc1(0))
            residual(M(2))
            norm(1, hT, [(uT, G(1))])
            ffn_static(0, HALVES0)
            dve.wait_ge(s_dn, HALVES0)
            add_sums(M(5))
            mods_from(1, 28, 48, 48, pk("b_ada")[:, 48:96], 1)
            mods_from(2, 28, 96, 16, pk("b_kv_ada"), 1)
            gain(G(2), M(13), pk("kv_gain"))
            gain(G(3), M(7), pk("attn_gain")[:, KT:2 * KT])
            gain(G(4), M(10), pk("ffn_gain")[:, KT:2 * KT])
            norm(2, hT, [(uk, G(2)), (uT, G(3))])
            V(rope_dup(kd[:, 0, 0:2, :]))
            V(rope_dup(kd[:, 0, 2:4, :]), s_rope)
            for i in range(2):
                b = next_job(dve, "dup", "V")
                V(dve.tensor_copy(vcd[:, 512 * i:512 * i + 512], b), dve_took)
            dve.sem_inc(s_rope, 1)
            count[s_rope] += 1
            V(rope_dup(kd[:, 1, 0:2, :]))
            V(rope_dup(kd[:, 1, 2:4, :]), s_rope)
            V(rope_dup(kd[:, 2, 0:2, :]))
            V(rope_dup(kd[:, 2, 2:4, :]), s_rope)
            windows(0, kd[:, 0], pk("pe_k"))
            dve.wait_ge(*mark["w1"][0])
            windows(1, vcd.rearrange("p (g n) -> p g n", g=4), pk("pe_v"))
            b = next_job(dve, "kc", "V")
            V(dve.tensor_copy(kcT, b3(b[:, 0:60], 4)), dve_took)
            b = next_job(dve, "vc", "V")
            V(dve.tensor_copy(vc[0:NCMP], b3(b[0:NCMP, 0:256], 4)), dve_took)
            for i in range(4):
                V(rope_pair(qT[:, 2 * i:2 * i + 2, :], raw[:, i % 2], mark["raw"][12 + i]), s_rope)
            dve.wait_ge(*mark["gates"][0])
            attention("nsa", [pk("cmpneg", NT), causal, causal], gates)
            ada2_columns(11)
            residual(M(8))
            norm(3, hT, [(uT, G(4))])

            gain(G(5), M2(1, 0), pk("g_pre_mix"))
            gain(G(6), M2(1, 1), pk("g_pre_mix"))
            V(tt(G(7), M2(2, 0), pk("g_post_mix"), ALU.mult))
            gain(G(8), M2(4, 0), pk("g_pre_ffn"))
            V(tt(G(9), M2(5, 0), pk("g_post_ffn"), ALU.mult))
            b = next_job(dve, "router", "V")
            lg = small[:, 0:2, 32:32 + E1]
            V(dve.tensor_copy(lg, b[:, 0:2 * E1].rearrange("p (t n) -> p t n", t=2)), dve_took)
            top2(0, lg)
            mixture(0)
            add_sums(M(11))
            for t in range(NT):
                for g in range(2):
                    b = next_job(dve, "xT", "V")
                    V(dve.tensor_copy(ctxT[:, 4 * g:4 * g + 4, P * t:P * t + P], b3(b, 4)), dve_took)
            dve.sem_inc(s_ctxT, 1)
            dve.wait_ge(*mark["ms"][4])
            V(dve.reciprocal(rstd[:], root[:]))
            for k in range(KT):
                ins = stt(uT[:, k, :], hT[:, k, :], pk("final_gain")[:, k:k + 1], rstd[:], ALU.mult, ALU.mult)
            N(ins, s_norm)
            dve.wait_ge(s_norm, 5)
            dve.wait_ge(s_sc, 16)
            V(tt(hT[:], uT[:], sincos[:], ALU.add), s_hT)
            dve.wait_ge(*mark["msc"][0])
            V(dve.reciprocal(rstd_c, root_c))
            scaled(ctxT, ctxT, G(6), rstd_c)
            norm(5, hT, [(uT, G(5))])
            V(dve.memset(xm[:], 0.0), s_pad)
            wb = pk("wblk").rearrange("p (w j o) -> p w j o", w=3, j=4)
            dve.wait_ge(s_p2, 16)
            for i, bd in enumerate((bdq, bdk, bdv)):
                for j in range(MH):
                    ins = tt(bd[:, P * j:P * j + P].rearrange("p (m o) -> p m o", o=4),
                             pk2("blkmask").rearrange("p (m o) -> p m o", o=1).to_broadcast([P, 32, 4]),
                             wb[:, i, j:j + 1, :].to_broadcast([P, 32, 4]), ALU.mult)
            V(ins, s_blk)
            dve.wait_ge(*mark["uf"][1])
            cv = pk("conv_w", 3)
            for j in range(MH):
                o = act2[:, j, :].rearrange("p (s n) -> p s n", s=2)
                V(ts(o, xm[:, j, :, 1:1 + T], cv[:, 1, j:j + 1], pk("conv_b")[:, j:j + 1], ALU.mult, ALU.add))
                V(stt(o, xm[:, j, :, 0:T], cv[:, 0, j:j + 1], o, ALU.mult, ALU.add))
                V(stt(o, xm[:, j, :, 2:2 + T], cv[:, 2, j:j + 1], o, ALU.mult, ALU.add), s_conv)
            V(dve.memset(vtok[:, :, :, P:P + 1], 1.0))
            V(dve.memset(root[:], 1.0))
            R = slice(0, 8)
            b = next_job(dve, "gate8", "V")
            V(ts(igr[R], b3(b, 2)[R], pk("bif")[R, 0:1], None, ALU.add), dve_took)
            b = next_job(dve, "gate8", "V")
            V(ts(lfr[R], b3(b, 2)[R], pk("bif")[R, 1:2], None, ALU.add), dve_took)
            V(ts(t1r[R], lfr[R], -1.0, None, ALU.mult))
            V(tt(t1r[R], t1r[R], lfr[R], ALU.min), s_soft)
            dve.wait_ge(s_softd, 2)
            V(stt(lfr[R], lfr[R], 0.0, t1r[R], ALU.min, ALU.subtract))
            for s in range(2):
                V(dve.tensor_tensor_scan(prer[R, s, :], root[R, :], lfr[R, s, :], 0.0, ALU.mult, ALU.add))
            V(stt(t1r[R], prer[R], -2.0, lfr[R], ALU.mult, ALU.add))
            for s in range(2):
                V(ts(t1r[R, s, :], t1r[R, s, :], prer[R, s, T - 1:T], pk("bwd")[R], ALU.add, ALU.mult))
            V(tt(br_[R], t1r[R], prer[R], ALU.add))
            tot = prer[R, 1, T - 1:T]
            V(tt(t1r[R, 1, :], igr[R, 1, :], br_[R, 1, :], ALU.subtract))
            V(ts(t1r[R, 1, :], t1r[R, 1, :], tot, None, ALU.add))
            V(dve.tensor_reduce(cols[R, 60:61], t1r[R, 1, :], AX, ALU.max))
            V(tt(cols[R, 60:61], cols[R, 60:61], tot, ALU.max))
            V(ts(cols[R, 61:62], cols[R, 60:61], -1.0, None, ALU.mult), s_rows)
            V(tt(rstd[R, :], igr[R, 0, :], br_[R, 0, :], ALU.subtract), s_lat)
            b = next_job(dve, "gcols", "V")
            gc = small[:, 5:8, 16:32]
            V(dve.tensor_copy(gc[:, 0:2, :], b[:, 0:32].rearrange("p (a n) -> p a n", a=2)))
            V(dve.tensor_copy(gc[:, 2, 0:8], b[:, 32:40]), dve_took)
            wk, bcol, m0 = gc[:, 0, :], gc[:, 1, :].rearrange("p (t n) -> p t n", t=2), gc[:, 2, 0:8]
            for j in range(8):
                for t in range(NT):
                    b = next_job(dve, "r1", "V")
                    s0, s1 = srange(j, t)
                    ins = dve.tensor_reduce(cols[:, 64 + 8 * t + j:65 + 8 * t + j], b[:, 0:s1 - s0], AX, ALU.max)
                    N(ins, dve_took)
            for j in range(8):
                if j >= 2:
                    dve.wait_ge(*mark["c0"][j - 2])
                if j == 0:
                    dve.wait_ge(*mark["ktok"][1])
                for t in range(NT):
                    ins = ts(kw[:, j % 2, t, :], ktok[:, t, j % 4, :], wk[:, 8 * t + j:8 * t + j + 1], None, ALU.mult)
                N(ins, s_kw)
            dve.wait_ge(dve_took, count[dve_took])
            mx = cols[:, 64:80].rearrange("p (t n) -> p t n", t=2)
            ex = small[:, 0:4, 16:32].rearrange("p a (t n) -> p a t n", t=2)
            mt = small[:, 9, 16:32].rearrange("p (t n) -> p t n", t=2)
            mi = small[:, 8, 16:32].rearrange("p (t n) -> p t n", t=2)
            V(tt(mi, bcol, bc(m0, NT), ALU.add))
            V(tt(mt, bcol, mx, ALU.add))
            V(tt(mt, mt, mi, ALU.max))
            V(tt(small[:, 4, 16:32].rearrange("p (t n) -> p t n", t=2), bcol, mt, ALU.subtract))
            V(tt(ex[:, 0], mi, mt, ALU.subtract))
            V(ts(ex[:, 1], mt, -1.0, None, ALU.mult))
            V(dve.memset(small[:, 2:4, 16:32], 0.0), s_gcol)
            dve.wait_ge(s_gcold, 1)
            V(ts(ex[:, 0], ex[:, 0], M_SCALE, None, ALU.mult))
            units = mlstm_units()
            for s in range(len(units) + 3):
                if s < len(units):
                    j, t = units[s]
                    s0, s1 = srange(j, t)
                    b = next_job(dve, "qk", "V")
                    dve.wait_ge(*mark["r2"][s])
                    V(stt(prob[:, s % 3, 0:s1 - s0], b[:, 0:s1 - s0], M_SCALE, score[:, s % 3, 0:s1 - s0], ALU.mult, ALU.mult,
                          accum_out=cols[:, 80 + s % 4:81 + s % 4]), dve_took)
                    dve.sem_inc(s_sm, 1)
                if s >= 3:
                    u = s - 3
                    j, t = units[u]
                    b = next_job(dve, "num", "V")
                    c = 8 * t + j
                    V(ts(qc[:, u % 2, :], b[:, 256:385], small[:, 0, 16 + c:17 + c], None, ALU.mult))
                    nq, nn = cols[:, 84:85], cols[:, 85:86]
                    V(tt(nq, cols[:, 80 + u % 4:81 + u % 4], qc[:, u % 2, P:P + 1], ALU.add))
                    V(ts(nn, nq, -1.0, None, ALU.mult))
                    V(tt(nq, nq, nn, ALU.max))
                    V(tt(nq, nq, small[:, 1, 16 + c:17 + c], ALU.max))
                    V(dve.reciprocal(nq, nq))
                    V(tt(qc[:, u % 2, 0:P], b[:, 0:P], qc[:, u % 2, 0:P], ALU.add), dve_took)
                    o = hsum[:, t, j % 4, :]
                    if j < MH:
                        V(ts(o, qc[:, u % 2, 0:P], nq, None, ALU.mult))
                    else:
                        V(stt(o, qc[:, u % 2, 0:P], nq, o, ALU.mult, ALU.add))
            st = small[:, 10:12, :].rearrange("p a n -> p (a n)")
            mean = small[:, 4, 32:40]
            for i in range(8):
                t, h = i // 4, i % 4
                V(dve.bn_stats(st[:, 6 * i:6 * i + 6], hsum[:, t, h, :]))
                V(dve.bn_aggr(cols[:, 16 + 2 * i:18 + 2 * i], st[:, 6 * i:6 * i + 6]))
            mv = cols[:, 16:32].rearrange("p (i a) -> p i a", a=2)
            V(dve.tensor_copy(cols[:, 0:8], mv[:, :, 1]), s_var)
            dve.wait_ge(s_std, 1)
            V(dve.reciprocal(cols[:, 0:8], cols[:, 0:8]))
            for i in range(8):
                t, h = i // 4, i % 4
                ins = ts(hsum[:, t, h, :], hsum[:, t, h, :], mv[:, i, 0:1], cols[:, i:i + 1], ALU.subtract, ALU.mult)
            N(ins, s_hn)
            for hp in range(2):
                b = next_job(dve, "hT", "V")
                for i in range(2):
                    h = 2 * hp + i
                    V(ts(tmp[:, 0, 0:T], act2[:, h, 0:T], pk("skip")[:, h:h + 1], None, ALU.mult))
                    ins = stt(tmp[:, 1, 0:T], b[:, T * i:T * i + T], pk("norm_w")[:, h:h + 1], tmp[:, 0, 0:T], ALU.mult, ALU.add)
                    V(ins, dve_took if i else None)
                    V(tt(sq[:, h, :], tmp[:, 1, 0:T], zs[:, h, :], ALU.mult))
            dve.sem_inc(s_m, 1)

            def norm_residual(n, X, g):
                dve.wait_ge(*mark["ms"][n])
                V(dve.reciprocal(rstd[:], root[:]))
                V(tt(xn[:], X[:], bc(rstd[:], KT), ALU.mult))
                for k in range(KT):
                    ins = stt(hT[:, k, :], xn[:, k, :], g[:, k:k + 1], hT[:, k, :], ALU.mult, ALU.add)
                V(ins, s_norm)
                dve.sem_inc(s_hT, 1)
            norm_residual(6, yT, G(7))
            norm(7, hT, [(uT, G(8))])
            b = next_job(dve, "router", "V")
            lg20 = small[:, 11:12, 0:40].rearrange("p a (t n) -> p (a t) n", t=2)
            V(tt(lg20, b[:, 0:40].rearrange("p (t n) -> p t n", t=2), bc(pk("brouter2"), 2), ALU.add), dve_took)
            shape = [P, NT, EG]
            ohg = small[:, 9:11, 16:20]
            first_max(ohg, lg20[:, :, 0:4], shape, cols3(50), small[:, 7:9, 0:4])
            V(tt(small[:, 5:7, 0:4], lg20[:, :, 0:4], cols3(50).to_broadcast(shape), ALU.subtract), s_top)
            dve.wait_ge(s_e, 2)
            V(dve.tensor_reduce(cols3(52), small[:, 5:7, 0:4], AX, ALU.add))
            V(dve.reciprocal(cols3(52), cols3(52)))
            V(ts(ohg, ohg, -NEG, NEG, ALU.mult, ALU.add))
            lge = small[:, 0:2, 32:48]
            for t in range(NT):
                V(tt(lge[:, t].rearrange("p (g i) -> p g i", i=4), lg20[:, t, 4:20].rearrange("p (g i) -> p g i", i=4),
                     ohg[:, t].rearrange("p (g i) -> p g i", i=1).to_broadcast([P, 4, 4]), ALU.add))
            top2(1, lge, cols3(52))
            mixture(1)
            for i in range(4):
                ins = dve.tensor_copy(yT[:, 2 * i:2 * i + 2, :], b3(psum[:, 4 + i, :], 2))
            V(ins, s_y)
            norm_residual(8, yT, G(9))
            for t in range(NT):
                for g in range(2):
                    b = next_job(dve, "oT", "V")
                    V(dve.tensor_copy(uk_rows[:, t, 512 * g:512 * g + 512], b), dve_took)
            dve.sem_inc(s_fin, 1)

        @block.sync
        def _(sp):
            occupant = [None] * NSLOT

            def load(name, src=None, wait=True):
                slot, _, a, b = place[name]
                src = src if src is not None else SRC[name]
                if wait and occupant[slot] is not None:
                    sp.wait_ge(*freed[occupant[slot]])
                occupant[slot] = name
                sp.dma_start(ring[:, slot, 0:a * b].rearrange("p (a b) -> p a b", a=a), src).then_inc(land[slot], 16)

            SRC = dict(stream)
            names = [n for n, _ in stream]
            for n in names[:BEFORE_MOE1]:
                load(n)
            WEIGHTS = (("moe_w_gate", "moe_w_up", "moe_w_down"), ("w_gate_2", "w_up_2", "w_down_2"))

            def tile_load(m, e, u, c, r):
                slot, j, _, _ = tile_chunk(m, u, c, r)
                w = A[WEIGHTS[m][r]][0][bass.ds(e, 1)]
                w = w[:, 512 * c:512 * c + 512, :] if r == 2 else w[:, :, 512 * c:512 * c + 512]
                sp.dma_start(slot_view(slot, *((KT, 512) if r < 2 else (4, D))),
                             w.rearrange("e (k p) n -> p (e k) n", p=P)).then_inc(mix[m].land[j], 16)

            def used_up(m, q, u, c, r):
                M = mix[m]
                return (M.g, M.u, M.dn)[r], q * (M.CH * M.U) + (M.CH * u + c + (1, 1, 3)[r])

            M = mix[0]
            for n in range(7):
                if n < NSLOT:
                    sp.wait_ge(*freed[occupant[M.slots[n]]])
                else:
                    sp.wait_ge(s_otook, 16)
                tile_load(0, 0, 0, n // 3, n % 3)
            sp.wait_ge(s_tab, 1)
            last = sp.value_load(M.tab[0:1, TABLE:TABLE + 1], min_val=0, max_val=TABLE - 2)
            with sp.Fori(0, last) as q:
                e = sp.value_load(M.tab[0:1, bass.ds(q, 1)], min_val=0, max_val=E1 - 1)
                for n in range(7, 21):
                    sp.wait_ge(*used_up(0, q, 0, (n - 7) // 3, (n - 7) % 3))
                    tile_load(0, e, 0, n // 3, n % 3)
                e = sp.value_load(M.tab[0:1, bass.ds(q + 1, 1)], min_val=0, max_val=E1 - 1)
                for n in range(7):
                    sp.wait_ge(*used_up(0, q, 0, (n + 14) // 3, (n + 14) % 3))
                    tile_load(0, e, 0, n // 3, n % 3)
            for n in range(7, 21):
                sp.wait_ge(*used_up(0, last, 0, (n - 7) // 3, (n - 7) % 3))
                tile_load(0, E1 - 1, 0, n // 3, n % 3)
            for n in range(14, 20):
                slot = M.slots[n % 7]
                occupant[slot] = n
                freed[n] = used_up(0, last, 0, n // 3, n % 3)
            for n in names[AFTER_MOE1:]:
                load(n)
            M = mix[1]
            for r in range(3):
                sp.wait_ge(*freed[occupant[M.slots[r]]])
                tile_load(1, 0, 0, 0, r)
            sp.wait_ge(s_tab, 2)
            last = sp.value_load(M.tab[0:1, TABLE:TABLE + 1], min_val=0, max_val=TABLE - 2)
            with sp.Fori(0, last) as q:
                e = sp.value_load(M.tab[0:1, bass.ds(q + 1, 1)], min_val=0, max_val=E2 - 1)
                for r in range(3):
                    sp.wait_ge(*used_up(1, q, 0, 0, r))
                    tile_load(1, e, 0, 0, r)
            sp.wait_ge(s_fin, 1)
            sp.dma_start(out[0].rearrange("(t p) n -> p t n", p=P), uk_rows).then_inc(s_out, 16)
            sp.wait_ge(s_out, 16)


def constants():
    C = {}
    C["ident"] = np.eye(P)
    rot = np.zeros((P, P))
    dup = np.zeros((2, P, P))
    rotdup = np.zeros((2, P, P))
    for m in range(P):
        i = m % HD
        src, sign = (i + 32, -1.0) if i < 32 else (i - 32, 1.0)
        rot[m - i + src, m] = sign
        for d in range(2):
            dup[d, HD * d + i, m] = 1.0
            rotdup[d, HD * d + src, m] = sign
    C["rot"], C["dup0"], C["dup1"], C["rotdup0"], C["rotdup1"] = rot, dup[0], dup[1], rotdup[0], rotdup[1]
    q = np.arange(T).reshape(NT, P).T[:, :, None]
    k = np.arange(T)[None, None, :]
    C["causal"] = np.where(k <= q, 0.0, NEG)
    C["anticausal"] = np.where(k >= q, 0.0, NEG)
    end = 16 * np.arange(NCMP)[None, None, :] + 31
    C["cmpneg"] = np.where(end <= q, 0.0, NEG)
    C["cmp01"] = np.where(end <= q, 1.0, 0.0)
    inv = (np.float32(1.0) / np.float32(10000.0) ** (np.arange(0, HD, 2, dtype=np.float32) / np.float32(HD)))
    C["inv"] = inv[np.arange(P) % 32][:, None]
    C["rank"] = np.tile(E2 - np.arange(E2), (P, 1))
    C["blkmask"] = np.arange(32)[None, :] == np.arange(P)[:, None] // 4
    C["before"] = (np.arange(P)[:, None] < np.arange(P)[None, :]) / D
    C["iota"] = np.tile(np.arange(96), (P, 1))
    C["part"] = np.arange(P)[:, None]
    C["bwd"] = (np.arange(P) >= MH).astype(np.float64)[:, None]
    a = 2 * np.pi * np.outer(np.arange(P), np.arange(P)) / P
    C["dftc"] = np.concatenate([np.cos(a), np.sin(a)], 1) / np.sqrt(P)
    b = 2 * np.pi * ((np.arange(T)[:, None] * np.arange(T)[None, :]) % T) / T
    C["dftt"] = (np.cos(b) / np.sqrt(T)).reshape(NT, P, T).transpose(1, 0, 2)
    C["dfts"] = (-np.sin(b) / np.sqrt(T)).reshape(NT, P, T).transpose(1, 0, 2)
    return C


def positions_2d():
    quarter = D // 4
    freq = (np.float32(1.0) / np.float32(10000.0) ** (np.arange(quarter, dtype=np.float32) / np.float32(quarter)))
    r = np.arange(T // 64, dtype=np.float32)[:, None] * freq
    cl = np.arange(64, dtype=np.float32)[:, None] * freq
    er = np.concatenate([np.sin(r), np.cos(r)], -1)
    ec = np.concatenate([np.sin(cl), np.cos(cl)], -1)
    emb = np.concatenate([np.repeat(er, 64, 0), np.tile(ec, (T // 64, 1))], -1)
    return emb.T.reshape(KT, P, T).transpose(1, 0, 2)


BIG = ["w_ada", "w_kv_ada", "w_ada_2", "a_w_in", "a_w_out", "ffn_w_gate", "ffn_w_up", "ffn_w_down", "w_kv",
       "cmp_w1_k", "cmp_w1_v", "b_w_q", "b_w_out", "moe_w_gate", "moe_w_up", "moe_w_down", "w_in_2", "w_out_2",
       "w_gate_2", "w_up_2", "w_down_2", "x", "positions", "ctx_2"]


def kernel(**inputs):
    import concourse.bacc as bacc
    from concourse.bass_utils import run_bass_kernel_spmd

    x = {k: np.asarray(v) for k, v in inputs.items()}

    def col(v):
        return v.reshape(-1, P).T

    def rows(w, k):
        return w.reshape(k, P, -1).transpose(1, 0, 2).reshape(P, -1)

    L = dict(constants())
    for n in ("attn_gain", "ffn_gain", "kv_gain", "final_gain", "b_ada", "b_kv_ada", "b_ada_2"):
        L[n] = col(x[n])
    for n in ("g_pre_mix", "g_post_mix", "g_pre_ffn", "g_post_ffn"):
        L[n] = col(x[n + "_2"])
    L["c"] = col(x["c"])
    L["c2"] = np.stack([col(x["c_2"]), col(x["c_ctx_2"])], -1)
    L["router"] = rows(x["moe_w_router"][0], KT)
    L["router2"] = rows(np.concatenate([x["w_router_group_2"][0], x["w_router_expert_2"][0]], 1), KT)
    L["brouter2"] = np.tile(np.concatenate([x["b_router_group_2"][0], x["b_router_expert_2"][0]]), (P, 1))
    L["pe_k"], L["pe_v"] = x["cmp_pe_k"].reshape(16, P).T, x["cmp_pe_v"].reshape(16, P).T
    L["w2k"] = rows(np.concatenate([x["cmp_w2_k"]] * 2, 1), 2)
    L["w2v"] = rows(x["cmp_w2_v"], 2)
    L["conv_w"] = x["conv_w_2"][0].reshape(3, MH, P).transpose(2, 0, 1)
    L["conv_b"], L["norm_w"], L["skip"] = col(x["conv_b_2"]), col(x["mlstm_norm_w_2"]), col(x["mlstm_skip_2"])
    L["wblk"] = np.stack([x[n][0].reshape(MH, 32, 4, 4).transpose(1, 2, 0, 3).reshape(P, 16)
                          for n in ("w_q_2", "w_k_2", "w_v_2")], 1)
    f, b = x["w_if_fwd_2"][0], x["w_if_bwd_2"][0]
    L["wif"] = np.stack([rows(np.concatenate([f[:, s], b[:, s]], 1), 12).reshape(P, 12, 8)
                         for s in (slice(0, 4), slice(4, 8))], 2)
    bf, bb = x["b_if_fwd_2"][0], x["b_if_bwd_2"][0]
    bif = np.zeros((P, 2), np.float32)
    for i, s in enumerate((slice(0, 4), slice(4, 8))):
        bif[0:8, i] = np.concatenate([bf[s], bb[s]])
    L["bif"] = bif
    L["wfour"] = x["w_fourier_2"][0].transpose(1, 0, 2)
    packed = np.concatenate([np.asarray(L[n], np.float32).reshape(P, w) for n, w in PACK], 1)

    nc = bacc.Bacc("TRN2", target_bir_lowering=False, num_devices=1)
    arrays = {n: np.ascontiguousarray(x[n]) for n in BIG}
    arrays["pack"] = np.ascontiguousarray(packed)
    arrays["pack2"] = np.ascontiguousarray(
        np.concatenate([np.asarray(L[n], np.float32).reshape(P, w) for n, w in PACK2], 1))
    arrays["sincos"] = np.ascontiguousarray(positions_2d().astype(np.float32))
    A = {n: nc.dram_tensor(f"in_{n}", a.shape, mybir.dt.from_np(a.dtype), kind="ExternalInput").ap()
         for n, a in arrays.items()}
    out = nc.dram_tensor("out", (1, T, D), F32, kind="ExternalOutput").ap()
    program(nc, A, out)
    r = run_bass_kernel_spmd(nc, [{f"in_{n}": a for n, a in arrays.items()}], core_ids=[0])
    return r.results[0]["out"]
```
